# Optimizing a Trainium2 kernel written in Bass

```python
import jax, jax.numpy as jnp
from jax import lax
import numpy as np

D_MODEL = 1024
BATCH = 1
SEQ = 256
DEPTH = 2

HEAD_DIM = 64
H_A = 4
H_B = 4
H_C = 4
H_D = 4
N_BRANCH = 4
BRANCH_WIDTH = 4 * HEAD_DIM
N_ALIBI = H_A + H_B
MOBA_BLOCK = 256
MOBA_TOPK = 3
MOBA_Q_CHUNK = 32
NSA_CMP_LEN = 32
NSA_CMP_STRIDE = 16
NSA_CMP_HIDDEN = 4 * HEAD_DIM
NSA_SLC_BLOCK = 64
NSA_TOP_N = 16
NSA_WINDOW = 512
NSA_Q_CHUNK = 64
NSA_FORCE_BONUS = 1.0e4
ATTN_Q_BLOCK = 128
MLA_Q_RANK = 256
MLA_KV_RANK = 128
MLA_NOPE = 64
MLA_ROPE = 32
MLA_V = 64
ROPE_BASE = 10000.0
MEM_LEN = 256
N_MEM_HEADS = 4
D_FF = 2816
N_SUBLAYERS = 4
ALPHA = (2 * DEPTH) ** 0.25
BETA = (8 * DEPTH) ** -0.25
LN_EPS = 1e-5
RMS_EPS = 1e-6
NEG_INF = -1e30
MAX_POS_OFFSET = 4096
IN_SPLITS = (H_A * HEAD_DIM, H_A * HEAD_DIM, H_A * HEAD_DIM,
             H_B * HEAD_DIM, HEAD_DIM, HEAD_DIM, HEAD_DIM,
             HEAD_DIM, HEAD_DIM, HEAD_DIM, 3 * H_B,
             H_C * HEAD_DIM, H_C * HEAD_DIM, H_C * HEAD_DIM, H_C,
             MLA_Q_RANK, MLA_KV_RANK, MLA_ROPE,
             N_BRANCH * D_MODEL)
N_IN = sum(IN_SPLITS)
FOX_F_OFFSET = 3 * H_A * HEAD_DIM + H_B * HEAD_DIM + 6 * HEAD_DIM + 3 * H_B + 3 * H_C * HEAD_DIM

kernel_name = "hybrid_moba_nsa_fox_mla_deepnorm"

def split_points(sizes):
    return [int(v) for v in np.cumsum(sizes)[:-1]]

def layer_norm(x, g, b):
    xf = x.astype(jnp.float32)
    mu = jnp.mean(xf, -1, keepdims=True)
    var = jnp.mean(jnp.square(xf - mu), -1, keepdims=True)
    return ((xf - mu) * lax.rsqrt(var + LN_EPS) * g + b).astype(x.dtype)

def rms_norm(x, g):
    xf = x.astype(jnp.float32)
    return (xf * lax.rsqrt(jnp.mean(jnp.square(xf), -1, keepdims=True) + RMS_EPS) * g).astype(x.dtype)

def masked_softmax(s, mask):
    s = jnp.where(mask, s, NEG_INF)
    m = jnp.max(s, -1, keepdims=True)
    e = jnp.where(mask, jnp.exp(s - m), 0.0)
    return e / jnp.maximum(jnp.sum(e, -1, keepdims=True), 1e-30)

def swiglu(x, w_in, w_out):
    g, u = jnp.split(x @ w_in, 2, axis=-1)
    return (jax.nn.silu(g) * u) @ w_out

def to_heads(x, h):
    B, S, _ = x.shape
    return x.reshape(B, S, h, -1).transpose(0, 2, 1, 3)

def from_heads(x):
    B, H, S, d = x.shape
    return x.transpose(0, 2, 1, 3).reshape(B, S, H * d)

def alibi_slopes(n):
    return jnp.exp2(-8.0 * jnp.arange(1, n + 1, dtype=jnp.float32) / n)

def apply_rope(x, cos, sin):
    half = x.shape[-1] // 2
    x1, x2 = x[..., :half].astype(jnp.float32), x[..., half:].astype(jnp.float32)
    return jnp.concatenate([x1 * cos - x2 * sin, x1 * sin + x2 * cos], -1).astype(x.dtype)

def swept_causal_attention(q, k, v, decay=None):
    B, H, S, dk = q.shape
    C = ATTN_Q_BLOCK
    nc = S // C
    scale = dk ** -0.5
    s_pos = jnp.arange(S)
    xs = (jnp.arange(nc), q.reshape(B, H, nc, C, dk).transpose(2, 0, 1, 3, 4))
    if decay is not None:
        xs = xs + (decay.reshape(B, H, nc, C).transpose(2, 0, 1, 3),)

    def one_block(args):
        ci, qb, *rest = args
        t = ci * C + jnp.arange(C)
        logits = jnp.einsum('bhqd,bhkd->bhqk', qb, k).astype(jnp.float32) * scale
        if decay is not None:
            logits = logits + rest[0][..., None] - decay[:, :, None, :]
        p = masked_softmax(logits, s_pos[None, :] <= t[:, None])
        return jnp.einsum('bhqk,bhkd->bhqd', p.astype(v.dtype), v)

    o = lax.map(one_block, xs)
    return o.transpose(1, 2, 0, 3, 4).reshape(B, H, S, v.shape[-1])

def moba_attention(q, k, v, slopes):
    B, H, S, dh = q.shape
    nb = -(-S // MOBA_BLOCK)
    pad = nb * MOBA_BLOCK - S
    kb = jnp.pad(k, ((0, 0), (0, 0), (0, pad), (0, 0))).reshape(B, H, nb, MOBA_BLOCK, dh)
    vb = jnp.pad(v, ((0, 0), (0, 0), (0, pad), (0, 0))).reshape(B, H, nb, MOBA_BLOCK, dh)
    n_sel = min(MOBA_TOPK, nb - 1)
    C = MOBA_Q_CHUNK
    nc = S // C
    scale = dh ** -0.5
    blk_pos = jnp.arange(MOBA_BLOCK)
    xs = (jnp.arange(nc), q.reshape(B, H, nc, C, dh).transpose(2, 0, 1, 3, 4))
    if n_sel > 0:
        own_all = jnp.arange(S) // MOBA_BLOCK
        k_mean = jnp.mean(kb.astype(jnp.float32), axis=3)
        gate = jnp.einsum('bhtd,bhnd->bhtn', q.astype(jnp.float32), k_mean)
        cand = jnp.arange(nb)[None, :] < own_all[:, None]
        _, sel = lax.top_k(jnp.where(cand, gate, NEG_INF), n_sel)
        xs = xs + (sel.reshape(B, H, nc, C, n_sel).transpose(2, 0, 1, 3, 4),)
    gather = jax.vmap(jax.vmap(lambda table, idx: table[idx]))

    def one_chunk(args):
        ci, qc, *rest = args
        t = ci * C + jnp.arange(C)
        b_own = (ci * C) // MOBA_BLOCK
        k_own = lax.dynamic_index_in_dim(kb, b_own, axis=2, keepdims=False)
        v_own = lax.dynamic_index_in_dim(vb, b_own, axis=2, keepdims=False)
        pos_own = jnp.broadcast_to(b_own * MOBA_BLOCK + blk_pos, (B, H, C, MOBA_BLOCK))
        s = jnp.einsum('bhqd,bhkd->bhqk', qc, k_own)
        pos = pos_own
        mask = pos_own <= t[:, None]
        if n_sel > 0:
            sc = rest[0]
            k_sel = gather(kb, sc)
            v_sel = gather(vb, sc)
            s_sel = jnp.einsum('bhqd,bhqnkd->bhqnk', qc, k_sel).reshape(B, H, C, n_sel * MOBA_BLOCK)
            pos_sel = (sc[..., None] * MOBA_BLOCK + blk_pos).reshape(B, H, C, n_sel * MOBA_BLOCK)
            mask_sel = jnp.repeat(sc < b_own, MOBA_BLOCK, axis=-1)
            s = jnp.concatenate([s_sel, s], -1)
            pos = jnp.concatenate([pos_sel, pos], -1)
            mask = jnp.concatenate([mask_sel, mask], -1)
        dist = (t[:, None] - pos).astype(jnp.float32)
        logits = s.astype(jnp.float32) * scale - slopes[:, None, None] * dist
        p = masked_softmax(logits, mask).astype(v.dtype)
        o = jnp.einsum('bhqk,bhkd->bhqd', p[..., -MOBA_BLOCK:], v_own)
        if n_sel > 0:
            p_sel = p[..., :n_sel * MOBA_BLOCK].reshape(B, H, C, n_sel, MOBA_BLOCK)
            o = o + jnp.einsum('bhqnk,bhqnkd->bhqd', p_sel, v_sel)
        return o

    o = lax.map(one_chunk, xs)
    return o.transpose(1, 2, 0, 3, 4).reshape(B, H, S, dh)

def nsa_compress(x, pos, w1, w2):
    B, S, dh = x.shape
    n_cmp = (S - NSA_CMP_LEN) // NSA_CMP_STRIDE + 1
    idx = jnp.arange(n_cmp)[:, None] * NSA_CMP_STRIDE + jnp.arange(NSA_CMP_LEN)[None, :]
    blocks = (x[:, idx] + pos).reshape(B, n_cmp, NSA_CMP_LEN * dh)
    return jax.nn.gelu(blocks @ w1) @ w2

def nsa_selected(q, k, v, sel, slopes):
    B, H, S, dh = q.shape
    n_slc = S // NSA_SLC_BLOCK
    n_top = sel.shape[-1]
    kb = k.reshape(B, n_slc, NSA_SLC_BLOCK, dh)
    vb = v.reshape(B, n_slc, NSA_SLC_BLOCK, dh)
    C = NSA_Q_CHUNK
    nc = S // C
    scale = dh ** -0.5
    blk = jnp.arange(NSA_SLC_BLOCK)
    gather = jax.vmap(lambda table, idx: table[idx])
    xs = (jnp.arange(nc), q.reshape(B, H, nc, C, dh).transpose(2, 0, 1, 3, 4),
          sel.reshape(B, nc, C, n_top).transpose(1, 0, 2, 3))

    def one_chunk(args):
        ci, qc, sc = args
        t = ci * C + jnp.arange(C)
        k_sel = gather(kb, sc)
        v_sel = gather(vb, sc)
        pos = (sc[..., None] * NSA_SLC_BLOCK + blk).reshape(B, 1, C, n_top * NSA_SLC_BLOCK)
        dist = (t[:, None] - pos).astype(jnp.float32)
        s = jnp.einsum('bhqd,bqnkd->bhqnk', qc, k_sel).reshape(B, H, C, n_top * NSA_SLC_BLOCK)
        logits = s.astype(jnp.float32) * scale - slopes[:, None, None] * dist
        p = masked_softmax(logits, dist >= 0).astype(v.dtype)
        return jnp.einsum('bhqnk,bqnkd->bhqd', p.reshape(B, H, C, n_top, NSA_SLC_BLOCK), v_sel)

    o = lax.map(one_chunk, xs)
    return o.transpose(1, 2, 0, 3, 4).reshape(B, H, S, dh)

def sliding_window_attention(q, k, v, slopes):
    B, H, S, dh = q.shape
    C, W = ATTN_Q_BLOCK, NSA_WINDOW
    nc = S // C
    kp = jnp.pad(k, ((0, 0), (W, 0), (0, 0)))
    vp = jnp.pad(v, ((0, 0), (W, 0), (0, 0)))
    idx = jnp.arange(nc)[:, None] * C + jnp.arange(C + W)[None, :]
    kw, vw = kp[:, idx], vp[:, idx]
    qb = q.reshape(B, H, nc, C, dh)
    t = jnp.arange(nc)[:, None] * C + jnp.arange(C)[None, :]
    s_pos = idx - W
    dist = t[:, :, None] - s_pos[:, None, :]
    mask = (dist >= 0) & (dist < W) & (s_pos[:, None, :] >= 0)
    s = jnp.einsum('bhcqd,bckd->bhcqk', qb, kw).astype(jnp.float32) * dh ** -0.5
    logits = s - slopes[:, None, None, None] * dist.astype(jnp.float32)
    p = masked_softmax(logits, mask).astype(v.dtype)
    return jnp.einsum('bhcqk,bckd->bhcqd', p, vw).reshape(B, H, S, dh)

def nsa_attention(q, k_c, v_c, k_s, v_s, k_w, v_w, gate_logits, slopes, cmp_pos, cmp_w1, cmp_w2):
    B, H, S, dh = q.shape
    t_all = jnp.arange(S)
    k_cmp = nsa_compress(k_c, cmp_pos[0], cmp_w1[0], cmp_w2[0])
    v_cmp = nsa_compress(v_c, cmp_pos[1], cmp_w1[1], cmp_w2[1])
    n_cmp = k_cmp.shape[1]
    cmp_start = jnp.arange(n_cmp) * NSA_CMP_STRIDE
    dist = (t_all[:, None] - (cmp_start + NSA_CMP_LEN - 1)[None, :]).astype(jnp.float32)
    logits = jnp.einsum('bhtd,bcd->bhtc', q, k_cmp).astype(jnp.float32) * dh ** -0.5 - slopes[:, None, None] * dist
    p_cmp = masked_softmax(logits, dist >= 0)
    o_cmp = jnp.einsum('bhtc,bcd->bhtd', p_cmp.astype(v_cmp.dtype), v_cmp)
    n_slc = S // NSA_SLC_BLOCK
    slc_start = jnp.arange(n_slc) * NSA_SLC_BLOCK
    overlap = ((cmp_start[:, None] < slc_start[None, :] + NSA_SLC_BLOCK)
               & (cmp_start[:, None] + NSA_CMP_LEN > slc_start[None, :])).astype(jnp.float32)
    imp = jnp.einsum('bhtc,cj->btj', p_cmp, overlap)
    own = t_all // NSA_SLC_BLOCK
    j = jnp.arange(n_slc)[None, :]
    forced = (j == 0) | (j == own[:, None]) | (j == own[:, None] - 1)
    imp = jnp.where(j <= own[:, None], imp + NSA_FORCE_BONUS * forced.astype(jnp.float32), NEG_INF)
    _, sel = lax.top_k(imp, min(NSA_TOP_N, n_slc))
    o_slc = nsa_selected(q, k_s, v_s, sel, slopes)
    o_win = sliding_window_attention(q, k_w, v_w, slopes)
    g = jax.nn.sigmoid(gate_logits.astype(jnp.float32)).reshape(B, S, H, 3).transpose(0, 2, 1, 3).astype(q.dtype)
    return g[..., 0:1] * o_cmp + g[..., 1:2] * o_slc + g[..., 2:3] * o_win

def mla_attention(c_q, c_kv, k_rope, positions, q_norm, w_uq, kv_norm, w_ukv):
    B, S, _ = c_q.shape
    q = (rms_norm(c_q, q_norm) @ w_uq).reshape(B, S, H_D, MLA_NOPE + MLA_ROPE)
    kv = (rms_norm(c_kv, kv_norm) @ w_ukv).reshape(B, S, H_D, MLA_NOPE + MLA_V)
    inv_freq = ROPE_BASE ** (-jnp.arange(0, MLA_ROPE, 2, dtype=jnp.float32) / MLA_ROPE)
    ang = positions.astype(jnp.float32)[..., None] * inv_freq
    cos, sin = jnp.cos(ang), jnp.sin(ang)
    q_rope = apply_rope(q[..., MLA_NOPE:], cos[:, :, None], sin[:, :, None])
    k_r = apply_rope(k_rope, cos, sin)[:, :, None, :]
    qh = jnp.concatenate([q[..., :MLA_NOPE], q_rope], -1).transpose(0, 2, 1, 3)
    kh = jnp.concatenate([kv[..., :MLA_NOPE], jnp.broadcast_to(k_r, (B, S, H_D, MLA_ROPE))], -1).transpose(0, 2, 1, 3)
    vh = kv[..., MLA_NOPE:].transpose(0, 2, 1, 3)
    return swept_causal_attention(qh, kh, vh)

def token_mixer(x, positions, w_in, b_in, w_branch, w_o, q_norm, w_uq, kv_norm, w_ukv,
                cmp_pos, cmp_w1, cmp_w2):
    B, S, _ = x.shape
    proj = x @ w_in + b_in
    (a_q, a_k, a_v, b_q, b_kc, b_vc, b_ks, b_vs, b_kw, b_vw, b_g,
     c_q, c_k, c_v, c_f, d_cq, d_ckv, d_kr, g_merge) = jnp.split(proj, split_points(IN_SPLITS), axis=-1)
    slopes = alibi_slopes(N_ALIBI)
    o_a = moba_attention(to_heads(a_q, H_A), to_heads(a_k, H_A), to_heads(a_v, H_A), slopes[0::2])
    o_b = nsa_attention(to_heads(b_q, H_B), b_kc, b_vc, b_ks, b_vs, b_kw, b_vw, b_g, slopes[1::2],
                        cmp_pos, cmp_w1, cmp_w2)
    decay = jnp.cumsum(jax.nn.log_sigmoid(c_f.astype(jnp.float32)), axis=1).transpose(0, 2, 1)
    o_c = swept_causal_attention(to_heads(c_q, H_C), to_heads(c_k, H_C), to_heads(c_v, H_C), decay)
    o_d = mla_attention(d_cq, d_ckv, d_kr, positions, q_norm, w_uq, kv_norm, w_ukv)
    branches = jnp.stack([from_heads(o_a), from_heads(o_b), from_heads(o_c), from_heads(o_d)], axis=2)
    y = jnp.einsum('bsnk,nkd->bsnd', branches, w_branch)
    g = jax.nn.sigmoid(g_merge.reshape(B, S, N_BRANCH, D_MODEL))
    return jnp.sum(g * y, axis=2) @ w_o

def memory_cross_attention(x, mem, w_q, w_kv, w_o):
    q = to_heads(x @ w_q, N_MEM_HEADS)
    k, v = jnp.split(mem @ w_kv, 2, axis=-1)
    k, v = to_heads(k, N_MEM_HEADS), to_heads(v, N_MEM_HEADS)
    logits = jnp.einsum('bhqd,bhkd->bhqk', q, k).astype(jnp.float32) * HEAD_DIM ** -0.5
    p = jax.nn.softmax(logits, axis=-1).astype(v.dtype)
    return from_heads(jnp.einsum('bhqk,bhkd->bhqd', p, v)) @ w_o

def setup_inputs(seed: int = 0) -> dict:
    key = jax.random.key(seed)
    ks = jax.random.split(key, 26)
    L = DEPTH

    def nrm(k, shape, scale):
        return jax.random.normal(k, shape, jnp.float32) * scale

    x = nrm(ks[0], (BATCH, SEQ, D_MODEL), 1.0)
    mem = nrm(ks[1], (BATCH, MEM_LEN, D_MODEL), 1.0)
    positions = (jnp.arange(SEQ, dtype=jnp.int32)[None, :]
                 + jax.random.randint(ks[2], (BATCH, 1), 0, MAX_POS_OFFSET, dtype=jnp.int32))
    ln_g = 1.0 + nrm(ks[3], (L, N_SUBLAYERS, D_MODEL), 0.02)
    ln_b = nrm(ks[4], (L, N_SUBLAYERS, D_MODEL), 0.02)
    ffn1_w_in = nrm(ks[5], (L, D_MODEL, 2 * D_FF), D_MODEL ** -0.5)
    ffn1_w_out = nrm(ks[6], (L, D_FF, D_MODEL), D_FF ** -0.5 * BETA)
    ffn2_w_in = nrm(ks[7], (L, D_MODEL, 2 * D_FF), D_MODEL ** -0.5)
    ffn2_w_out = nrm(ks[8], (L, D_FF, D_MODEL), D_FF ** -0.5 * BETA)
    w_in = nrm(ks[9], (L, D_MODEL, N_IN), D_MODEL ** -0.5)
    b_in = nrm(ks[10], (L, N_IN), 0.02)
    b_in = b_in.at[:, FOX_F_OFFSET:FOX_F_OFFSET + H_C].set(
        jax.random.uniform(ks[11], (L, H_C), jnp.float32, 2.0, 5.0))
    w_branch = nrm(ks[12], (L, N_BRANCH, BRANCH_WIDTH, D_MODEL), BRANCH_WIDTH ** -0.5)
    w_o = nrm(ks[13], (L, D_MODEL, D_MODEL), D_MODEL ** -0.5 * BETA)
    mla_q_norm = 1.0 + nrm(ks[14], (L, MLA_Q_RANK), 0.02)
    mla_w_uq = nrm(ks[15], (L, MLA_Q_RANK, H_D * (MLA_NOPE + MLA_ROPE)), MLA_Q_RANK ** -0.5)
    mla_kv_norm = 1.0 + nrm(ks[16], (L, MLA_KV_RANK), 0.02)
    mla_w_ukv = nrm(ks[17], (L, MLA_KV_RANK, H_D * (MLA_NOPE + MLA_V)), MLA_KV_RANK ** -0.5)
    nsa_cmp_pos = nrm(ks[18], (L, 2, NSA_CMP_LEN, HEAD_DIM), 0.02)
    nsa_cmp_w1 = nrm(ks[19], (L, 2, NSA_CMP_LEN * HEAD_DIM, NSA_CMP_HIDDEN), (NSA_CMP_LEN * HEAD_DIM) ** -0.5)
    nsa_cmp_w2 = nrm(ks[20], (L, 2, NSA_CMP_HIDDEN, HEAD_DIM), NSA_CMP_HIDDEN ** -0.5)
    xa_w_q = nrm(ks[21], (L, D_MODEL, N_MEM_HEADS * HEAD_DIM), D_MODEL ** -0.5)
    xa_w_kv = nrm(ks[22], (L, D_MODEL, 2 * N_MEM_HEADS * HEAD_DIM), D_MODEL ** -0.5)
    xa_w_o = nrm(ks[23], (L, N_MEM_HEADS * HEAD_DIM, D_MODEL), (N_MEM_HEADS * HEAD_DIM) ** -0.5 * BETA)
    return {"x": x, "mem": mem, "positions": positions, "ln_g": ln_g, "ln_b": ln_b,
            "ffn1_w_in": ffn1_w_in, "ffn1_w_out": ffn1_w_out, "ffn2_w_in": ffn2_w_in, "ffn2_w_out": ffn2_w_out,
            "w_in": w_in, "b_in": b_in, "w_branch": w_branch, "w_o": w_o,
            "mla_q_norm": mla_q_norm, "mla_w_uq": mla_w_uq, "mla_kv_norm": mla_kv_norm, "mla_w_ukv": mla_w_ukv,
            "nsa_cmp_pos": nsa_cmp_pos, "nsa_cmp_w1": nsa_cmp_w1, "nsa_cmp_w2": nsa_cmp_w2,
            "xa_w_q": xa_w_q, "xa_w_kv": xa_w_kv, "xa_w_o": xa_w_o}

def reference(x, mem, positions, ln_g, ln_b, ffn1_w_in, ffn1_w_out, ffn2_w_in, ffn2_w_out,
              w_in, b_in, w_branch, w_o, mla_q_norm, mla_w_uq, mla_kv_norm, mla_w_ukv,
              nsa_cmp_pos, nsa_cmp_w1, nsa_cmp_w2, xa_w_q, xa_w_kv, xa_w_o):
    for l in range(DEPTH):
        x = layer_norm(ALPHA * x + 0.5 * swiglu(x, ffn1_w_in[l], ffn1_w_out[l]), ln_g[l, 0], ln_b[l, 0])
        mix = token_mixer(x, positions, w_in[l], b_in[l], w_branch[l], w_o[l],
                          mla_q_norm[l], mla_w_uq[l], mla_kv_norm[l], mla_w_ukv[l],
                          nsa_cmp_pos[l], nsa_cmp_w1[l], nsa_cmp_w2[l])
        x = layer_norm(ALPHA * x + mix, ln_g[l, 1], ln_b[l, 1])
        x = layer_norm(ALPHA * x + memory_cross_attention(x, mem, xa_w_q[l], xa_w_kv[l], xa_w_o[l]),
                       ln_g[l, 2], ln_b[l, 2])
        x = layer_norm(ALPHA * x + 0.5 * swiglu(x, ffn2_w_in[l], ffn2_w_out[l]), ln_g[l, 3], ln_b[l, 3])
    return x


_drawn_inputs = setup_inputs


def setup_inputs(seed=0):
    import zlib

    import numpy as np

    out = dict(_drawn_inputs(seed))
    spreads = {}
    factors = {'mla_q_norm': 8.0, 'mla_kv_norm': 8.0, 'nsa_cmp_pos': 8.0}
    for name, (base, spread) in spreads.items():
        noise = np.random.default_rng([zlib.crc32(name.encode()), seed]).standard_normal(out[name].shape)
        drawn = base * np.exp(spread * noise) if base else spread * noise
        out[name] = __import__('jax').numpy.asarray(drawn.astype(out[name].dtype))
    for name, factor in factors.items():
        out[name] = (out[name] * factor).astype(out[name].dtype)
    return out
```

```python
from contextlib import ExitStack

import numpy as np
import concourse.bass as bass
from concourse import mybir

F32 = mybir.dt.float32
F32R = mybir.dt.float32r
I32 = mybir.dt.int32
ACT = mybir.ActivationFunctionType
ALU = mybir.AluOpType
AX = mybir.AxisListType

P = 128
D = 1024
S = 256
L = 2
FF = 2816
KT = D // P
TT = S // P
FT = FF // P
HD = 64
NH = 4
CMP = 15
CMPW = 16
SCALE = HD ** -0.5
SCALE_D = 96 ** -0.5
ALPHA = (2 * L) ** 0.25
LN_EPS = 1e-5
RMS_EPS = 1e-6
NEG = -1e30

RAW_SLOTS = 3
WT_SLOTS = 6
AHEAD = WT_SLOTS - 1

A_Q, A_K, A_V, B_Q, B_KC, B_KS, B_VS, B_KW, B_VW, B_G = 0, 256, 512, 768, 1024, 1152, 1216, 1280, 1344, 1408
C_Q, C_K, C_V, C_F, D_CQ, D_CKV, D_KR, G_M = 1420, 1676, 1932, 2188, 2192, 2448, 2576, 2608

BRANCHES = (3, 2, 0, 1)
PROJ = [("col", D_CQ), ("col", D_CQ + 128), ("col", D_CKV), ("kr", D_KR), ("col", B_KC), ("pair", B_KS),
        ("col", B_Q), ("col", B_Q + 128), ("pair", B_VS), ("narrow", B_G, 12), ("narrow", C_F, 4),
        ("col", C_Q), ("col", C_Q + 128), ("col", C_K), ("col", C_K + 128), ("col", C_V), ("col", C_V + 128),
        ("uq",), ("ukv",)] + [("w1", br, c) for br in range(2) for c in range(4)] + [
        ("col", A_Q), ("col", A_Q + 128), ("col", A_K), ("col", A_K + 128), ("col", A_V), ("col", A_V + 128),
        ("w2",)]
MIXER = list(PROJ)
for _b in range(4):
    MIXER += [("gate", _b, _n) for _n in range(KT)]
    MIXER += [("branch", _b, _h) for _h in range(2)]
MIXER += [("wo", _k) for _k in range(KT)]
MIXER += [("xk", 0), ("xk", 1), ("xv", 0), ("xv", 1), ("xq", 0), ("xq", 1), ("xo", 0), ("xo", 1)]

FFN_UNITS = 3 * FT
MIX0 = FFN_UNITS
FFN2_0 = MIX0 + len(MIXER)
UNITS = FFN2_0 + FFN_UNITS
assert UNITS % WT_SLOTS == 0 and UNITS % RAW_SLOTS == 0 and WT_SLOTS == 6 and RAW_SLOTS == 3

PA = ["dcq0", "dcq1", "dckv", "kc", "ks", "bq0", "bq1", "ssq", "cq0", "cq1", "ck0", "ck1", "kn0", "kn1",
      "aq0", "aq1", "ak0", "ak1", "cmp"] + [f"gate{b}_{n}" for b in range(4) for n in range(KT)]
PD = ["kr", "vs", "gf", "cv0", "cv1", "q0", "q1", "q2", "q3", "vd0", "vd1", "hid0", "decay", "hid1",
      "av0", "av1"] + [f"y{b}_{n}" for b in range(4) for n in range(KT)]

MAIN_PA = {0: "dcq0", 1: "dcq1", 2: "dckv", 4: "kc", 5: "ks", 6: "bq0", 7: "bq1", 11: "cq0", 12: "cq1",
           13: "ck0", 14: "ck1", 27: "aq0", 28: "aq1", 29: "ak0", 30: "ak1"}
U_KR, U_VS, U_G, U_F, U_CV, U_UQ, U_UKV, U_W1, U_AV, U_W2 = 3, 8, 9, 10, 15, 17, 18, 19, 31, 33
NPROJ = len(PROJ)
U_WO = NPROJ + 40
U_X = U_WO + KT
ENDS_UNIT = {name: n for n, name in MAIN_PA.items()}
ENDS_UNIT |= {"kr": U_KR, "vs": U_VS, "gf": U_F, "cv0": U_CV, "cv1": U_CV + 1, "q3": U_UQ, "vd1": U_UKV,
              "hid0": U_W1 + 3, "hid1": U_W1 + 7, "av0": U_AV, "av1": U_AV + 1, "cmp": U_W2}
for _n, _u in enumerate(MIXER):
    if _u[0] == "gate":
        ENDS_UNIT[f"gate{_u[1]}_{_u[2]}"] = _n
    if _u[0] == "branch":
        ENDS_UNIT[f"y{_u[1]}_{4 * _u[2] + 3}"] = _n
PA_MID = [n for n in PA if n not in ENDS_UNIT]
PD_MID = [n for n in PD if n not in ENDS_UNIT]

HEADS = [(0, h, "d") for h in range(NH)] + [(1, h, "c") for h in range(NH)] + [(2, h, "a") for h in range(NH)]
CMP_SLOT = len(HEADS)
HEADS += [(3, 0, "cmp")] + [(3, h, kind) for h in range(NH) for kind in ("s", "w")]
NSLOT = len(HEADS)
PAIR_AT = {4: 0, 6: 1, 8: 2, 10: 3, 12: 4, 14: 5, 19: 6, 23: 7}
PAIR_END = {pair: step - 3 for step, pair in PAIR_AT.items()}
PAIRS = 8

BIAS = {"dcq0": 0, "dcq1": 1, "dckv": 2, "kr": 3, "kc": 4, "ks": 5, "bq0": 6, "bq1": 7, "cq0": 8, "cq1": 9,
        "ck0": 10, "ck1": 11, "aq0": 12, "aq1": 13, "ak0": 14, "ak1": 15}
NB = 48
GB0 = 16
LNG, LNB, POS, QN, KN, HALF = NB, NB + 32, NB + 64, NB + 96, NB + 98, NB + 99
NCOLS = HALF + 32

C_ID, C_CAUSAL, C_ALIBI, C_TRI = 0, 128, 384, 384 + 8 * 256
C_CMPB, C_CMPM = C_TRI + 256, C_TRI + 256 + 128
C_INV, C_OFF, C_PHASE, C_SEL = C_CMPM + 128, C_CMPM + 129, C_CMPM + 130, C_CMPM + 131
NCONST = C_SEL + 16
TWO_PI = 2 * np.pi
PI_1 = float(np.float32(6.28125))
PI_2 = 0.0019350051879882812
PI_3 = float(np.float32(TWO_PI - PI_1 - PI_2))
ROUND = float(1.5 * 2 ** 23)


def constants():
    t = np.arange(P)
    c = np.zeros((P, NCONST), np.float32)
    c[:, C_ID:C_ID + P] = np.eye(P)
    diag = np.where(t[None, :] <= t[:, None], 0.0, NEG)
    c[:, C_CAUSAL + P:C_CAUSAL + 2 * P] = diag
    slopes = 2.0 ** -np.arange(1, 9)
    dist = (t[:, None] - t[None, :]).astype(np.float64)
    for i in range(8):
        at = C_ALIBI + 256 * i
        c[:, at:at + P] = -slopes[i] * (dist + P) / SCALE
        c[:, at + P:at + 2 * P] = np.where(dist >= 0, -slopes[i] * dist / SCALE, NEG)
    tri = (t[:, None] <= np.arange(S)[None, :]).astype(np.float32)
    c[:, C_TRI:C_TRI + S] = tri
    for q in range(TT):
        for h in range(NH):
            at = (q * NH + h) * CMPW
            gone = (q * P + t[:, None]) - (np.arange(CMPW) * 16 + 31)[None, :]
            seen = (gone >= 0) & (np.arange(CMPW) < CMP)[None, :]
            c[:, C_CMPB + at:C_CMPB + at + CMPW] = np.where(seen, -slopes[2 * h + 1] * gone, NEG)
            c[:, C_CMPM + at:C_CMPM + at + CMPW] = seen
    inv = (np.float32(10000.0) ** (-np.arange(0, 32, 2, dtype=np.float32) / np.float32(32))).astype(np.float32)
    both = np.concatenate([inv, inv])
    for base in (0, 64):
        c[base:base + 32, C_INV] = both
        c[base + 32:base + 64, C_INV] = np.concatenate([-inv, inv])
        c[base:base + 32, C_OFF] = 0.25
        c[base:base + 32, C_PHASE] = np.pi / 2
    for h in range(NH):
        c[h, C_SEL + h] = 1.0
        c[NH + h, C_SEL + 4 + h] = 1.0
        c[NH + h, C_SEL + 8 + h] = -1.0
        c[h, C_SEL + 12 + h] = 1.0
    return c


def build(nc, a, out):
    with ExitStack() as ctx:
        def sb(name, shape, dt=F32):
            return ctx.enter_context(nc.sbuf_tensor(name, shape, dt))

        def sem(name):
            return ctx.enter_context(nc.semaphore(name))

        raw = sb("raw", [P, RAW_SLOTS, 1024])
        wh = sb("wh", [P, WT_SLOTS, 1024], F32R)
        wl = sb("wl", [P, WT_SLOTS, 1024], F32R)
        xb = sb("xb", [P, TT, D])
        xTh, xTl = sb("xTh", [P, KT, S], F32R), sb("xTl", [P, KT, S], F32R)
        memTh, memTl = sb("memTh", [P, KT, S], F32R), sb("memTl", [P, KT, S], F32R)
        gb = sb("gb", [P, 2, D])
        gates = sb("gates", [P, 2 * KT, S])
        z = sb("z", [P, KT, S])
        oTh, oTl = sb("oTh", [P, 4, S], F32R), sb("oTl", [P, 4, S], F32R)
        qD, kD, vD = sb("qD", [P, NH, S]), sb("kD", [P, NH, S]), sb("vD", [P, TT, 256])
        qC, kC, vC = sb("qC", [P, 2, S]), sb("kC", [P, 2, S]), sb("vC", [P, TT, 256])
        qA, kA, vA = sb("qA", [P, 2, S]), sb("kA", [P, 2, S]), sb("vA", [P, TT, 256])
        qB, kB, vB = sb("qB", [P, 2, S]), sb("kB", [P, 2, S]), sb("vB", [P, TT, 128])
        x2 = sb("x2", [P, 2, S])
        blkf = sb("blkf", [P, 2, 16, CMP])
        blkh, blkl = sb("blkh", [P, 2, 16, CMPW], F32R), sb("blkl", [P, 2, 16, CMPW], F32R)
        hx, hu, hg = (sb(n, [P, 2, 2 * CMPW]) for n in ("hx", "hu", "hg"))
        hkh, hkl = sb("hkh", [P, 2, CMPW], F32R), sb("hkl", [P, 2, CMPW], F32R)
        hvh, hvl = sb("hvh", [P, 2, NH, 32], F32R), sb("hvl", [P, 2, NH, 32], F32R)
        kcmp, vcmp = sb("kcmp", [P, 2 * CMPW]), sb("vcmp", [P, HD])
        pc = sb("pc", [P, TT, NH, 32])
        pcT = sb("pcT", [P, S])
        cstat = sb("cstat", [P, 3, 8])
        pS = sb("pS", [P, 2, 512])
        pT = sb("pT", [P, 2, 512])
        stat = sb("stat", [P, 2, 4, 2])
        gl, gth = sb("gl", [P, TT, 16]), sb("gth", [P, TT, 12])
        gt = sb("gt", [P, TT, 12])
        fx = sb("fx", [P, 5, TT, 4])
        ls8 = sb("ls8", [P, TT, 8])
        vbias = sb("vbias", [P, 656])
        cs, csq = sb("cs", [P, S]), sb("csq", [P, S])
        const = sb("const", [P, NCONST])
        cols = sb("cols", [P, 96 + 128 + 70])
        cur = sb("cur", [P, NCOLS])
        ones = sb("ones", [P, P])
        bst, mv = sb("bst", [P, TT, 2, 6]), sb("mv", [P, TT, 2])
        vare, rstd, nmr = sb("vare", [P, TT]), sb("rstd", [P, TT]), sb("nmr", [P, TT])
        mhalf, eps_rms, fence = sb("mhalf", [P, 1]), sb("eps_rms", [P, 1]), sb("fence", [P, 1])
        ps = ctx.enter_context(nc.psum_tensor("ps", [P, 8, 512], F32))

        cqf, sq, rms = gates[:, 0:3, :], gates[:, 3:6, :], gates[:, 6:8, :]
        krt, krs = gates[:, 8, :], gates[:, 9, :]
        rows = gates[:, 0:3, 0:P]
        stage = gates[:, 8:16, :].rearrange("p a s -> p (a s)").rearrange("p (t d) -> p t d", t=TT)
        trig = pS[:, :, :].rearrange("p i n -> p (i n)")
        posi, angle = gates[:, 4, :].bitcast(I32), gates[:, 5, :]
        hs, hf = z[:, 0:2, :], z[:, 2:4, :]
        lq, rk = z[0:8, 0:4, :], z[0:8, 4:8, :]
        xq, xk, xv = qA, kA, vA

        const_in, cast_in = sem("const_in"), sem("cast_in")
        raw_in = [sem(f"raw_in{i}") for i in range(RAW_SLOTS)]
        pair_in = sem("pair_in")
        hi_done, lo_done = sem("hi_done"), sem("lo_done")
        units_used = sem("units_used")
        pa_ready, pa_out = sem("pa_ready"), sem("pa_out")
        pd_ready, pd_out = sem("pd_ready"), sem("pd_out")
        cols_ready, cols_psum = sem("cols_ready"), sem("cols_psum")
        trig_done, setup_done = sem("trig_done"), sem("setup_done")
        acc_ready, stat_done, rstd_done = sem("acc_ready"), sem("stat_done"), sem("rstd_done")
        nm_done, xn_done = sem("nm_done"), sem("xn_done")
        tp_ready, xf_done, xT_ready = sem("tp_ready"), sem("xf_done"), sem("xT_ready")
        x_mul, x_done = sem("x_mul"), sem("x_done")
        gb_in, vb_in, out_done = sem("gb_in"), sem("vb_in"), sem("out_done")
        silu_done, gu_out, hT_ready = sem("silu_done"), sem("gu_out"), sem("hT_ready")
        sq_done, cqn_ready = sem("sq_done"), sem("cqn_ready")
        kr_shift, kr_added, kr_sum = sem("kr_shift"), sem("kr_added"), sem("kr_sum")
        gth_done, fx_abs, fx_exp, fx_ln, ls_ready = (sem("gth_done"), sem("fx_abs"), sem("fx_exp"), sem("fx_ln"),
                                                     sem("ls_ready"))
        blk_ready, hu_done, hg_done, hid_ready = sem("blk_ready"), sem("hu_done"), sem("hg_done"), sem("hid_ready")
        s_ready, s_out, s_max = sem("s_ready"), sem("s_out"), sem("s_max")
        p_exp, p_ready = sem("p_exp"), sem("p_ready")
        pt_ready, pt_out, pv_done = sem("pt_ready"), sem("pt_out"), sem("pv_done")
        o_hi, o_out = sem("o_hi"), sem("o_out")
        zh_done, z_ready, y_out = sem("zh_done"), sem("z_ready"), sem("y_out")
        xk_out, xv_out, xq_out = sem("xk_out"), sem("xv_out"), sem("xq_out")
        xs_ready, xmax, xexp, xp_ready = sem("xs_ready"), sem("xmax"), sem("xexp"), sem("xp_ready")
        xpt_ready, xpt_out, xo_ready, xo_hi, xo_out = (sem("xpt_ready"), sem("xpt_out"), sem("xo_ready"),
                                                       sem("xo_hi"), sem("xo_out"))
        credits_set, sin_done = sem("credits_set"), sem("sin_done")

        ident = const[:, C_ID:C_ID + P]

        def bias_table(kind, h, q):
            if kind in "dc":
                at = C_CAUSAL
            else:
                at = C_ALIBI + 256 * (2 * h + (kind != "a"))
            return const[:, at + P:at + 2 * P] if q == 0 else const[:, at:at + 2 * P]

        def col(i):
            return cur[:, i:i + 1]

        def k_rows(w):
            return w.rearrange("(kt p) n -> p kt n", p=P)

        def ffn_source(w_in, w_out, l, what, f):
            if what == "out":
                return w_out[l].rearrange("(f p) n -> f p n", p=P)[f]
            return k_rows(w_in[l]).rearrange("p kt (c f j) -> c f p kt j", c=2, f=FT)[0 if what == "g" else 1][f]

        def mixer_source(unit, l):
            kind, x = unit[0], unit[1] if len(unit) > 1 else 0
            w_in = k_rows(a["w_in"][l])
            if kind == "col" and x == 0:
                tiles = a["w_in"].rearrange("l (kt p) n -> (l kt) p n", p=P)[bass.ds(l * KT, KT)]
                return tiles.rearrange("kt p n -> p kt n")[:, :, 0:P]
            if kind == "col":
                return w_in[:, :, x:x + P]
            if kind == "kr":
                return w_in[:, :, x:x + 32]
            if kind == "narrow":
                return w_in[:, :, x:x + unit[2]]
            if kind == "pair":
                return w_in[:, :, x:x + 256].rearrange("p kt (c j) -> p kt c j", c=2)[:, :, :, 0:HD]
            if kind == "uq":
                return k_rows(a["mla_w_uq"][l])
            if kind == "ukv":
                return a["mla_w_ukv"][l]
            if kind == "w1":
                return a["nsa_cmp_w1"][l][x].rearrange("(c lp p) n -> c p lp n", c=4, p=P)[unit[2]]
            if kind == "w2":
                return a["nsa_cmp_w2"][l].rearrange("b (kt p) n -> p b kt n", p=P)
            if kind == "gate":
                at = G_M + BRANCHES[x] * D + unit[2] * P
                return w_in[:, :, at:at + P]
            if kind == "branch":
                w = k_rows(a["w_branch"][l][BRANCHES[x]])
                return w[:, :, 512 * unit[2]:512 * unit[2] + 512]
            if kind == "wo":
                return a["w_o"][l].rearrange("(k p) n -> k p n", p=P)[x]
            if kind == "xk":
                return k_rows(a["xa_w_kv"][l])[:, :, P * x:P * x + P]
            if kind == "xv":
                return k_rows(a["xa_w_kv"][l])[:, :, 256 + P * x:256 + P * x + P]
            if kind == "xq":
                return k_rows(a["xa_w_q"][l])[:, :, P * x:P * x + P]
            return a["xa_w_o"][l].rearrange("(k p) n -> k p n", p=P)[x]

        def raw_view(unit, slot):
            r = raw[:, slot, :]
            kind = unit[0]
            if kind in ("col", "gate", "xk", "xv", "xq"):
                return r.rearrange("p (kt n) -> p kt n", kt=KT)
            if kind == "kr":
                return r[:, 0:KT * 32].rearrange("p (kt n) -> p kt n", kt=KT)
            if kind == "narrow":
                return r[:, 0:KT * unit[2]].rearrange("p (kt n) -> p kt n", kt=KT)
            if kind == "pair":
                return r.rearrange("p (kt c j) -> p kt c j", kt=KT, c=2)
            if kind == "uq":
                return r[:, 0:768].rearrange("p (kt n) -> p kt n", kt=2)
            if kind == "ukv":
                return r[:, 0:512]
            if kind == "w1":
                return r.rearrange("p (lp n) -> p lp n", lp=4)
            if kind == "w2":
                return r[:, 0:256].rearrange("p (b kt n) -> p b kt n", b=2, kt=2)
            if kind == "branch":
                return r.rearrange("p (kt n) -> p kt n", kt=2)
            return r

        def split_views(unit, rslot, w):
            r = raw[:, rslot, :]
            kind = unit[0]
            if kind == "kr":
                s_, d_ = raw_view(unit, rslot), w.rearrange("p (kt n) -> p kt n", kt=KT)
                pairs = []
                for at in (0, 64):
                    pairs += [(s_, d_[:, :, at:at + 32]), (s_[:, :, 16:32], d_[:, :, at + 32:at + 48]),
                              (s_[:, :, 0:16], d_[:, :, at + 48:at + 64])]
                return pairs
            if kind == "uq":
                s_ = r[:, 0:768].rearrange("p (kh n) -> p kh n", n=96)
                d_ = w.rearrange("p (kh n) -> p kh n", n=P)
                return [(s_, d_[:, :, 0:96]), (s_[:, :, 80:96], d_[:, :, 96:112]), (s_[:, :, 64:80], d_[:, :, 112:128])]
            if kind == "ukv":
                s_ = r[:, 0:512].rearrange("p (h c n) -> p c h n", h=NH, c=2)
                return [(s_, w[:, 0:512].rearrange("p (c h n) -> p c h n", h=NH, c=2))]
            if kind == "w2":
                s_ = raw_view(unit, rslot)
                d_ = w[:, 0:512].rearrange("p (b kt n) -> p b kt n", b=2, kt=2)
                return [(s_, d_[:, :, :, 0:HD]), (s_, d_[:, :, :, HD:P])]
            n = KT * unit[2] if kind == "narrow" else 1024
            return [(r[:, 0:n], w[:, 0:n])]

        PLAIN = ("ffn",)

        def unit_at(j):
            return MIXER[j - MIX0] if MIX0 <= j < FFN2_0 else PLAIN

        def units_before(l, j, more=0):
            return l * UNITS + more * 6 + j

        def raw_fills(l, j, more=0):
            return l * (UNITS // RAW_SLOTS) + more * 2 + j // RAW_SLOTS + 1

        def at(l, per_layer, n):
            return l * per_layer + n

        def unit_done(l, j, more=0):
            return units_before(l, j, more) + 1 + WT_SLOTS

        def signal(name):
            return units_used if name in ENDS_UNIT else pa_ready if name in PA else pd_ready

        def ready(l, name):
            if name in ENDS_UNIT:
                return units_used, unit_done(l, MIX0 + ENDS_UNIT[name])
            own = PA_MID if name in PA else PD_MID
            return (pa_ready if name in PA else pd_ready), at(l, len(own), own.index(name) + 1)

        def free(l, name):
            own = PA if name in PA else PD
            return (pa_out if name in PA else pd_out), at(l, len(own), own.index(name) + 1)

        def evacuated(l, name):
            own = PA if name in PA else PD
            return (pa_out if name in PA else pd_out), at(l, len(own), own.index(name) + 3)

        block = ctx.enter_context(nc.Block())

        @block.sync
        def _(sp):
            sp.dma_start(const[:, :], a["const"]).then_inc(const_in, 16)
            sp.dma_start(xb[:, :, :], a["x"][0].rearrange("(t p) d -> p t d", p=P)).then_inc(const_in, 16)
            sp.dma_start(stage, a["mem"][0].rearrange("(t p) d -> p t d", p=P)).then_inc(const_in, 16)
            pos_row = a["positions"]
            sp.dma_start(posi, pos_row.broadcast_to([P, S])).then_inc(const_in, 16)
            for l in range(L):
                b = a["b_in"][l]

                def bias_rows(r0, at_, n):
                    sp.dma_start(rows[l * NB + r0:l * NB + r0 + n, 0, :],
                                 b[at_:at_ + n * P].rearrange("(r c) -> r c", c=P)).then_inc(const_in, 16)

                def bias_part(r0, c0, at_, n):
                    sp.dma_start(rows[l * NB + r0:l * NB + r0 + 1, 0, c0:c0 + n],
                                 b[at_:at_ + n].unsqueeze(0)).then_inc(const_in, 16)
                bias_rows(BIAS["dcq0"], D_CQ, 3)
                for c0 in (0, 64):
                    bias_part(BIAS["kr"], c0, D_KR, 32)
                    bias_part(BIAS["kr"], c0 + 32, D_KR + 16, 16)
                    bias_part(BIAS["kr"], c0 + 48, D_KR, 16)
                bias_rows(BIAS["kc"], B_KC, 1)
                bias_part(BIAS["ks"], 0, B_KS, HD)
                bias_part(BIAS["ks"], HD, B_KW, HD)
                bias_rows(BIAS["bq0"], B_Q, 2)
                bias_rows(BIAS["cq0"], C_Q, 4)
                bias_rows(BIAS["aq0"], A_Q, 4)
                bias_rows(GB0, G_M, 32)
            sp.dma_start(rows[0:64, 1, :], a["ln_g"].rearrange("l s (k c) -> (l s k) c", c=P)).then_inc(const_in, 16)
            sp.dma_start(rows[64:128, 1, :], a["ln_b"].rearrange("l s (k c) -> (l s k) c", c=P)).then_inc(const_in, 16)
            sp.dma_start(rows[0:64, 2, :], a["nsa_cmp_pos"].rearrange("l b (r two) c -> (l b r) (two c)", two=2)).then_inc(const_in, 16)
            sp.dma_start(rows[64:68, 2, :], a["mla_q_norm"].rearrange("l (k c) -> (l k) c", c=P)).then_inc(const_in, 16)
            sp.dma_start(rows[68:70, 2, :], a["mla_kv_norm"]).then_inc(const_in, 16)

            def load(src, dst, l, j, more=0):
                sp.wait_ge(lo_done, units_before(l, j, more) + 1)
                sp.dma_start(dst, src).then_inc(raw_in[j % RAW_SLOTS], 16)

            def load_ffn(l, j, w_in, w_out, what, f, more=0):
                dst = raw[:, j % RAW_SLOTS, :]
                if what != "out":
                    dst = dst.rearrange("p (kt n) -> p kt n", kt=KT)
                load(ffn_source(w_in, w_out, l, what, f), dst, l, j, more)

            def ffn(l, j0, w_in, w_out):
                for n, (what, f) in enumerate((("g", 0), ("u", 0), ("g", 1), ("u", 1), ("out", 0))):
                    load_ffn(l, j0 + n, w_in, w_out, what, f)
                with sp.Fori(0, FT // 2 - 1) as i:
                    for n, (what, f) in enumerate((("g", 2), ("u", 2), ("out", 1), ("g", 3), ("u", 3), ("out", 2))):
                        load_ffn(l, j0 + 5 + n, w_in, w_out, what, i * 2 + f, i)
                load_ffn(l, j0 + FFN_UNITS - 1, w_in, w_out, "out", FT - 1)

            with sp.Fori(0, L) as l:
                ffn(l, 0, a["ffn1_w_in"], a["ffn1_w_out"])
                for n, unit in enumerate(MIXER):
                    j = MIX0 + n
                    src, dst = mixer_source(unit, l), raw_view(unit, j % RAW_SLOTS)
                    if unit[0] == "pair":
                        sp.wait_ge(lo_done, units_before(l, j) + 1)
                        sp.dma_start(dst[:, :, 0, :], src[:, :, 0, :]).then_inc(pair_in, 16)
                        src, dst = src[:, :, 1, :], dst[:, :, 1, :]
                    load(src, dst, l, j)
                ffn(l, FFN2_0, a["ffn2_w_in"], a["ffn2_w_out"])

        N_CONST_DMAS = 4 + L * 14 + 5

        @block.gpsimd
        def _(pool):
            pool.memset(mhalf[:, :], -0.5)
            pool.memset(ones[:, :], 1.0)
            pool.memset(csq[0:64, :], 1.0)
            pool.memset(kcmp[:, :], 0.0)
            pool.memset(blkh[:, :, :, :].bitcast(F32), 0.0)
            pool.memset(blkl[:, :, :, :].bitcast(F32), 0.0)
            pool.memset(hvh[:, :, :, :].bitcast(F32), 0.0)
            pool.memset(hvl[:, :, :, :].bitcast(F32), 0.0)
            pool.memset(pc[:, :, :, :], 0.0).then_inc(setup_done, 1)
            pool.wait_ge(setup_done, 1)

            def norm(l, s):
                pool.wait_ge(x_done, at(l, 4 * TT, TT * s + TT))
                pool.dma_start(gb[:, 0, :], a["ln_g"][l][s:s + 1, :].broadcast_to([P, D])).then_inc(gb_in, 16)
                pool.dma_start(gb[:, 1, :], a["ln_b"][l][s:s + 1, :].broadcast_to([P, D])).then_inc(gb_in, 16)
                for t in range(TT):
                    pool.wait_ge(stat_done, at(l, 4 * TT, TT * s + t + 1))
                    pool.tensor_tensor(rstd[:, t:t + 1], vare[:, t:t + 1], mhalf[:, :], ALU.pow).then_inc(rstd_done, 1)
                pool.wait_ge(tp_ready, at(l, 16, 8 + 4 * s + 4))
                pool.wait_ge(gb_in, at(l, 4 * 32, 32 * s + 32))
                for t in range(TT):
                    pool.tensor_tensor(xb[:, t, :], xb[:, t, :], gb[:, 0, :], ALU.mult).then_inc(x_mul, 1)
                    pool.wait_ge(x_mul, at(l, 4 * TT, TT * s + t + 1))
                    pool.tensor_tensor(xb[:, t, :], xb[:, t, :], gb[:, 1, :], ALU.add).then_inc(x_done, 1)

            with pool.Fori(0, L) as l:
                bl = a["b_in"][l].unsqueeze(0)
                for to, frm, n in ((0, A_V, 256), (256, B_VS, HD), (320, B_VW, HD + 12), (396, C_V, 260)):
                    pool.dma_start(vbias[:, to:to + n], bl[:, frm:frm + n].broadcast_to([P, n])).then_inc(vb_in, 16)
                for s in range(4):
                    norm(l, s)
            for t in range(TT):
                pool.wait_ge(x_done, L * 4 * TT + t + 1)
                pool.dma_start(out[0].rearrange("(t p) d -> t p d", p=P)[t], xb[:, t, :]).then_inc(out_done, 16)
            pool.wait_ge(out_done, TT * 16)

        def tp_bank(q):
            return ps[:, 6 + q % 2, :].rearrange("p (k t n) -> p k t n", k=2, t=TT)

        def pa_tile(name):
            return ps[:, PA.index(name) % 2, :]

        def pd_tile(name):
            return ps[:, 2 + PD.index(name) % 2, 0:256]

        S_BANK = ps[:, 4, :]

        PT_BANK = ps[:, 5, :]

        def o_bank(pair):
            return ps[:, 6 + pair % 2, 0:S]

        def value_tile(kind, h, t):
            if kind == "s":
                return vB[:, t, 0:HD]
            if kind == "w":
                return vB[:, t, HD:2 * HD]
            v = {"d": vD, "c": vC, "a": vA}[kind]
            return v[:, t, HD * h:HD * h + HD]

        @block.tensor
        def _(pe):
            def mm3(o, lh, ll, rh, rl, first, last):
                pe.matmul(o, lh, rh, start=first, stop=False)
                pe.matmul(o, lh, rl, start=False, stop=False)
                return pe.matmul(o, ll, rh, start=False, stop=last)

            def transpose_in(l, idx, src, l_per=16):
                for q in range(4):
                    if q >= 2:
                        pe.wait_ge(xf_done, at(l, 32, 8 * idx + 2 * (q - 2) + 2))
                    for k in range(2):
                        for t in range(TT):
                            last = pe.transpose(tp_bank(q)[:, k, t, :], src[:, t, P * (2 * q + k):P * (2 * q + k) + P], ident)
                    last.then_inc(tp_ready, 1)

            def take(l, j, more=0):
                pe.wait_ge(lo_done, units_before(l, j, more) + RAW_SLOTS + 1)
                s_ = j % WT_SLOTS
                return wh[:, s_, :], wl[:, s_, :]

            pe.wait_ge(const_in, 16 * N_CONST_DMAS)
            pe.wait_ge(setup_done, 1)
            for i, (n, at_) in enumerate(((96, 0), (128, 96), (70, 224))):
                last = pe.transpose(ps[:, 5, at_ % 512:at_ % 512 + n], rows[0:n, i, :], ident[0:n, 0:n])
            last.then_inc(cols_psum, 1)
            transpose_in(0, 0, stage)
            pe.wait_ge(xf_done, 8)
            transpose_in(0, 1, xb)

            def feature_tile(o, h_, l_, l, ln=None):
                hv, lv = (w.rearrange("p (kt n) -> p kt n", kt=KT) for w in (h_, l_))
                for k in range(KT):
                    if ln is not None and k % 2 == 0:
                        pe.wait_ge(xT_ready, at(l, 16, 4 * ln + k // 2 + 1))
                    last = mm3(o, hv[:, k, :], lv[:, k, :], xTh[:, k, :], xTl[:, k, :], k == 0, k == KT - 1)
                return last

            def token_tile(o, h_, l_, n, xh=xTh, xl=xTl):
                hv, lv = (w[:, 0:KT * n].rearrange("p (kt n) -> p kt n", kt=KT) for w in (h_, l_))
                for t in range(TT):
                    for k in range(KT):
                        last = mm3(o[:, t, :], xh[:, k, P * t:P * t + P], xl[:, k, P * t:P * t + P],
                                   hv[:, k, :], lv[:, k, :], k == 0, k == KT - 1)
                return last

            def ffn(l, which, j0, ln):
                def hidden(f, j, more=0, ln_=None):
                    h_, l_ = take(l, j, more)
                    pe.wait_ge(gu_out, at(l, 2 * FT, FT * which + f + 1) + more * 2)
                    feature_tile(ps[:, 4 + f % 2, 0:S], h_, l_, l, ln_).then_inc(units_used, 1)
                    h_, l_ = take(l, j + 1, more)
                    feature_tile(ps[:, 4 + f % 2, S:2 * S], h_, l_, l).then_inc(units_used, 1)

                def down(f, j, more=0):
                    h_, l_ = take(l, j, more)
                    pe.wait_ge(hT_ready, at(l, 2 * FT, FT * which + f + 1) + more * 2)
                    for t in range(TT):
                        th, tl = oTh[:, f % 2, P * t:P * t + P], oTl[:, f % 2, P * t:P * t + P]
                        for c in range(2):
                            w = slice(512 * c, 512 * c + 512)
                            last = mm3(ps[:, 2 * t + c, :], th, tl, h_[:, w], l_[:, w], f == 0, f == FT - 1)
                        if f == FT - 1 and t == 0:
                            last.then_inc(acc_ready, 1)
                    last.then_inc(units_used, 1)

                hidden(0, j0, ln_=ln)
                hidden(1, j0 + 2)
                down(0, j0 + 4)
                with pe.Fori(0, FT // 2 - 1) as i:
                    hidden(2, j0 + 5, i)
                    down(1, j0 + 7, i)
                    hidden(3, j0 + 8, i)
                    down(2, j0 + 10, i)
                down(FT - 1, j0 + FFN_UNITS - 1)

            def scores(l, n):
                b, h, kind = HEADS[n]
                pe.wait_ge(s_out, at(l, NSLOT, n + 1))
                o = S_BANK
                if kind == "cmp":
                    for q in range(TT):
                        for hh in (0, 2):
                            i = (q * NH + hh) * CMPW
                            last = pe.matmul(o[:, i:i + 2 * CMPW], qB[:, hh // 2, P * q:P * q + P], kcmp[:, :],
                                             start=True, stop=True)
                    last.then_inc(s_ready, 1)
                    return
                for q in range(TT):
                    ob = o[:, 0:P] if q == 0 else o[:, P:3 * P]
                    nk = P * (q + 1)
                    if kind == "d":
                        last = pe.matmul(ob, qD[:, h, P * q:P * q + P], kD[:, h, 0:nk], start=True, stop=True)
                        continue
                    r = slice(64 * (h % 2), 64 * (h % 2) + 64)
                    qq = {"c": qC, "a": qA}.get(kind, qB)[r, h // 2, P * q:P * q + P]
                    if kind in "sw":
                        kk = kB[r, 0 if kind == "s" else 1, 0:nk]
                    else:
                        kk = (kC if kind == "c" else kA)[r, h // 2, 0:nk]
                    last = pe.matmul(ob, qq, kk, start=True, stop=(kind != "c"))
                    if kind == "c":
                        last = pe.matmul(ob, lq[:, h, P * q:P * q + P], rk[:, h, 0:nk], start=False, stop=True)
                last.then_inc(s_ready, 1)

            def turn(l, n):
                pe.wait_ge(p_ready, at(l, NSLOT, n + 1))
                pe.wait_ge(pt_out, at(l, NSLOT, n + 1))
                for i in range(2 if HEADS[n][2] == "cmp" else 3):
                    src = (pc[:, i, :, :].rearrange("p h c -> p (h c)") if HEADS[n][2] == "cmp"
                           else pS[:, n % 2, P * i:P * i + P])
                    last = pe.transpose(PT_BANK[:, P * i:P * i + P], src, ident)
                last.then_inc(pt_ready, 1)

            def cmp_values(h):
                r = slice(32 * h, 32 * h + CMPW)
                return pe.matmul(o_bank(6 + h // 2)[64 * (h % 2):64 * (h % 2) + 64, :], vcmp[r, :], pcT[r, :],
                                 start=True, stop=False)

            def values(l, n):
                b, h, kind = HEADS[n]
                pair = 2 * b + h // 2
                pe.wait_ge(pt_out, at(l, NSLOT, n + 2))
                if kind == "cmp":
                    pe.wait_ge(o_out, at(l, PAIRS, 6 + 1))
                    cmp_values(0)
                    cmp_values(1).then_inc(pv_done, 1)
                    return
                if kind == "s" and h == 2:
                    pe.wait_ge(o_out, at(l, PAIRS, 7 + 1))
                    cmp_values(2)
                    cmp_values(3)
                if kind in "dca" and h % 2 == 0:
                    pe.wait_ge(o_out, at(l, PAIRS, pair + 1))
                o = o_bank(pair)[64 * (h % 2):64 * (h % 2) + 64, :]
                pe.matmul(o, value_tile(kind, h, 0), pT[:, n % 2, 0:S], start=kind in "dca", stop=False)
                last = pe.matmul(o[:, P:S], value_tile(kind, h, 1), pT[:, n % 2, S:S + P], start=False,
                                 stop=kind != "s")
                last.then_inc(pv_done, 1)

            def project(l):
                for n in range(NPROJ):
                    h_, l_ = take(l, MIX0 + n)
                    if n in MAIN_PA:
                        name = MAIN_PA[n]
                        pe.wait_ge(*free(l, name))
                        feature_tile(pa_tile(name)[:, 0:S], h_, l_, l, 2 if n == 0 else None).then_inc(signal(name), 1)
                    elif n == U_KR:
                        pe.wait_ge(*free(l, "kr"))
                        feature_tile(pd_tile("kr"), h_, l_, l).then_inc(signal("kr"), 1)
                    elif n in (U_VS, U_CV, U_CV + 1, U_AV, U_AV + 1):
                        name = {U_VS: "vs", U_CV: "cv0", U_CV + 1: "cv1", U_AV: "av0", U_AV + 1: "av1"}[n]
                        pe.wait_ge(*free(l, name))
                        o = pd_tile(name).rearrange("p (t n) -> p t n", t=TT)
                        token_tile(o, h_, l_, P).then_inc(signal(name), 1)
                    elif n in (U_G, U_F):
                        if n == U_G:
                            pe.wait_ge(*free(l, "gf"))
                        o = pd_tile("gf")[:, 0:32].rearrange("p (t n) -> p t n", t=TT)
                        c0, w = (0, 12) if n == U_G else (12, 4)
                        token_tile(o[:, :, c0:c0 + w], h_, l_, w).then_inc(units_used, 1)
                    elif n == U_UQ:
                        pe.wait_ge(cqn_ready, at(l, 1, 1))
                        for h in range(NH):
                            name = f"q{h}"
                            pe.wait_ge(*free(l, name))
                            for k in range(2):
                                c0 = 512 * k + P * h
                                last = mm3(pd_tile(name), h_[:, c0:c0 + P], l_[:, c0:c0 + P],
                                           oTh[:, k, :], oTl[:, k, :], k == 0, k == 1)
                            last.then_inc(signal(name), 1)
                    elif n == U_UKV:
                        for i in range(2):
                            pe.wait_ge(*free(l, f"kn{i}"))
                            mm3(pa_tile(f"kn{i}")[:, 0:S], h_[:, P * i:P * i + P], l_[:, P * i:P * i + P],
                                oTh[:, 2, :], oTl[:, 2, :], True, True).then_inc(signal(f"kn{i}"), 1)
                        for t in range(TT):
                            pe.wait_ge(*free(l, f"vd{t}"))
                            mm3(pd_tile(f"vd{t}"), oTh[:, 2, P * t:P * t + P], oTl[:, 2, P * t:P * t + P],
                                h_[:, 256:512], l_[:, 256:512], True, True).then_inc(signal(f"vd{t}"), 1)
                    elif U_W1 <= n < U_W1 + 8:
                        br, c = divmod(n - U_W1, 4)
                        name = f"hid{br}"
                        if c == 0:
                            pe.wait_ge(*free(l, name))
                        if n == U_W1:
                            pe.wait_ge(blk_ready, at(l, 1, 1))
                        wvh, wvl = (w.rearrange("p (lp n) -> p lp n", lp=4) for w in (h_, l_))
                        for half in range(2):
                            o = pd_tile(name)[:, (2 * c + half) * CMPW:(2 * c + half + 1) * CMPW]
                            for lp in range(4):
                                last = mm3(o, wvh[:, lp, P * half:P * half + P], wvl[:, lp, P * half:P * half + P],
                                           blkh[:, br, 4 * c + lp, :], blkl[:, br, 4 * c + lp, :], lp == 0, lp == 3)
                        last.then_inc(units_used, 1)
                    elif n == U_W2:
                        pe.wait_ge(hid_ready, at(l, 2, 2))
                        pe.wait_ge(*free(l, "cmp"))
                        o = pa_tile("cmp")
                        wvh, wvl = (w[:, 0:512].rearrange("p (b kt n) -> p b kt n", b=2, kt=2) for w in (h_, l_))
                        for k in range(2):
                            mm3(o[:, 0:CMPW], wvh[:, 0, k, :], wvl[:, 0, k, :], hkh[:, k, :], hkl[:, k, :], k == 0, k == 1)
                        for k in range(2):
                            last = mm3(o[:, 64:128], hvh[:, k, :, :].rearrange("p h c -> p (h c)"),
                                       hvl[:, k, :, :].rearrange("p h c -> p (h c)"),
                                       wvh[:, 1, k, 0:HD], wvl[:, 1, k, 0:HD], k == 0, k == 1)
                        last.then_inc(signal("cmp"), 1)
                    if n == 7:
                        pe.wait_ge(sq_done, at(l, 1, 1))
                        pe.wait_ge(*free(l, "ssq"))
                        o = pa_tile("ssq")
                        for k in range(2):
                            pe.matmul(o[:, 0:S], ones[:, :], sq[:, k, :], start=(k == 0), stop=(k == 1))
                        pe.matmul(o[:, S:2 * S], ones[:, :], sq[:, 2, :], start=True, stop=True)\
                            .then_inc(signal("ssq"), 1)
                    if n == U_W1 + 3:
                        pe.wait_ge(ls_ready, at(l, 1, 1))
                        pe.wait_ge(*free(l, "decay"))
                        o = pd_tile("decay")[0:8, :]
                        tri = const[:, C_TRI:C_TRI + S]
                        pe.matmul(o, ls8[:, 0, :], tri, start=True, stop=False)
                        pe.matmul(o[:, P:S], ls8[:, 1, :], tri[:, 0:P], start=False, stop=True)\
                            .then_inc(signal("decay"), 1)

            def attend(l):
                pe.wait_ge(kr_sum, at(l, 2, 2))
                pe.wait_ge(*evacuated(l, "cmp"))
                pe.wait_ge(*evacuated(l, "av1"))
                step = 0
                for n in range(NPROJ, U_WO):
                    kind, b, i = MIXER[n]
                    h_, l_ = take(l, MIX0 + n)
                    if kind == "gate":
                        if step < NSLOT:
                            scores(l, step)
                        name = f"gate{b}_{i}"
                        pe.wait_ge(*free(l, name))
                        feature_tile(pa_tile(name)[:, 0:S], h_, l_, l).then_inc(signal(name), 1)
                        if 1 <= step <= NSLOT:
                            turn(l, step - 1)
                        if 2 <= step <= NSLOT + 1:
                            values(l, step - 2)
                        step += 1
                        continue
                    if i == 0:
                        pe.wait_ge(o_out, at(l, PAIRS, 2 * b + 2 + 2))
                    wvh, wvl = (w.rearrange("p (kt n) -> p kt n", kt=2) for w in (h_, l_))
                    for q in range(4):
                        name = f"y{b}_{4 * i + q}"
                        pe.wait_ge(*free(l, name))
                        for k in range(2):
                            s_ = 2 * (b % 2) + k
                            last = mm3(pd_tile(name), wvh[:, k, P * q:P * q + P], wvl[:, k, P * q:P * q + P],
                                       oTh[:, s_, :], oTl[:, s_, :], k == 0, k == 1)
                        last.then_inc(signal(name), 1)

            def merged_out(l):
                for k in range(KT):
                    h_, l_ = take(l, MIX0 + U_WO + k)
                    pe.wait_ge(z_ready, at(l, KT, k + 1))
                    for t in range(TT):
                        for c in range(2):
                            w = slice(512 * c, 512 * c + 512)
                            last = mm3(ps[:, 2 * t + c, :], xTh[:, k, P * t:P * t + P], xTl[:, k, P * t:P * t + P],
                                       h_[:, w], l_[:, w], k == 0, k == KT - 1)
                        if k == KT - 1 and t == 0:
                            last.then_inc(acc_ready, 1)
                    last.then_inc(units_used, 1)

            def cross(l):
                j0 = MIX0 + U_X
                for i in range(2):
                    h_, l_ = take(l, j0 + i)
                    hv, lv = (w.rearrange("p (kt n) -> p kt n", kt=KT) for w in (h_, l_))
                    for k in range(KT):
                        last = mm3(ps[:, 4, S * i:S * i + S], hv[:, k, :], lv[:, k, :], memTh[:, k, :], memTl[:, k, :],
                                   k == 0, k == KT - 1)
                    last.then_inc(units_used, 1)
                for i in range(2):
                    h_, l_ = take(l, j0 + 2 + i)
                    o = ps[:, 5, S * i:S * i + S].rearrange("p (t n) -> p t n", t=TT)
                    token_tile(o, h_, l_, P, memTh, memTl).then_inc(units_used, 1)
                pe.wait_ge(xn_done, at(l, 4 * TT, 2 * TT))
                transpose_in(l, 3, xb)
                for i in range(2):
                    h_, l_ = take(l, j0 + 4 + i)
                    if i == 0:
                        pe.wait_ge(xk_out, at(l, 1, 1))
                    feature_tile(ps[:, 4, S * i:S * i + S], h_, l_, l, 3 if i == 0 else None).then_inc(units_used, 1)
                pe.wait_ge(xq_out, at(l, 1, 1))
                pe.wait_ge(xv_out, at(l, 1, 1))
                for h in range(NH):
                    r = slice(64 * (h % 2), 64 * (h % 2) + 64)
                    for q in range(TT):
                        last = pe.matmul(ps[:, h, S * q:S * q + S], xq[r, h // 2, P * q:P * q + P], xk[r, h // 2, :],
                                         start=True, stop=True)
                    last.then_inc(xs_ready, 1)
                for h in range(NH + 1):
                    if h < NH:
                        pe.wait_ge(xp_ready, at(l, NH, h + 1))
                        if h >= 2:
                            pe.wait_ge(xpt_out, at(l, NH, h - 1))
                        bank = ps[:, 5 + h % 2, :]
                        for k in range(TT):
                            for q in range(TT):
                                last = pe.transpose(bank[:, S * k + P * q:S * k + P * q + P],
                                                    pS[:, h % 2, S * q + P * k:S * q + P * k + P], ident)
                        last.then_inc(xpt_ready, 1)
                    if h >= 1:
                        g = h - 1
                        pe.wait_ge(xpt_out, at(l, NH, g + 1))
                        o = ps[64 * (g % 2):64 * (g % 2) + 64, 7 if g < 2 else 4, 0:S]
                        for k in range(TT):
                            last = pe.matmul(o, xv[:, k, HD * g:HD * g + HD], pT[:, g % 2, S * k:S * k + S],
                                             start=(k == 0), stop=(k == TT - 1))
                        last.then_inc(xo_ready, 1)
                for k in range(2):
                    h_, l_ = take(l, j0 + 6 + k)
                    pe.wait_ge(xo_out, at(l, 2, k + 1))
                    for t in range(TT):
                        for c in range(2):
                            w = slice(512 * c, 512 * c + 512)
                            last = mm3(ps[:, 2 * t + c, :], oTh[:, k, P * t:P * t + P], oTl[:, k, P * t:P * t + P],
                                       h_[:, w], l_[:, w], k == 0, k == 1)
                        if k == 1 and t == 0:
                            last.then_inc(acc_ready, 1)
                    last.then_inc(units_used, 1)
                pe.wait_ge(xn_done, at(l, 4 * TT, 3 * TT))
                transpose_in(l, 4, xb)

            pe.sem_inc(units_used, WT_SLOTS)
            with pe.Fori(0, L) as l:
                ffn(l, 0, 0, 1)
                pe.wait_ge(xn_done, at(l, 4 * TT, TT))
                transpose_in(l, 2, xb)
                project(l)
                attend(l)
                merged_out(l)
                cross(l)
                ffn(l, 1, FFN2_0, 4)
                pe.wait_ge(xn_done, at(l, 4 * TT, 4 * TT))
                transpose_in(l, 5, xb)

        @block.scalar
        def _(act):
            def split_hi(l, j, more=0):
                act.wait_ge(raw_in[j % RAW_SLOTS], raw_fills(l, j, more) * 16)
                act.wait_ge(units_used, units_before(l, j, more) + 1)
                if unit_at(j)[0] == "pair":
                    act.wait_ge(pair_in, at(l, 32, 16 if unit_at(j)[1] == B_KS else 32))
                for src, dst in split_views(unit_at(j), j % RAW_SLOTS, wh[:, j % WT_SLOTS, :]):
                    last = act.activation(dst, src, ACT.Copy)
                last.then_inc(hi_done, 1)

            def ahead(l, j, more=0):
                if j + AHEAD < UNITS:
                    split_hi(l, j + AHEAD, more)

            def normalise(l, s):
                for t in range(TT):
                    act.wait_ge(nm_done, at(l, 4 * TT, TT * s + t + 1))
                    act.activation(xb[:, t, :], xb[:, t, :], ACT.Identity, bias=nmr[:, t:t + 1],
                                   scale=rstd[:, t:t + 1]).then_inc(xn_done, 1)

            def evacuate(l, idx, s=None):
                for k in range(KT):
                    if k % 2 == 0:
                        act.wait_ge(tp_ready, at(l, 16, 4 * idx + k // 2 + 1))
                    src = tp_bank(k // 2)[:, k % 2, :, :].rearrange("p t n -> p (t n)")
                    if s is None:
                        act.activation(z[:, k, :], src, ACT.Copy).then_inc(xf_done, 1)
                    else:
                        act.activation(z[:, k, :], src, ACT.Identity, bias=col(LNB + 8 * s + k),
                                       scale=col(LNG + 8 * s + k)).then_inc(xf_done, 1)

            def silu(l, f, up, more=0):
                act.wait_ge(units_used, unit_done(l, up, more))
                act.activation(hs[:, f % 2, :], ps[:, 4 + f % 2, 0:256], ACT.Silu).then_inc(silu_done, 1)

            def ffn(l, j0):
                for n in range(3):
                    ahead(l, j0 + n)
                silu(l, 0, j0 + 1)
                ahead(l, j0 + 3)
                ahead(l, j0 + 4)

                def turn(j, i=0):
                    ahead(l, j, i)
                    silu(l, 1, j - 2, i)
                    for n in range(1, 4):
                        ahead(l, j + n, i)
                    silu(l, 2, j + 1, i)
                    ahead(l, j + 4, i)
                    ahead(l, j + 5, i)
                with act.Fori(0, FT // 2 - 2) as i:
                    turn(j0 + 5, i)
                turn(j0 + 5 + 6 * (FT // 2 - 2))
                silu(l, FT - 1, j0 + FFN_UNITS - 3)
                ahead(l, j0 + FFN_UNITS - 1)

            def pa_wait(l, name):
                act.wait_ge(*ready(l, name))
                return pa_tile(name)

            def pa_main(l, name):
                src = pa_wait(l, name)[:, 0:S]
                bcol = col(BIAS[name])
                if name in ("dcq0", "dcq1", "dckv"):
                    i = ("dcq0", "dcq1", "dckv").index(name)
                    act.activation(cqf[:, i, :], src, ACT.Identity, bias=bcol).then_inc(pa_out, 1)
                elif name == "kc":
                    for i in range(2):
                        r = slice(64 * i, 64 * i + 64)
                        act.activation(x2[0:64, i, :], src[r, :], ACT.Identity, bias=bcol[r, :])
                        last = act.activation(x2[64:128, i, 0:S - 1], src[r, 1:S], ACT.Identity, bias=bcol[r, :])
                    last.then_inc(pa_out, 1)
                elif name == "ks":
                    for i in range(2):
                        r = slice(64 * i, 64 * i + 64)
                        act.activation(kB[0:64, i, :], src[r, :], ACT.Identity, bias=bcol[r, :])
                        last = act.activation(kB[64:128, i, :], src[r, :], ACT.Identity, bias=bcol[r, :])
                    last.then_inc(pa_out, 1)
                else:
                    dst = {"bq": qB, "cq": qC, "ck": kC, "aq": qA, "ak": kA}[name[:2]][:, int(name[2]), :]
                    act.activation(dst, src, ACT.Identity, bias=bcol).then_inc(pa_out, 1)

            def exp_head(l, n):
                if HEADS[n][2] == "cmp":
                    act.wait_ge(s_max, at(l, NSLOT, n + 1))
                    act.activation(pc[:, :, :, 0:CMPW], pc[:, :, :, 0:CMPW], ACT.Exp).then_inc(p_exp, 1)
                    return
                act.wait_ge(s_max, at(l, NSLOT, n + 1))
                i = n % 2
                act.activation(pS[:, i, 0:P], pS[:, i, 0:P], ACT.Exp, bias=stat[:, i, 1, 0:1], accum_out=stat[:, i, 2, 0:1])
                act.activation(pS[:, i, P:3 * P], pS[:, i, P:3 * P], ACT.Exp, bias=stat[:, i, 1, 1:2],
                               accum_out=stat[:, i, 2, 1:2]).then_inc(p_exp, 1)

            def copy_turned(l, n):
                act.wait_ge(pt_ready, at(l, NSLOT, n + 1))
                if HEADS[n][2] == "cmp":
                    act.activation(pcT[:, :], PT_BANK[:, 0:S], ACT.Copy).then_inc(pt_out, 1)
                    return
                if n >= 2:
                    act.wait_ge(pv_done, at(l, NSLOT, n - 1))
                act.activation(pT[:, n % 2, 0:3 * P], PT_BANK[:, 0:3 * P], ACT.Copy).then_inc(pt_out, 1)

            def pair_hi(l, pair):
                act.wait_ge(pv_done, at(l, NSLOT, PAIR_END[pair] + 1))
                s_ = pair % 4
                act.activation(oTh[:, s_, :], o_bank(pair), ACT.Copy).then_inc(o_hi, 1)

            def mixer(l):
                for n in range(NPROJ):
                    ahead(l, MIX0 + n)
                    if n - 1 in MAIN_PA:
                        pa_main(l, MAIN_PA[n - 1])
                    if n == 9:
                        src = pa_wait(l, "ssq")
                        act.activation(rms[:, 0, :], src[:, 0:S], ACT.Sqrt, bias=eps_rms[:, 0:1], scale=1.0 / 256)
                        act.activation(rms[:, 1, :], src[:, S:2 * S], ACT.Sqrt, bias=eps_rms[:, 0:1], scale=1.0 / 128)\
                            .then_inc(pa_out, 1)
                        act.wait_ge(*evacuated(l, "kr"))
                        act.activation(krs[0:32, :], krt[32:64, :], ACT.Copy).then_inc(kr_shift, 1)
                    if n == 12:
                        act.wait_ge(kr_added, at(l, 1, 1))
                        src = krs[0:32, :].unsqueeze(1).broadcast_to([32, NH, S])
                        act.activation(kD[64:96, :, :], src, ACT.Copy).then_inc(kr_sum, 1)
                        act.activation(kD[96:128, :, :], src, ACT.Copy).then_inc(kr_sum, 1)
                        act.wait_ge(*evacuated(l, "gf"))
                        act.activation(gth[:, :, :], gl[:, :, 0:12], ACT.Tanh, scale=0.5).then_inc(gth_done, 1)
                        act.wait_ge(fx_abs, at(l, 1, 1))
                        act.activation(fx[:, 2, :, :], fx[:, 1, :, :], ACT.Exp, scale=-1.0).then_inc(fx_exp, 1)
                        act.wait_ge(fx_exp, at(l, 1, 1))
                        act.activation(fx[:, 3, :, :], fx[:, 2, :, :], ACT.Ln, bias=1.0).then_inc(fx_ln, 1)
                    if n == U_UKV:
                        for i in range(2):
                            src = pa_wait(l, f"kn{i}")
                            act.activation(kD[0:64, 2 * i, :], src[0:64, 0:S], ACT.Copy)
                            act.activation(kD[0:64, 2 * i + 1, :], src[64:128, 0:S], ACT.Copy).then_inc(pa_out, 1)
                    if n in (U_W1 + 5, U_W1 + 9):
                        br = 0 if n == U_W1 + 5 else 1
                        act.wait_ge(hu_done, at(l, 2, br + 1))
                        act.activation(hg[:, br, :], hu[:, br, :], ACT.Tanh, scale=0.7978845608028654).then_inc(hg_done, 1)
                step = 0
                for n in range(NPROJ, U_WO):
                    ahead(l, MIX0 + n)
                    if n == NPROJ:
                        src = pa_wait(l, "cmp")
                        act.activation(kcmp[0:64, 0:CMPW], src[0:64, 0:CMPW], ACT.Copy)
                        act.activation(kcmp[64:128, CMPW:2 * CMPW], src[64:128, 0:CMPW], ACT.Copy)
                        act.activation(vcmp[:, :], src[:, 64:128], ACT.Copy).then_inc(pa_out, 1)
                    is_gate = MIXER[n][0] == "gate"
                    if is_gate and 2 <= step < NSLOT + 2:
                        copy_turned(l, step - 2)
                    if MIXER[n - 1][0] == "gate":
                        gate_tanh(l, step - 1)
                    if not is_gate:
                        continue
                    if step < NSLOT:
                        exp_head(l, step)
                    if step in PAIR_AT:
                        pair_hi(l, PAIR_AT[step])
                    step += 1
                for k in range(KT):
                    act.wait_ge(y_out, at(l, 3 * KT, 2 * KT + k + 1))
                    act.activation(xTh[:, k, :], z[:, k, :], ACT.Copy, scale=0.5).then_inc(zh_done, 1)
                    ahead(l, MIX0 + U_WO + k)

            def gate_tanh(l, g):
                b, n = divmod(g, KT)
                src = pa_wait(l, f"gate{b}_{n}")[:, 0:S]
                if b == 2:
                    act.wait_ge(*evacuated(l, f"y0_{n}"))
                if b == 3:
                    act.wait_ge(y_out, at(l, 3 * KT, n + 1))
                act.activation(gates[:, KT * (b % 2) + n, :], src, ACT.Tanh, bias=col(HALF + BRANCHES[b] * KT + n),
                               scale=0.5).then_inc(pa_out, 1)

            def cross(l):
                j0 = MIX0 + U_X
                normalise(l, 1)
                evacuate(l, 3, 1)
                for i in range(4):
                    ahead(l, j0 + i)
                act.wait_ge(units_used, unit_done(l, j0 + 3))
                act.activation(xk[:, :, :].rearrange("p i s -> p (i s)"), ps[:, 4, :], ACT.Copy).then_inc(xk_out, 1)
                ahead(l, j0 + 4)
                ahead(l, j0 + 5)
                act.wait_ge(units_used, unit_done(l, j0 + 5))
                act.activation(xq[:, :, :].rearrange("p i s -> p (i s)"), ps[:, 4, :], ACT.Copy).then_inc(xq_out, 1)
                for h in range(NH + 1):
                    if h < NH:
                        act.wait_ge(xmax, at(l, NH, h + 1))
                        if h >= 2:
                            act.wait_ge(xpt_ready, at(l, NH, h - 1))
                        i = h % 2
                        for q in range(TT):
                            last = act.activation(pS[:, i, S * q:S * q + S], ps[:, h, S * q:S * q + S], ACT.Exp,
                                                  bias=stat[:, i, 1, q:q + 1], scale=SCALE, accum_out=stat[:, i, 2, q:q + 1])
                        last.then_inc(xexp, 1)
                    if h >= 1:
                        g = h - 1
                        act.wait_ge(xpt_ready, at(l, NH, g + 1))
                        if g >= 2:
                            act.wait_ge(xo_ready, at(l, NH, g - 1))
                        act.activation(pT[:, g % 2, :], ps[:, 5 + g % 2, :], ACT.Copy).then_inc(xpt_out, 1)
                for k in range(2):
                    act.wait_ge(xo_ready, at(l, NH, 2 * k + 2))
                    act.activation(oTh[:, k, :], ps[:, 7 if k == 0 else 4, 0:S], ACT.Copy).then_inc(xo_hi, 1)
                ahead(l, j0 + 6)
                ahead(l, j0 + 7)
                normalise(l, 2)
                evacuate(l, 4, 2)

            act.wait_ge(credits_set, 1)
            evacuate(0, 0)
            act.wait_ge(trig_done, 1)
            act.activation(cs[:, :], angle, ACT.Sin).then_inc(sin_done, 1)
            act.wait_ge(sin_done, 1)
            act.activation(csq[64:128, :], cs[64:128, :], ACT.Copy).then_inc(sin_done, 1)
            act.wait_ge(xT_ready, 4)
            evacuate(0, 1)
            with act.Fori(0, L) as l:
                for j in range(AHEAD):
                    split_hi(l, j)
                ffn(l, 0)
                act.wait_ge(cols_ready, at(l, 1, 1))
                normalise(l, 0)
                evacuate(l, 2, 0)
                mixer(l)
                cross(l)
                ffn(l, FFN2_0)
                normalise(l, 3)
                evacuate(l, 5, 3)

        @block.vector
        def _(dve):
            def split_lo(l, j, more=0):
                dve.wait_ge(hi_done, units_before(l, j, more) + 1)
                views = zip(split_views(unit_at(j), j % RAW_SLOTS, wh[:, j % WT_SLOTS, :]),
                            split_views(unit_at(j), j % RAW_SLOTS, wl[:, j % WT_SLOTS, :]))
                for (src, hi), (_, lo) in views:
                    last = dve.tensor_tensor(lo, src, hi.bitcast(F32), ALU.subtract)
                last.then_inc(lo_done, 1)

            def ahead(l, j, more=0):
                if j + AHEAD < UNITS:
                    split_lo(l, j + AHEAD, more)

            def split_act(fh, fl, src):
                dve.tensor_copy(fh, src)
                dve.drain()
                return dve.tensor_tensor(fl, src, fh.bitcast(F32), ALU.subtract)

            def split_x(l, idx, th=xTh, tl=xTl):
                for q in range(4):
                    dve.wait_ge(xf_done, at(l, 32, 8 * idx + 2 * q + 2))
                    k = slice(2 * q, 2 * q + 2)
                    split_act(th[:, k, :], tl[:, k, :], z[:, k, :]).then_inc(xT_ready, 1)

            def norm(l, s, j_end):
                for t in range(TT):
                    if t == 0:
                        dve.wait_ge(acc_ready, at(l, 4, s + 1))
                    else:
                        dve.wait_ge(units_used, unit_done(l, j_end))
                    dve.wait_ge(x_done, at(l, 4 * TT, TT * s + t + 1))
                    acc = ps[:, 2 * t:2 * t + 2, :].rearrange("p a b -> p (a b)")
                    dve.scalar_tensor_tensor(xb[:, t, :], xb[:, t, :], ALPHA, acc, ALU.mult, ALU.add)
                    dve.drain()
                    for c in range(2):
                        dve.bn_stats(bst[:, t, c, :], xb[:, t, 512 * c:512 * c + 512])
                    dve.drain()
                    dve.bn_aggr(mv[:, t, :], bst[:, t, :, :].rearrange("p c s -> p (c s)"))
                    dve.drain()
                    dve.tensor_scalar(vare[:, t:t + 1], mv[:, t, 1:2], LN_EPS, None, ALU.add).then_inc(stat_done, 1)
                for t in range(TT):
                    dve.wait_ge(rstd_done, at(l, 4 * TT, TT * s + t + 1))
                    dve.scalar_tensor_tensor(nmr[:, t:t + 1], mv[:, t, 0:1], -1.0, rstd[:, t:t + 1], ALU.mult, ALU.mult)\
                        .then_inc(nm_done, 1)

            def hidden(l, which, f, more=0):
                dve.wait_ge(silu_done, at(l, 2 * FT, FT * which + f + 1) + more * 2)
                p = f % 2
                dve.scalar_tensor_tensor(hf[:, p, :], hs[:, p, :], 0.5, ps[:, 4 + p, 256:512], ALU.mult, ALU.mult)\
                    .then_inc(gu_out, 1)
                dve.drain()
                split_act(oTh[:, p, :], oTl[:, p, :], hf[:, p, :]).then_inc(hT_ready, 1)

            def ffn(l, which, j0):
                for n in range(3):
                    ahead(l, j0 + n)
                hidden(l, which, 0)
                ahead(l, j0 + 3)
                ahead(l, j0 + 4)

                def turn(j, i=0):
                    f = 1 + (j - j0 - 5) // 3
                    ahead(l, j, i)
                    hidden(l, which, f, i)
                    for n in range(1, 4):
                        ahead(l, j + n, i)
                    hidden(l, which, f + 1, i)
                    ahead(l, j + 4, i)
                    ahead(l, j + 5, i)
                with dve.Fori(0, FT // 2 - 2) as i:
                    turn(j0 + 5, i)
                turn(j0 + 5 + 6 * (FT // 2 - 2))
                hidden(l, which, FT - 1)
                ahead(l, j0 + FFN_UNITS - 1)

            def pd_wait(l, name):
                dve.wait_ge(*ready(l, name))
                return pd_tile(name)

            def value_out(l, name, dst, b0):
                src = pd_wait(l, name).rearrange("p (t n) -> p t n", t=TT)
                n = P
                bb = vbias[:, b0:b0 + n].unsqueeze(1).broadcast_to([P, TT, n])
                dve.tensor_tensor(dst, src, bb, ALU.add).then_inc(pd_out, 1)

            def softmax_max(l, n):
                b, h, kind = HEADS[n]
                dve.wait_ge(s_ready, at(l, NSLOT, n + 1))
                i = n % 2
                src = S_BANK
                if kind == "cmp":
                    lg = pc[:, :, :, 0:CMPW].rearrange("p q h c -> p (q h) c")
                    tab = const[:, C_CMPB:C_CMPB + 128].rearrange("p (g c) -> p g c", c=CMPW)
                    dve.scalar_tensor_tensor(lg, src[:, 0:128].rearrange("p (g c) -> p g c", c=CMPW), SCALE, tab,
                                             ALU.mult, ALU.add).then_inc(s_out, 1)
                    dve.drain()
                    dve.tensor_reduce(cstat[:, 0, :], lg, AX.X, ALU.max)
                    dve.drain()
                    dve.tensor_tensor(lg, lg, cstat[:, 0, :].unsqueeze(2).broadcast_to([P, 8, CMPW]), ALU.subtract)\
                        .then_inc(s_max, 1)
                    return
                scale = SCALE_D if kind == "d" else SCALE
                if n >= 2:
                    dve.wait_ge(pt_ready, at(l, NSLOT, n - 1))
                dve.memset(fence[:, :], 0.0)
                dve.tensor_tensor_reduce(pS[:, i, 0:P], src[:, 0:P], bias_table(kind, h, 0), scale, -3.4e38,
                                         ALU.add, ALU.max, stat[:, i, 0, 0:1])
                dve.tensor_tensor_reduce(pS[:, i, P:3 * P], src[:, P:3 * P], bias_table(kind, h, 1), scale, -3.4e38,
                                         ALU.add, ALU.max, stat[:, i, 0, 1:2]).then_inc(s_out, 1)
                dve.drain()
                dve.tensor_scalar(stat[:, i, 1, :], stat[:, i, 0, :], -1.0, None, ALU.mult).then_inc(s_max, 1)

            def softmax_norm(l, n):
                b, h, kind = HEADS[n]
                dve.wait_ge(p_exp, at(l, NSLOT, n + 1))
                i = n % 2
                if kind == "cmp":
                    lg = pc[:, :, :, 0:CMPW].rearrange("p q h c -> p (q h) c")
                    tab = const[:, C_CMPM:C_CMPM + 128].rearrange("p (g c) -> p g c", c=CMPW)
                    dve.tensor_tensor(lg, lg, tab, ALU.mult)
                    dve.drain()
                    dve.tensor_reduce(cstat[:, 1, :], lg, AX.X, ALU.add)
                    dve.drain()
                    dve.tensor_scalar(cstat[:, 1, :], cstat[:, 1, :], 1e-30, None, ALU.max)
                    dve.drain()
                    dve.reciprocal(cstat[:, 2, :], cstat[:, 1, :])
                    dve.drain()
                    g0 = gt[:, :, :].rearrange("p q (h b) -> p q h b", b=3)[:, :, :, 0]
                    dve.tensor_tensor(cstat[:, 2, :].rearrange("p (q h) -> p q h", h=NH),
                                      cstat[:, 2, :].rearrange("p (q h) -> p q h", h=NH), g0, ALU.mult)
                    dve.drain()
                    dve.tensor_tensor(lg, lg, cstat[:, 2, :].unsqueeze(2).broadcast_to([P, 8, CMPW]), ALU.mult)\
                        .then_inc(p_ready, 1)
                    return
                dve.tensor_scalar(stat[:, i, 2, :], stat[:, i, 2, :], 1e-30, None, ALU.max)
                dve.drain()
                dve.reciprocal(stat[:, i, 3, :], stat[:, i, 2, :])
                dve.drain()
                parts = ((0, 0, P), (1, P, 3 * P))
                for q, c0, c1 in parts:
                    if kind in "sw":
                        g = 3 * h + (1 if kind == "s" else 2)
                        last = dve.tensor_scalar(pS[:, i, c0:c1], pS[:, i, c0:c1], stat[:, i, 3, q:q + 1],
                                                 gt[:, q, g:g + 1], ALU.mult, ALU.mult)
                    else:
                        last = dve.tensor_scalar(pS[:, i, c0:c1], pS[:, i, c0:c1], stat[:, i, 3, q:q + 1], None, ALU.mult)
                last.then_inc(p_ready, 1)

            def pair_lo(l, pair):
                dve.wait_ge(o_hi, at(l, PAIRS, pair + 1))
                s_ = pair % 4
                dve.tensor_tensor(oTl[:, s_, :], o_bank(pair), oTh[:, s_, :].bitcast(F32), ALU.subtract).then_inc(o_out, 1)

            def merge(l, b, n):
                src = pd_wait(l, f"y{b}_{n}")
                g = gates[:, KT * (b % 2) + n, :]
                dve.wait_ge(*evacuated(l, f"gate{b}_{n}"))
                dst = z[:, n, :] if b == 0 else g
                dve.scalar_tensor_tensor(dst, g, 1.0, src, ALU.add, ALU.mult).then_inc(pd_out, 1)
                if b:
                    dve.drain()
                    dve.tensor_tensor(z[:, n, :], z[:, n, :], g, ALU.add).then_inc(y_out, 1)

            def mixer(l):
                for n in range(NPROJ):
                    ahead(l, MIX0 + n)
                    if n == 3:
                        dve.wait_ge(*evacuated(l, "dckv"))
                        dve.tensor_tensor(sq, cqf, cqf, ALU.mult).then_inc(sq_done, 1)
                    if n == 4:
                        src = pd_wait(l, "kr")
                        dve.scalar_tensor_tensor(krt, src, col(BIAS["kr"]), cs[:, :], ALU.add, ALU.mult).then_inc(pd_out, 1)
                    if n == 6:
                        dve.wait_ge(*evacuated(l, "kc"))
                        for br in range(2):
                            for lp in range(16):
                                src = x2[:, br, 2 * lp:2 * lp + 16 * (CMP - 1) + 1:16]
                                last = dve.tensor_scalar(blkf[:, br, lp, :], src, col(POS + 16 * br + lp), None, ALU.add)
                        dve.drain()
                        split_act(blkh[:, :, :, 0:CMP].rearrange("p b l c -> p (b l) c"),
                                  blkl[:, :, :, 0:CMP].rearrange("p b l c -> p (b l) c"),
                                  blkf[:, :, :, :].rearrange("p b l c -> p (b l) c")).then_inc(blk_ready, 1)
                    if n == 9:
                        value_out(l, "vs", vB[:, :, :], 256)
                    if n == 10:
                        dve.wait_ge(*evacuated(l, "ssq"))
                        dve.reciprocal(rms, rms)
                        dve.drain()
                        for i in range(3):
                            dve.scalar_tensor_tensor(cqf[:, i, :], cqf[:, i, :], col(QN + i), rms[:, i // 2, :],
                                                     ALU.mult, ALU.mult)
                        dve.drain()
                        split_act(oTh[:, 0:3, :], oTl[:, 0:3, :], cqf).then_inc(cqn_ready, 1)
                        dve.wait_ge(kr_shift, at(l, 1, 1))
                        dve.tensor_tensor(krs[0:32, :], krt[0:32, :], krs[0:32, :], ALU.add).then_inc(kr_added, 1)
                    if n == 11:
                        src = pd_wait(l, "gf")[:, 0:32].rearrange("p (t n) -> p t n", t=TT)
                        dve.tensor_tensor(gl[:, :, 0:12], src[:, :, 0:12],
                                          vbias[:, 384:396].unsqueeze(1).broadcast_to([P, TT, 12]), ALU.add)
                        dve.tensor_tensor(gl[:, :, 12:16], src[:, :, 12:16],
                                          vbias[:, 652:656].unsqueeze(1).broadcast_to([P, TT, 4]), ALU.add)\
                            .then_inc(pd_out, 1)
                        dve.drain()
                        f = gl[:, :, 12:16]
                        dve.tensor_scalar(fx[:, 0, :, :], f, -1.0, None, ALU.mult)
                        dve.tensor_scalar(fx[:, 4, :, :], f, 0.0, None, ALU.min)
                        dve.drain()
                        dve.tensor_tensor(fx[:, 1, :, :], f, fx[:, 0, :, :], ALU.max).then_inc(fx_abs, 1)
                    if n == 14:
                        dve.wait_ge(gth_done, at(l, 1, 1))
                        dve.tensor_scalar(gt[:, :, :], gth[:, :, :], 0.5, 0.5, ALU.mult, ALU.add)
                        dve.wait_ge(fx_ln, at(l, 1, 1))
                        dve.tensor_tensor(fx[:, 0, :, :], fx[:, 4, :, :], fx[:, 3, :, :], ALU.subtract)
                        dve.drain()
                        for i in range(2):
                            last = dve.tensor_scalar(ls8[:, :, 4 * i:4 * i + 4], fx[:, 0, :, :], 1.0 / SCALE, None, ALU.mult)
                        last.then_inc(ls_ready, 1)
                    if n in (U_CV + 1, U_CV + 2):
                        i = n - U_CV - 1
                        value_out(l, f"cv{i}", vC[:, :, P * i:P * i + P], 396 + P * i)
                    if n == U_UQ:
                        for h in range(NH):
                            src = pd_wait(l, f"q{h}")
                            dve.tensor_tensor(qD[:, h, :], src, csq[:, :], ALU.mult).then_inc(pd_out, 1)
                    if n == U_UKV:
                        for t in range(TT):
                            src = pd_wait(l, f"vd{t}")
                            dve.tensor_copy(vD[:, t, :], src).then_inc(pd_out, 1)
                    if n in (U_W1 + 4, U_W1 + 8):
                        br = 0 if n == U_W1 + 4 else 1
                        src = pd_wait(l, f"hid{br}")
                        parts = src[:, 0:8 * CMPW].rearrange("p (c x) -> p x c", c=4)
                        dve.tensor_reduce(hx[:, br, :], parts, AX.X, ALU.add).then_inc(pd_out, 1)
                        dve.drain()
                        dve.tensor_tensor(hu[:, br, :], hx[:, br, :], hx[:, br, :], ALU.mult)
                        dve.drain()
                        dve.tensor_scalar(hu[:, br, :], hu[:, br, :], 0.044715, 1.0, ALU.mult, ALU.add)
                        dve.drain()
                        dve.tensor_tensor(hu[:, br, :], hu[:, br, :], hx[:, br, :], ALU.mult).then_inc(hu_done, 1)
                    if n == U_W1 + 5:
                        src = pd_wait(l, "decay")[0:8, :]
                        for h in range(NH):
                            sel = const[0:8, C_SEL + h:C_SEL + 13 + h]
                            dve.tensor_scalar(lq[:, h, :], src, sel[:, 0:1], sel[:, 4:5], ALU.mult, ALU.add)
                            last = dve.tensor_scalar(rk[:, h, :], src, sel[:, 8:9], sel[:, 12:13], ALU.mult, ALU.add)
                        last.then_inc(pd_out, 1)
                    if n in (U_W1 + 6, U_W1 + 10):
                        br = 0 if n == U_W1 + 6 else 1
                        dve.wait_ge(hg_done, at(l, 2, br + 1))
                        dve.scalar_tensor_tensor(hx[:, br, :], hg[:, br, :], 1.0, hx[:, br, :], ALU.add, ALU.mult)
                        dve.drain()
                        dve.tensor_scalar(hg[:, br, :], hx[:, br, :], 0.5, None, ALU.mult)
                        dve.drain()
                        src = hg[:, br, :].rearrange("p (k c) -> p k c", k=2)
                        if br == 0:
                            split_act(hkh[:, :, :], hkl[:, :, :], src).then_inc(hid_ready, 1)
                        else:
                            for k in range(2):
                                s_ = src[:, k, :].unsqueeze(1).broadcast_to([P, NH, CMPW])
                                last = split_act(hvh[:, k, :, 0:CMPW], hvl[:, k, :, 0:CMPW], s_)
                            last.then_inc(hid_ready, 1)
                    if n in (U_AV + 1, U_AV + 2):
                        i = n - U_AV - 1
                        value_out(l, f"av{i}", vA[:, :, P * i:P * i + P], P * i)
                step = 0
                for n in range(NPROJ, U_WO):
                    ahead(l, MIX0 + n)
                    kind, b, i = MIXER[n]
                    if kind == "branch":
                        for q in range(4):
                            merge(l, b, 4 * i + q)
                        continue
                    if 1 <= step <= NSLOT:
                        softmax_norm(l, step - 1)
                    if step < NSLOT:
                        softmax_max(l, step)
                    if step in PAIR_AT:
                        pair_lo(l, PAIR_AT[step])
                    step += 1
                for k in range(KT):
                    dve.wait_ge(zh_done, at(l, KT, k + 1))
                    dve.scalar_tensor_tensor(xTl[:, k, :], z[:, k, :], 0.5, xTh[:, k, :].bitcast(F32), ALU.mult,
                                             ALU.subtract).then_inc(z_ready, 1)
                    ahead(l, MIX0 + U_WO + k)

            def cross(l):
                j0 = MIX0 + U_X
                norm(l, 1, j0 - 1)
                split_x(l, 3)
                for i in range(4):
                    ahead(l, j0 + i)
                dve.wait_ge(units_used, unit_done(l, j0 + 3))
                dst = xv[:, :, :].rearrange("p t (i n) -> p i t n", i=2)
                dve.tensor_copy(dst, ps[:, 5, :].rearrange("p (i t n) -> p i t n", i=2, t=TT)).then_inc(xv_out, 1)
                ahead(l, j0 + 4)
                ahead(l, j0 + 5)

                def maxima(h):
                    dve.wait_ge(xs_ready, at(l, NH, h + 1))
                    i = h % 2
                    dve.tensor_reduce(stat[:, i, 0, :], ps[:, h, :].rearrange("p (q k) -> p q k", q=TT), AX.X, ALU.max)
                    dve.drain()
                    dve.tensor_scalar(stat[:, i, 1, :], stat[:, i, 0, :], -SCALE, None, ALU.mult).then_inc(xmax, 1)

                maxima(0)
                for h in range(NH):
                    if h + 1 < NH:
                        maxima(h + 1)
                    dve.wait_ge(xexp, at(l, NH, h + 1))
                    i = h % 2
                    dve.reciprocal(stat[:, i, 3, :], stat[:, i, 2, :])
                    dve.drain()
                    for q in range(TT):
                        last = dve.tensor_scalar(pS[:, i, S * q:S * q + S], pS[:, i, S * q:S * q + S],
                                                 stat[:, i, 3, q:q + 1], None, ALU.mult)
                    last.then_inc(xp_ready, 1)
                for k in range(2):
                    dve.wait_ge(xo_hi, at(l, 2, k + 1))
                    dve.tensor_tensor(oTl[:, k, :], ps[:, 7 if k == 0 else 4, 0:S], oTh[:, k, :].bitcast(F32),
                                      ALU.subtract).then_inc(xo_out, 1)
                ahead(l, j0 + 6)
                ahead(l, j0 + 7)
                norm(l, 2, j0 + 7)
                split_x(l, 4)

            dve.memset(eps_rms[:, :], RMS_EPS)
            dve.sem_inc(lo_done, RAW_SLOTS)
            dve.sem_inc(pa_out, 2)
            dve.sem_inc(pd_out, 2)
            dve.sem_inc(gu_out, 2)
            dve.sem_inc(s_out, 1)
            dve.sem_inc(pt_out, 1)
            dve.sem_inc(o_out, 2)
            dve.sem_inc(x_done, TT)
            dve.drain()
            dve.sem_inc(credits_set, 1)
            dve.wait_ge(const_in, 16 * N_CONST_DMAS)
            tf, an, kn, rr = (trig[:, i * S:(i + 1) * S] for i in range(4))
            dve.tensor_copy(tf, posi)
            dve.drain()
            dve.tensor_scalar(an, tf, const[:, C_INV:C_INV + 1], None, ALU.mult)
            dve.drain()
            dve.tensor_scalar(kn, an, 1.0 / TWO_PI, const[:, C_OFF:C_OFF + 1], ALU.mult, ALU.add)
            dve.drain()
            dve.tensor_scalar(kn, kn, ROUND, None, ALU.add)
            dve.drain()
            dve.tensor_scalar(kn, kn, ROUND, None, ALU.subtract)
            dve.drain()
            for c in (PI_1, PI_2, PI_3):
                dve.scalar_tensor_tensor(an, kn, -c, an, ALU.mult, ALU.add)
                dve.drain()
            dve.tensor_scalar(an, an, const[:, C_PHASE:C_PHASE + 1], 3.1415925, ALU.add, ALU.min)
            dve.drain()
            dve.tensor_scalar(angle, an, -3.1415925, None, ALU.max).then_inc(trig_done, 1)
            dve.wait_ge(cols_psum, 1)
            dve.tensor_copy(cols[:, :], ps[:, 5, 0:294])
            split_x(0, 0, memTh, memTl)
            split_x(0, 1)
            with dve.Fori(0, L) as l:
                for dst, n, src in ((0, NB, 0), (LNG, 32, 96), (LNB, 32, 160), (POS, 32, 224), (QN, 2, 288), (KN, 1, 292)):
                    dve.tensor_copy(cur[:, dst:dst + n], cols[:, bass.ds(l * n + src, n)])
                dve.drain()
                dve.tensor_scalar(cur[:, HALF:HALF + 32], cur[:, GB0:GB0 + 32], 0.5, None, ALU.mult).then_inc(cols_ready, 1)
                for j in range(AHEAD):
                    split_lo(l, j)
                ffn(l, 0, 0)
                norm(l, 0, FFN_UNITS - 1)
                split_x(l, 2)
                dve.wait_ge(vb_in, at(l, 64, 64))
                mixer(l)
                cross(l)
                ffn(l, 1, FFN2_0)
                norm(l, 3, UNITS - 1)
                split_x(l, 5)


_INPUTS = ("x", "mem", "positions", "ln_g", "ln_b", "ffn1_w_in", "ffn1_w_out", "ffn2_w_in", "ffn2_w_out", "w_in",
           "b_in", "w_branch", "w_o", "mla_q_norm", "mla_w_uq", "mla_kv_norm", "mla_w_ukv", "nsa_cmp_pos",
           "nsa_cmp_w1", "nsa_cmp_w2", "xa_w_q", "xa_w_kv", "xa_w_o")


def kernel(**inputs):
    import concourse.bacc as bacc
    from concourse.bass_utils import run_bass_kernel_spmd
    nc = bacc.Bacc("TRN2", target_bir_lowering=False, num_devices=1)
    arrays, a = {}, {}
    for name in _INPUTS:
        v = np.ascontiguousarray(inputs[name])
        arrays["in_" + name] = v
        a[name] = nc.dram_tensor("in_" + name, v.shape, mybir.dt.from_np(v.dtype), kind="ExternalInput").ap()
    arrays["in_const"] = constants()
    a["const"] = nc.dram_tensor("in_const", (P, NCONST), F32, kind="ExternalInput").ap()
    out = nc.dram_tensor("out_0", (1, S, D), F32, kind="ExternalOutput").ap()
    build(nc, a, out)
    r = run_bass_kernel_spmd(nc, [arrays], core_ids=[0])
    return r.results[0]["out_0"]
```

```python
from contextlib import ExitStack

import numpy as np
import concourse.bass as bass
from concourse import mybir

F32 = mybir.dt.float32
F32R = mybir.dt.float32r
I32 = mybir.dt.int32
ACT = mybir.ActivationFunctionType
ALU = mybir.AluOpType
AX = mybir.AxisListType

P = 128
D = 1024
S = 256
L = 2
FF = 2816
KT = D // P
TT = S // P
FT = FF // P
HD = 64
NH = 4
CMP = 15
CMPW = 16
WINDOW = 80
SCALE = HD ** -0.5
SCALE_D = 96 ** -0.5
ALPHA = (2 * L) ** 0.25
LN_EPS = 1e-5
RMS_EPS = 1e-6
NEG = -1e30

RAW_SLOTS = 3
WT_SLOTS = 6
AHEAD = WT_SLOTS - 1

A_Q, A_K, A_V, B_Q, B_KC, B_KS, B_VS, B_KW, B_VW, B_G = 0, 256, 512, 768, 1024, 1152, 1216, 1280, 1344, 1408
C_Q, C_K, C_V, C_F, D_CQ, D_CKV, D_KR, G_M = 1420, 1676, 1932, 2188, 2192, 2448, 2576, 2608

BRANCHES = (3, 2, 0, 1)
PROJ = [("col", D_CQ), ("col", D_CQ + 128), ("col", D_CKV), ("kr",), ("col", B_KC), ("pair", B_KS),
        ("col", B_Q), ("col", B_Q + 128), ("pair", B_VS),
        ("col", C_Q), ("col", C_Q + 128), ("col", C_K), ("col", C_K + 128), ("half", C_V, 0), ("half", C_V, 1),
        ("uq", 0), ("uq", 1), ("ukv",)] + [("w1", br, c) for br in range(2) for c in range(4)] + [
        ("col", A_Q), ("col", A_Q + 128), ("col", A_K), ("col", A_K + 128), ("half", A_V, 0), ("half", A_V, 1),
        ("w2", 0), ("w2", 1)]
MIXER = list(PROJ)
AFTER_GATE = {8: (0, 0), 10: (0, 1), 13: (1, 0), 16: (1, 1), 20: (2, 0), 24: (2, 1), 28: (3, 0), 31: (3, 1)}
for _s in range(4 * KT):
    MIXER += [("gate", *divmod(_s, KT))] 
    if _s in AFTER_GATE:
        MIXER += [("branch", *AFTER_GATE[_s])]
MIXER += [("wo", _k) for _k in range(KT)]
MIXER += [("xk", 0), ("xk", 1), ("xv", 0), ("xv", 1), ("xq", 0), ("xq", 1), ("xo", 0), ("xo", 1)]

FFN_UNITS = 3 * FT
MIX0 = FFN_UNITS
FFN2_0 = MIX0 + len(MIXER)
UNITS = FFN2_0 + FFN_UNITS
assert UNITS % WT_SLOTS == 0 and UNITS % RAW_SLOTS == 0 and WT_SLOTS == 6 and RAW_SLOTS == 3

PA = ["dcq0", "dcq1", "dckv", "kc", "ks", "bq0", "bq1", "ssq", "cq0", "cq1", "ck0", "ck1", "kn0", "kn1",
      "aq0", "aq1", "ak0", "ak1", "cmp"] + [f"gate{b}_{n}" for b in range(4) for n in range(KT)]
PD = ["kr", "gf", "vs", "cv", "q0", "q1", "q2", "q3", "vd0", "vd1", "hid0", "decay", "hid1", "turn0",
      "turn1", "av"] + [f"y{b}_{n}" for b in range(4) for n in range(KT)]

MAIN_PA = {0: "dcq0", 1: "dcq1", 2: "dckv", 4: "kc", 5: "ks", 6: "bq0", 7: "bq1", 9: "cq0", 10: "cq1",
           11: "ck0", 12: "ck1", 26: "aq0", 27: "aq1", 28: "ak0", 29: "ak1"}
U_KR, U_VS, U_CV, U_UQ, U_UKV, U_W1, U_AV, U_W2 = (PROJ.index(u) for u in (
    ("kr",), ("pair", B_VS), ("half", C_V, 0), ("uq", 0), ("ukv",), ("w1", 0, 0), ("half", A_V, 0), ("w2", 0)))
NPROJ = len(PROJ)
U_WO = NPROJ + 40
U_X = U_WO + KT
ENDS_UNIT = {name: n for n, name in MAIN_PA.items()}
ENDS_UNIT |= {"kr": U_KR, "vs": U_VS, "cv": U_CV + 1, "q1": U_UQ, "q3": U_UQ + 1, "vd1": U_UKV,
              "hid0": U_W1 + 3, "hid1": U_W1 + 7, "av": U_AV + 1, "cmp": U_W2 + 1}
for _n, _u in enumerate(MIXER):
    if _u[0] == "gate":
        ENDS_UNIT[f"gate{_u[1]}_{_u[2]}"] = _n
    if _u[0] == "branch":
        ENDS_UNIT[f"y{_u[1]}_{4 * _u[2] + 3}"] = _n
PA_MID = [n for n in PA if n not in ENDS_UNIT]
PD_MID = [n for n in PD if n not in ENDS_UNIT]

HEADS = [(0, h, "d") for h in range(NH)] + [(1, h, "c") for h in range(NH)] + [(2, h, "a") for h in range(NH)]
CMP_SLOT = len(HEADS)
HEADS += [(3, 0, "cmp")] + [(3, h, kind) for h in range(NH) for kind in ("s", "w")]
NSLOT = len(HEADS)
PAIR_AT = {3: 0, 5: 1, 7: 2, 9: 3, 11: 4, 13: 5, 18: 6, 22: 7}
PAIR_END = {pair: step - 2 for step, pair in PAIR_AT.items()}
PAIRS = 8

BIAS = {"dcq0": 0, "dcq1": 1, "dckv": 2, "kr": 3, "kc": 4, "ks": 5, "bq0": 6, "bq1": 7, "cq0": 8, "cq1": 9,
        "ck0": 10, "ck1": 11, "aq0": 12, "aq1": 13, "ak0": 14, "ak1": 15}
NB = 48
GB0 = 16
LNG, LNB, POS, QN, KN, HALF = NB, NB + 32, NB + 64, NB + 96, NB + 98, NB + 99
NCOLS = HALF + 32

C_ID, C_CAUSAL, C_ALIBI, C_TRI = 0, 128, 384, 384 + 8 * 256
C_CMPB, C_CMPM = C_TRI + 256, C_TRI + 256 + 128
C_INV, C_OFF, C_PHASE, C_SEL = C_CMPM + 128, C_CMPM + 129, C_CMPM + 130, C_CMPM + 131
NCONST = C_SEL + 16
TWO_PI = 2 * np.pi
PI_1 = float(np.float32(6.28125))
PI_2 = 0.0019350051879882812
PI_3 = float(np.float32(TWO_PI - PI_1 - PI_2))
ROUND = float(1.5 * 2 ** 23)


def constants():
    t = np.arange(P)
    c = np.zeros((P, NCONST), np.float32)
    c[:, C_ID:C_ID + P] = np.eye(P)
    diag = np.where(t[None, :] <= t[:, None], 0.0, NEG)
    c[:, C_CAUSAL + P:C_CAUSAL + 2 * P] = diag
    slopes = 2.0 ** -np.arange(1, 9)
    dist = (t[:, None] - t[None, :]).astype(np.float64)
    for i in range(8):
        at = C_ALIBI + 256 * i
        c[:, at:at + P] = -slopes[i] * (dist + P) / SCALE
        c[:, at + P:at + 2 * P] = np.where(dist >= 0, -slopes[i] * dist / SCALE, NEG)
    tri = (t[:, None] <= np.arange(S)[None, :]).astype(np.float32)
    c[:, C_TRI:C_TRI + S] = tri
    for q in range(TT):
        for h in range(NH):
            at = (q * NH + h) * CMPW
            gone = (q * P + t[:, None]) - (np.arange(CMPW) * 16 + 31)[None, :]
            seen = (gone >= 0) & (np.arange(CMPW) < CMP)[None, :]
            c[:, C_CMPB + at:C_CMPB + at + CMPW] = np.where(seen, -slopes[2 * h + 1] * gone, NEG)
            c[:, C_CMPM + at:C_CMPM + at + CMPW] = seen
    inv = (np.float32(10000.0) ** (-np.arange(0, 32, 2, dtype=np.float32) / np.float32(32))).astype(np.float32)
    both = np.concatenate([inv, inv])
    for base in (0, 64):
        c[base:base + 32, C_INV] = both
        c[base + 32:base + 64, C_INV] = np.concatenate([-inv, inv])
        c[base:base + 32, C_OFF] = 0.25
        c[base:base + 32, C_PHASE] = np.pi / 2
    for h in range(NH):
        c[h, C_SEL + h] = 1.0
        c[NH + h, C_SEL + 4 + h] = 1.0
        c[NH + h, C_SEL + 8 + h] = -1.0
        c[h, C_SEL + 12 + h] = 1.0
    return c


def build(nc, a, out):
    with ExitStack() as ctx:
        def sb(name, shape, dt=F32):
            return ctx.enter_context(nc.sbuf_tensor(name, shape, dt))

        def sem(name):
            return ctx.enter_context(nc.semaphore(name))

        raw = sb("raw", [P, RAW_SLOTS, 1024])
        wh = sb("wh", [P, WT_SLOTS, 1024], F32R)
        wl = sb("wl", [P, WT_SLOTS, 1024], F32R)
        xb = sb("xb", [P, TT, D])
        xTh, xTl = sb("xTh", [P, KT, S], F32R), sb("xTl", [P, KT, S], F32R)
        memTh, memTl = sb("memTh", [P, KT, S], F32R), sb("memTl", [P, KT, S], F32R)
        gb = sb("gb", [P, 2, D])
        gates = sb("gates", [P, 2 * KT, S])
        z = sb("z", [P, KT, S])
        oTh, oTl = sb("oTh", [P, 4, S], F32R), sb("oTl", [P, 4, S], F32R)
        qD, kD, vD = sb("qD", [P, NH, S]), sb("kD", [P, NH, S]), sb("vD", [P, TT, 256])
        qC, kC, vC = sb("qC", [P, 2, S]), sb("kC", [P, 2, S]), sb("vC", [P, TT, 256])
        qA, kA, vA = sb("qA", [P, 2, S]), sb("kA", [P, 2, S]), sb("vA", [P, TT, 256])
        qB, kB, vB = sb("qB", [P, 2, S]), sb("kB", [P, 2, S]), sb("vB", [P, TT, 128])
        x2 = sb("x2", [P, 2, S])
        blkf = sb("blkf", [P, 2, 16, CMP])
        blkh, blkl = sb("blkh", [P, 32 * CMPW + WINDOW - CMPW], F32R), sb("blkl", [P, 32 * CMPW + WINDOW - CMPW], F32R)
        hT = sb("hT", [P, 2, CMPW])
        hkh, hkl = sb("hkh", [P, 2, CMPW], F32R), sb("hkl", [P, 2, CMPW], F32R)
        hvh, hvl = sb("hvh", [P, 2, NH, 32], F32R), sb("hvl", [P, 2, NH, 32], F32R)
        kcmp, vcmp = sb("kcmp", [P, 2 * CMPW]), sb("vcmp", [P, HD])
        pc = sb("pc", [P, TT, NH, 32])
        pcT = sb("pcT", [P, S])
        cstat = sb("cstat", [P, 3, 8])
        pS = sb("pS", [P, 2, 512])
        pT = sb("pT", [P, 2, 512])
        stat = sb("stat", [P, 2, 4, 2])
        gl, gth = sb("gl", [P, TT, 16]), sb("gth", [P, TT, 12])
        gt = sb("gt", [P, TT, 12])
        fx = sb("fx", [P, 5, TT, 4])
        ls8 = sb("ls8", [P, TT, 8])
        vbias = sb("vbias", [P, 640])
        cs, csq = sb("cs", [P, S]), sb("csq", [P, S])
        const = sb("const", [P, NCONST])
        cols = sb("cols", [P, 96 + 128 + 70])
        cur = sb("cur", [P, NCOLS])
        ones = sb("ones", [P, P])
        bst, mv = sb("bst", [P, TT, 2, 6]), sb("mv", [P, TT, 2])
        vare, rstd, nmr = sb("vare", [P, TT]), sb("rstd", [P, TT]), sb("nmr", [P, TT])
        mhalf, eps_rms, fence = sb("mhalf", [P, 1]), sb("eps_rms", [P, 1]), sb("fence", [P, 1])
        ps = ctx.enter_context(nc.psum_tensor("ps", [P, 8, 512], F32))

        cqf, sq, rms = gates[:, 0:3, :], gates[:, 3:6, :], gates[:, 6:8, :]
        krt, krs = gates[:, 8, :], gates[:, 9, :]
        hx, hu = gates[0:CMPW, 10:12, :], gates[0:CMPW, 12:14, :]
        rows = gates[:, 0:3, 0:P]
        stage = gates[:, 8:16, :].rearrange("p a s -> p (a s)").rearrange("p (t d) -> p t d", t=TT)
        trig = pS[:, :, :].rearrange("p i n -> p (i n)")
        posi, angle = gates[:, 4, :].bitcast(I32), gates[:, 5, :]
        hs, hf = z[:, 0:2, :], z[:, 2:4, :]
        lq, rk = z[0:8, 0:4, :], z[0:8, 4:8, :]
        xq, xk, xv = qA, kA, vA

        const_in, cast_in = sem("const_in"), sem("cast_in")
        raw_in = [sem(f"raw_in{i}") for i in range(RAW_SLOTS)]
        pair_in = sem("pair_in")
        hi_done, lo_done = sem("hi_done"), sem("lo_done")
        units_used = sem("units_used")
        pa_ready, pa_out = sem("pa_ready"), sem("pa_out")
        pd_ready, pd_out = sem("pd_ready"), sem("pd_out")
        cols_ready, cols_psum = sem("cols_ready"), sem("cols_psum")
        trig_done, setup_done = sem("trig_done"), sem("setup_done")
        acc_ready, stat_done, rstd_done = sem("acc_ready"), sem("stat_done"), sem("rstd_done")
        nm_done, xn_done = sem("nm_done"), sem("xn_done")
        tp_ready, xf_done, xT_ready = sem("tp_ready"), sem("xf_done"), sem("xT_ready")
        x_mul, x_done = sem("x_mul"), sem("x_done")
        gb_in, vb_in, out_done = sem("gb_in"), sem("vb_in"), sem("out_done")
        silu_done, gu_out, hT_ready = sem("silu_done"), sem("gu_out"), sem("hT_ready")
        sq_done, cqn_ready = sem("sq_done"), sem("cqn_ready")
        kr_shift, kr_added, kr_sum = sem("kr_shift"), sem("kr_added"), sem("kr_sum")
        gth_done, fx_abs, fx_exp, fx_ln, ls_ready = (sem("gth_done"), sem("fx_abs"), sem("fx_exp"), sem("fx_ln"),
                                                     sem("ls_ready"))
        blk_ready, hu_done, hg_done, hid_ready, gelu_done = (sem(n) for n in ("blk_ready", "hu_done", "hg_done",
                                                                             "hid_ready", "gelu_done"))
        s_ready, s_out, s_max = sem("s_ready"), sem("s_out"), sem("s_max")
        p_exp, p_ready = sem("p_exp"), sem("p_ready")
        pt_ready, pt_out, pv_done = sem("pt_ready"), sem("pt_out"), sem("pv_done")
        o_hi, o_out = sem("o_hi"), sem("o_out")
        zh_done, z_ready, y_out = sem("zh_done"), sem("z_ready"), sem("y_out")
        xk_out, xv_out, xq_out = sem("xk_out"), sem("xv_out"), sem("xq_out")
        xs_ready, xmax, xexp, xp_ready = sem("xs_ready"), sem("xmax"), sem("xexp"), sem("xp_ready")
        xpt_ready, xpt_out, xo_ready, xo_hi, xo_out = (sem("xpt_ready"), sem("xpt_out"), sem("xo_ready"),
                                                       sem("xo_hi"), sem("xo_out"))
        credits_set, sin_done = sem("credits_set"), sem("sin_done")

        ident = const[:, C_ID:C_ID + P]

        def bias_table(kind, h, q):
            if kind in "dc":
                at = C_CAUSAL
            else:
                at = C_ALIBI + 256 * (2 * h + (kind != "a"))
            return const[:, at + P:at + 2 * P] if q == 0 else const[:, at:at + 2 * P]

        def col(i):
            return cur[:, i:i + 1]

        def k_rows(w):
            return w.rearrange("(kt p) n -> p kt n", p=P)

        def ffn_source(w_in, w_out, l, what, f):
            if what == "out":
                return w_out[l].rearrange("(f p) n -> f p n", p=P)[f]
            return k_rows(w_in[l]).rearrange("p kt (c f j) -> c f p kt j", c=2, f=FT)[0 if what == "g" else 1][f]

        def mixer_source(unit, l):
            kind, x = unit[0], unit[1] if len(unit) > 1 else 0
            w_in = k_rows(a["w_in"][l])
            if kind == "col" and x == 0:
                tiles = a["w_in"].rearrange("l (kt p) n -> (l kt) p n", p=P)[bass.ds(l * KT, KT)]
                return tiles.rearrange("kt p n -> p kt n")[:, :, 0:P]
            if kind == "col":
                return w_in[:, :, x:x + P]
            if kind == "half":
                return w_in[:, 4 * unit[2]:4 * unit[2] + 4, x:x + 256]
            if kind == "pair":
                return w_in[:, :, x:x + 256].rearrange("p kt (c j) -> p kt c j", c=2)[:, :, :, 0:HD]
            if kind == "uq":
                return k_rows(a["mla_w_uq"][l])[:, :, 192 * x:192 * x + 192]
            if kind == "ukv":
                return a["mla_w_ukv"][l]
            if kind == "w1":
                return a["nsa_cmp_w1"][l][x].rearrange("(c lp p) n -> c p lp n", c=4, p=P)[unit[2]]
            if kind == "w2":
                return k_rows(a["nsa_cmp_w2"][l][x])
            if kind == "gate":
                at = G_M + BRANCHES[x] * D + unit[2] * P
                return w_in[:, :, at:at + P]
            if kind == "branch":
                w = k_rows(a["w_branch"][l][BRANCHES[x]])
                return w[:, :, 512 * unit[2]:512 * unit[2] + 512]
            if kind == "wo":
                return a["w_o"][l].rearrange("(k p) n -> k p n", p=P)[x]
            if kind == "xk":
                return k_rows(a["xa_w_kv"][l])[:, :, P * x:P * x + P]
            if kind == "xv":
                return k_rows(a["xa_w_kv"][l])[:, 4 * x:4 * x + 4, 256:512]
            if kind == "xq":
                return k_rows(a["xa_w_q"][l])[:, :, P * x:P * x + P]
            return a["xa_w_o"][l].rearrange("(k p) n -> k p n", p=P)[x]

        def raw_view(unit, slot):
            r = raw[:, slot, :]
            kind = unit[0]
            if kind in ("col", "gate", "xk", "xq"):
                return r.rearrange("p (kt n) -> p kt n", kt=KT)
            if kind in ("half", "xv"):
                return r.rearrange("p (kt n) -> p kt n", kt=4)
            if kind == "kr":
                return r[:, 0:KT * 48].rearrange("p (kt n) -> p kt n", kt=KT)
            if kind == "pair":
                return r.rearrange("p (kt c j) -> p kt c j", kt=KT, c=2)
            if kind == "uq":
                return r[:, 0:384].rearrange("p (kt n) -> p kt n", kt=2)
            if kind == "ukv":
                return r[:, 0:512]
            if kind == "w1":
                return r.rearrange("p (lp n) -> p lp n", lp=4)
            if kind == "w2":
                return r[:, 0:128].rearrange("p (kt n) -> p kt n", kt=2)
            if kind == "branch":
                return r.rearrange("p (kt n) -> p kt n", kt=2)
            return r

        def split_views(unit, rslot, w):
            r = raw[:, rslot, :]
            kind = unit[0]
            if kind == "kr":
                s_, d_ = raw_view(unit, rslot), w.rearrange("p (kt n) -> p kt n", kt=KT)
                return [(s_[:, :, 0:32], d_[:, :, 0:32]), (s_[:, :, 16:32], d_[:, :, 32:48]),
                        (s_[:, :, 0:16], d_[:, :, 48:64]), (s_[:, :, 32:48], d_[:, :, 64:80]),
                        (s_[:, :, 0:48], d_[:, :, 80:128])]
            if kind == "uq":
                s_ = r[:, 0:384].rearrange("p (kh n) -> p kh n", n=96)
                d_ = w[:, 0:512].rearrange("p (kh n) -> p kh n", n=P)
                return [(s_, d_[:, :, 0:96]), (s_[:, :, 80:96], d_[:, :, 96:112]), (s_[:, :, 64:80], d_[:, :, 112:128])]
            if kind == "ukv":
                s_ = r[:, 0:512].rearrange("p (h c n) -> p c h n", h=NH, c=2)
                return [(s_, w[:, 0:512].rearrange("p (c h n) -> p c h n", h=NH, c=2))]
            if kind == "w2":
                s_ = raw_view(unit, rslot)
                d_ = w[:, 0:256].rearrange("p (kt n) -> p kt n", kt=2)
                return [(s_, d_[:, :, 0:HD]), (s_, d_[:, :, HD:P])]
            return [(r, w)]

        PLAIN = ("ffn",)

        def unit_at(j):
            return MIXER[j - MIX0] if MIX0 <= j < FFN2_0 else PLAIN

        def units_before(l, j, more=0):
            return l * UNITS + more * 6 + j

        def raw_fills(l, j, more=0):
            return l * (UNITS // RAW_SLOTS) + more * 2 + j // RAW_SLOTS + 1

        def at(l, per_layer, n):
            return l * per_layer + n

        def unit_done(l, j, more=0):
            return units_before(l, j, more) + 1 + WT_SLOTS

        def signal(name):
            return units_used if name in ENDS_UNIT else pa_ready if name in PA else pd_ready

        def ready(l, name):
            if name in ENDS_UNIT:
                return units_used, unit_done(l, MIX0 + ENDS_UNIT[name])
            own = PA_MID if name in PA else PD_MID
            return (pa_ready if name in PA else pd_ready), at(l, len(own), own.index(name) + 1)

        def free(l, name):
            own = PA if name in PA else PD
            return (pa_out if name in PA else pd_out), at(l, len(own), own.index(name) + 1)

        def evacuated(l, name):
            own = PA if name in PA else PD
            return (pa_out if name in PA else pd_out), at(l, len(own), own.index(name) + 3)

        block = ctx.enter_context(nc.Block())

        @block.sync
        def _(sp):
            sp.dma_start(const[:, :], a["const"]).then_inc(const_in, 16)
            sp.dma_start(xb[:, :, :], a["x"][0].rearrange("(t p) d -> p t d", p=P)).then_inc(const_in, 16)
            sp.dma_start(stage, a["mem"][0].rearrange("(t p) d -> p t d", p=P)).then_inc(const_in, 16)
            pos_row = a["positions"]
            sp.dma_start(posi, pos_row.broadcast_to([P, S])).then_inc(const_in, 16)
            for l in range(L):
                b = a["b_in"][l]

                def bias_rows(r0, at_, n):
                    sp.dma_start(rows[l * NB + r0:l * NB + r0 + n, 0, :],
                                 b[at_:at_ + n * P].rearrange("(r c) -> r c", c=P)).then_inc(const_in, 16)

                def bias_part(r0, c0, at_, n):
                    sp.dma_start(rows[l * NB + r0:l * NB + r0 + 1, 0, c0:c0 + n],
                                 b[at_:at_ + n].unsqueeze(0)).then_inc(const_in, 16)
                bias_rows(BIAS["dcq0"], D_CQ, 3)
                for c0, at_, n in ((0, D_KR, 32), (32, D_KR + 16, 16), (48, D_KR, 16), (64, B_G, 12), (76, C_F, 4),
                                   (80, D_KR, 32), (112, D_KR, 16)):
                    bias_part(BIAS["kr"], c0, at_, n)
                bias_rows(BIAS["kc"], B_KC, 1)
                bias_part(BIAS["ks"], 0, B_KS, HD)
                bias_part(BIAS["ks"], HD, B_KW, HD)
                bias_rows(BIAS["bq0"], B_Q, 2)
                bias_rows(BIAS["cq0"], C_Q, 4)
                bias_rows(BIAS["aq0"], A_Q, 4)
                bias_rows(GB0, G_M, 32)
            sp.dma_start(rows[0:64, 1, :], a["ln_g"].rearrange("l s (k c) -> (l s k) c", c=P)).then_inc(const_in, 16)
            sp.dma_start(rows[64:128, 1, :], a["ln_b"].rearrange("l s (k c) -> (l s k) c", c=P)).then_inc(const_in, 16)
            sp.dma_start(rows[0:64, 2, :], a["nsa_cmp_pos"].rearrange("l b (r two) c -> (l b r) (two c)", two=2)).then_inc(const_in, 16)
            sp.dma_start(rows[64:68, 2, :], a["mla_q_norm"].rearrange("l (k c) -> (l k) c", c=P)).then_inc(const_in, 16)
            sp.dma_start(rows[68:70, 2, :], a["mla_kv_norm"]).then_inc(const_in, 16)

            def load(src, dst, l, j, more=0):
                sp.wait_ge(lo_done, units_before(l, j, more) + 1)
                sp.dma_start(dst, src).then_inc(raw_in[j % RAW_SLOTS], 16)

            def load_ffn(l, j, w_in, w_out, what, f, more=0):
                dst = raw[:, j % RAW_SLOTS, :]
                if what != "out":
                    dst = dst.rearrange("p (kt n) -> p kt n", kt=KT)
                load(ffn_source(w_in, w_out, l, what, f), dst, l, j, more)

            def ffn(l, j0, w_in, w_out):
                for n, (what, f) in enumerate((("g", 0), ("u", 0), ("g", 1), ("u", 1), ("out", 0))):
                    load_ffn(l, j0 + n, w_in, w_out, what, f)
                with sp.Fori(0, FT // 2 - 1) as i:
                    for n, (what, f) in enumerate((("g", 2), ("u", 2), ("out", 1), ("g", 3), ("u", 3), ("out", 2))):
                        load_ffn(l, j0 + 5 + n, w_in, w_out, what, i * 2 + f, i)
                load_ffn(l, j0 + FFN_UNITS - 1, w_in, w_out, "out", FT - 1)

            with sp.Fori(0, L) as l:
                ffn(l, 0, a["ffn1_w_in"], a["ffn1_w_out"])
                for n, unit in enumerate(MIXER):
                    j = MIX0 + n
                    dst = raw_view(unit, j % RAW_SLOTS)
                    if unit[0] == "kr":
                        w_in = k_rows(a["w_in"][l])
                        sp.wait_ge(lo_done, units_before(l, j) + 1)
                        sp.dma_start(dst[:, :, 0:32], w_in[:, :, D_KR:D_KR + 32]).then_inc(pair_in, 16)
                        sp.dma_start(dst[:, :, 32:44], w_in[:, :, B_G:B_G + 12]).then_inc(pair_in, 16)
                        load(w_in[:, :, C_F:C_F + 4], dst[:, :, 44:48], l, j)
                        continue
                    src = mixer_source(unit, l)
                    if unit[0] == "pair":
                        sp.wait_ge(lo_done, units_before(l, j) + 1)
                        sp.dma_start(dst[:, :, 0, :], src[:, :, 0, :]).then_inc(pair_in, 16)
                        src, dst = src[:, :, 1, :], dst[:, :, 1, :]
                    load(src, dst, l, j)
                ffn(l, FFN2_0, a["ffn2_w_in"], a["ffn2_w_out"])

        N_CONST_DMAS = 4 + L * 15 + 5

        @block.gpsimd
        def _(pool):
            pool.memset(mhalf[:, :], -0.5)
            pool.memset(ones[:, :], 1.0)
            pool.memset(csq[0:64, :], 1.0)
            pool.memset(kcmp[:, :], 0.0)
            pool.memset(blkh[:, :].bitcast(F32), 0.0)
            pool.memset(blkl[:, :].bitcast(F32), 0.0)
            pool.memset(hvh[:, :, :, :].bitcast(F32), 0.0)
            pool.memset(hvl[:, :, :, :].bitcast(F32), 0.0)
            pool.memset(pc[:, :, :, :], 0.0).then_inc(setup_done, 1)
            pool.wait_ge(setup_done, 1)

            def norm(l, s):
                pool.wait_ge(x_done, at(l, 4 * TT, TT * s + TT))
                pool.dma_start(gb[:, 0, :], a["ln_g"][l][s:s + 1, :].broadcast_to([P, D])).then_inc(gb_in, 16)
                pool.dma_start(gb[:, 1, :], a["ln_b"][l][s:s + 1, :].broadcast_to([P, D])).then_inc(gb_in, 16)
                for t in range(TT):
                    pool.wait_ge(stat_done, at(l, 4 * TT, TT * s + t + 1))
                    pool.tensor_tensor(rstd[:, t:t + 1], vare[:, t:t + 1], mhalf[:, :], ALU.pow).then_inc(rstd_done, 1)
                pool.wait_ge(tp_ready, at(l, 16, 8 + 4 * s + 4))
                pool.wait_ge(gb_in, at(l, 4 * 32, 32 * s + 32))
                for t in range(TT):
                    pool.tensor_tensor(xb[:, t, :], xb[:, t, :], gb[:, 0, :], ALU.mult).then_inc(x_mul, 1)
                    pool.wait_ge(x_mul, at(l, 4 * TT, TT * s + t + 1))
                    pool.tensor_tensor(xb[:, t, :], xb[:, t, :], gb[:, 1, :], ALU.add).then_inc(x_done, 1)

            with pool.Fori(0, L) as l:
                bl = a["b_in"][l].unsqueeze(0)
                for to, frm, n in ((0, A_V, 256), (256, B_VS, HD), (320, B_VW, HD), (384, C_V, 256)):
                    pool.dma_start(vbias[:, to:to + n], bl[:, frm:frm + n].broadcast_to([P, n])).then_inc(vb_in, 16)
                for s in range(4):
                    norm(l, s)
            for t in range(TT):
                pool.wait_ge(x_done, L * 4 * TT + t + 1)
                pool.dma_start(out[0].rearrange("(t p) d -> t p d", p=P)[t], xb[:, t, :]).then_inc(out_done, 16)
            pool.wait_ge(out_done, TT * 16)

        def tp_bank(q):
            return ps[:, 6 + q % 2, :].rearrange("p (k t n) -> p k t n", k=2, t=TT)

        def pa_tile(name):
            return ps[:, PA.index(name) % 2, :]

        def pd_tile(name):
            return ps[:, 2 + PD.index(name) % 2, :]

        S_BANK = ps[:, 4, :]

        PT_BANK = ps[:, 5, :]

        def o_bank(pair):
            return ps[:, 6 + pair % 2, 0:S]

        def value_tile(kind, h, t):
            if kind == "s":
                return vB[:, t, 0:HD]
            if kind == "w":
                return vB[:, t, HD:2 * HD]
            v = {"d": vD, "c": vC, "a": vA}[kind]
            return v[:, t, HD * h:HD * h + HD]

        @block.tensor
        def _(pe):
            def mm3(o, lh, ll, rh, rl, first, last):
                pe.matmul(o, lh, rh, start=first, stop=False)
                pe.matmul(o, lh, rl, start=False, stop=False)
                return pe.matmul(o, ll, rh, start=False, stop=last)

            def transpose_in(l, idx, src, l_per=16):
                for q in range(4):
                    if q >= 2:
                        pe.wait_ge(xf_done, at(l, 32, 8 * idx + 2 * (q - 2) + 2))
                    for k in range(2):
                        for t in range(TT):
                            last = pe.transpose(tp_bank(q)[:, k, t, :], src[:, t, P * (2 * q + k):P * (2 * q + k) + P], ident)
                    last.then_inc(tp_ready, 1)

            def take(l, j, more=0):
                pe.wait_ge(lo_done, units_before(l, j, more) + RAW_SLOTS + 1)
                s_ = j % WT_SLOTS
                return wh[:, s_, :], wl[:, s_, :]

            pe.wait_ge(const_in, 16 * N_CONST_DMAS)
            pe.wait_ge(setup_done, 1)
            for i, (n, at_) in enumerate(((96, 0), (128, 96), (70, 224))):
                last = pe.transpose(ps[:, 5, at_ % 512:at_ % 512 + n], rows[0:n, i, :], ident[0:n, 0:n])
            last.then_inc(cols_psum, 1)
            transpose_in(0, 0, stage)
            pe.wait_ge(xf_done, 8)
            transpose_in(0, 1, xb)

            def feature_tile(o, h_, l_, l, ln=None):
                hv, lv = (w.rearrange("p (kt n) -> p kt n", kt=KT) for w in (h_, l_))
                for k in range(KT):
                    if ln is not None and k % 2 == 0:
                        pe.wait_ge(xT_ready, at(l, 16, 4 * ln + k // 2 + 1))
                    last = mm3(o, hv[:, k, :], lv[:, k, :], xTh[:, k, :], xTl[:, k, :], k == 0, k == KT - 1)
                return last

            def half_units(l, j, o, xh=xTh, xl=xTl):
                parts = [[w.rearrange("p (kt n) -> p kt n", kt=4) for w in take(l, j + i)] for i in range(2)]
                for t in range(TT):
                    for k in range(KT):
                        hv, lv = parts[k // 4]
                        last = mm3(o[:, S * t:S * t + S], xh[:, k, P * t:P * t + P], xl[:, k, P * t:P * t + P],
                                   hv[:, k % 4, :], lv[:, k % 4, :], k == 0, k == KT - 1)
                        if t == TT - 1 and k == 3:
                            last.then_inc(units_used, 1)
                return last

            def token_tile(o, h_, l_, n, xh=xTh, xl=xTl):
                hv, lv = (w[:, 0:KT * n].rearrange("p (kt n) -> p kt n", kt=KT) for w in (h_, l_))
                for t in range(TT):
                    for k in range(KT):
                        last = mm3(o[:, t, :], xh[:, k, P * t:P * t + P], xl[:, k, P * t:P * t + P],
                                   hv[:, k, :], lv[:, k, :], k == 0, k == KT - 1)
                return last

            def ffn(l, which, j0, ln):
                def hidden(f, j, more=0, ln_=None):
                    h_, l_ = take(l, j, more)
                    pe.wait_ge(gu_out, at(l, 2 * FT, FT * which + f + 1) + more * 2)
                    feature_tile(ps[:, 4 + f % 2, 0:S], h_, l_, l, ln_).then_inc(units_used, 1)
                    h_, l_ = take(l, j + 1, more)
                    feature_tile(ps[:, 4 + f % 2, S:2 * S], h_, l_, l).then_inc(units_used, 1)

                def down(f, j, more=0):
                    h_, l_ = take(l, j, more)
                    pe.wait_ge(hT_ready, at(l, 2 * FT, FT * which + f + 1) + more * 2)
                    for t in range(TT):
                        th, tl = oTh[:, f % 2, P * t:P * t + P], oTl[:, f % 2, P * t:P * t + P]
                        for c in range(2):
                            w = slice(512 * c, 512 * c + 512)
                            last = mm3(ps[:, 2 * t + c, :], th, tl, h_[:, w], l_[:, w], f == 0, f == FT - 1)
                        if f == FT - 1 and t == 0:
                            last.then_inc(acc_ready, 1)
                    last.then_inc(units_used, 1)

                hidden(0, j0, ln_=ln)
                hidden(1, j0 + 2)
                down(0, j0 + 4)
                with pe.Fori(0, FT // 2 - 1) as i:
                    hidden(2, j0 + 5, i)
                    down(1, j0 + 7, i)
                    hidden(3, j0 + 8, i)
                    down(2, j0 + 10, i)
                down(FT - 1, j0 + FFN_UNITS - 1)

            def scores(l, n):
                b, h, kind = HEADS[n]
                pe.wait_ge(s_out, at(l, NSLOT, n + 1))
                o = S_BANK
                if kind == "cmp":
                    for q in range(TT):
                        for hh in (0, 2):
                            i = (q * NH + hh) * CMPW
                            last = pe.matmul(o[:, i:i + 2 * CMPW], qB[:, hh // 2, P * q:P * q + P], kcmp[:, :],
                                             start=True, stop=True)
                    last.then_inc(s_ready, 1)
                    return
                for q in range(TT):
                    ob = o[:, 0:P] if q == 0 else o[:, P:3 * P]
                    nk = P * (q + 1)
                    if kind == "d":
                        last = pe.matmul(ob, qD[:, h, P * q:P * q + P], kD[:, h, 0:nk], start=True, stop=True)
                        continue
                    r = slice(64 * (h % 2), 64 * (h % 2) + 64)
                    qq = {"c": qC, "a": qA}.get(kind, qB)[r, h // 2, P * q:P * q + P]
                    if kind in "sw":
                        kk = kB[r, 0 if kind == "s" else 1, 0:nk]
                    else:
                        kk = (kC if kind == "c" else kA)[r, h // 2, 0:nk]
                    last = pe.matmul(ob, qq, kk, start=True, stop=(kind != "c"))
                    if kind == "c":
                        last = pe.matmul(ob, lq[:, h, P * q:P * q + P], rk[:, h, 0:nk], start=False, stop=True)
                last.then_inc(s_ready, 1)

            def turn(l, n):
                pe.wait_ge(p_ready, at(l, NSLOT, n + 1))
                pe.wait_ge(pt_out, at(l, NSLOT, n + 1))
                for i in range(2 if HEADS[n][2] == "cmp" else 3):
                    src = (pc[:, i, :, :].rearrange("p h c -> p (h c)") if HEADS[n][2] == "cmp"
                           else pS[:, n % 2, P * i:P * i + P])
                    last = pe.transpose(PT_BANK[:, P * i:P * i + P], src, ident)
                last.then_inc(pt_ready, 1)

            def cmp_values(h):
                r = slice(32 * h, 32 * h + CMPW)
                return pe.matmul(o_bank(6 + h // 2)[64 * (h % 2):64 * (h % 2) + 64, :], vcmp[r, :], pcT[r, :],
                                 start=True, stop=False)

            def values(l, n):
                b, h, kind = HEADS[n]
                pair = 2 * b + h // 2
                pe.wait_ge(pt_out, at(l, NSLOT, n + 2))
                if kind == "cmp":
                    pe.wait_ge(o_out, at(l, PAIRS, 6 + 1))
                    cmp_values(0)
                    cmp_values(1).then_inc(pv_done, 1)
                    return
                if kind == "s" and h == 2:
                    pe.wait_ge(o_out, at(l, PAIRS, 7 + 1))
                    cmp_values(2)
                    cmp_values(3)
                if kind in "dca" and h % 2 == 0:
                    pe.wait_ge(o_out, at(l, PAIRS, pair + 1))
                o = o_bank(pair)[64 * (h % 2):64 * (h % 2) + 64, :]
                pe.matmul(o, value_tile(kind, h, 0), pT[:, n % 2, 0:S], start=kind in "dca", stop=False)
                last = pe.matmul(o[:, P:S], value_tile(kind, h, 1), pT[:, n % 2, S:S + P], start=False,
                                 stop=kind != "s")
                last.then_inc(pv_done, 1)

            def project(l):
                for n in range(NPROJ):
                    if n in (U_CV, U_AV):
                        name = "cv" if n == U_CV else "av"
                        pe.wait_ge(*free(l, name))
                        half_units(l, MIX0 + n, pd_tile(name)).then_inc(signal(name), 1)
                        continue
                    if n in (U_CV + 1, U_AV + 1):
                        continue
                    h_, l_ = take(l, MIX0 + n)
                    if n in MAIN_PA:
                        name = MAIN_PA[n]
                        pe.wait_ge(*free(l, name))
                        feature_tile(pa_tile(name)[:, 0:S], h_, l_, l, 2 if n == 0 else None).then_inc(signal(name), 1)
                    elif n == U_KR:
                        pe.wait_ge(*free(l, "kr"))
                        feature_tile(pd_tile("kr")[:, 0:S], h_, l_, l).then_inc(signal("kr"), 1)
                    elif n == U_VS:
                        pe.wait_ge(*free(l, "vs"))
                        o = pd_tile("vs")[:, 0:S].rearrange("p (t n) -> p t n", t=TT)
                        token_tile(o, h_, l_, P).then_inc(signal("vs"), 1)
                    elif n in (U_UQ, U_UQ + 1):
                        if n == U_UQ:
                            pe.wait_ge(cqn_ready, at(l, 1, 1))
                        for h in range(2):
                            name = f"q{2 * (n - U_UQ) + h}"
                            pe.wait_ge(*free(l, name))
                            for k in range(2):
                                c0 = 256 * k + P * h
                                last = mm3(pd_tile(name)[:, 0:S], h_[:, c0:c0 + P], l_[:, c0:c0 + P],
                                           oTh[:, k, :], oTl[:, k, :], k == 0, k == 1)
                            last.then_inc(signal(name), 1)
                    elif n == U_UKV:
                        for i in range(2):
                            pe.wait_ge(*free(l, f"kn{i}"))
                            mm3(pa_tile(f"kn{i}")[:, 0:S], h_[:, P * i:P * i + P], l_[:, P * i:P * i + P],
                                oTh[:, 2, :], oTl[:, 2, :], True, True).then_inc(signal(f"kn{i}"), 1)
                        for t in range(TT):
                            pe.wait_ge(*free(l, f"vd{t}"))
                            mm3(pd_tile(f"vd{t}")[:, 0:S], oTh[:, 2, P * t:P * t + P], oTl[:, 2, P * t:P * t + P],
                                h_[:, 256:512], l_[:, 256:512], True, True).then_inc(signal(f"vd{t}"), 1)
                    elif U_W1 <= n < U_W1 + 8:
                        br, c = divmod(n - U_W1, 4)
                        name = f"hid{br}"
                        if c == 0:
                            pe.wait_ge(*free(l, name))
                        if n == U_W1:
                            pe.wait_ge(blk_ready, at(l, 1, 1))
                        wvh, wvl = (w.rearrange("p (lp n) -> p lp n", lp=4) for w in (h_, l_))
                        for lp in range(4):
                            b0 = (16 * br + 4 * c + lp) * CMPW
                            last = mm3(pd_tile(name)[0:WINDOW, 0:S], blkh[:, b0:b0 + WINDOW], blkl[:, b0:b0 + WINDOW],
                                       wvh[:, lp, :], wvl[:, lp, :], c == 0 and lp == 0, c == 3 and lp == 3)
                        last.then_inc(units_used, 1)
                    elif n == U_W2:
                        pe.wait_ge(hid_ready, at(l, 2, 1))
                        pe.wait_ge(*free(l, "cmp"))
                        wvh, wvl = (w[:, 0:256].rearrange("p (kt n) -> p kt n", kt=2) for w in (h_, l_))
                        for k in range(2):
                            last = mm3(pa_tile("cmp")[:, 0:CMPW], wvh[:, k, :], wvl[:, k, :], hkh[:, k, :], hkl[:, k, :],
                                       k == 0, k == 1)
                        last.then_inc(units_used, 1)
                    elif n == U_W2 + 1:
                        pe.wait_ge(hid_ready, at(l, 2, 2))
                        wvh, wvl = (w[:, 0:256].rearrange("p (kt n) -> p kt n", kt=2) for w in (h_, l_))
                        for k in range(2):
                            last = mm3(pa_tile("cmp")[:, 64:128], hvh[:, k, :, :].rearrange("p h c -> p (h c)"),
                                       hvl[:, k, :, :].rearrange("p h c -> p (h c)"),
                                       wvh[:, k, 0:HD], wvl[:, k, 0:HD], k == 0, k == 1)
                        last.then_inc(signal("cmp"), 1)
                    if n == 5:
                        pe.wait_ge(*evacuated(l, "kr"))
                        pe.wait_ge(*free(l, "gf"))
                        for t in range(TT):
                            last = pe.matmul(pd_tile("gf")[:, 16 * t:16 * t + 16], krt[64:80, P * t:P * t + P],
                                             ident[64:80, 64:80], start=True, stop=True)
                        last.then_inc(signal("gf"), 1)
                    if n in (U_W1 + 7, U_W1 + 11):
                        br = (n - U_W1 - 7) // 4
                        pe.wait_ge(gelu_done, at(l, 2, br + 1))
                        pe.wait_ge(*free(l, f"turn{br}"))
                        for k in range(2):
                            last = pe.matmul(pd_tile(f"turn{br}")[:, CMPW * k:CMPW * k + CMPW],
                                             hx[:, br, P * k:P * k + P], ident[0:CMPW, 0:CMPW], start=True, stop=True)
                        last.then_inc(signal(f"turn{br}"), 1)
                    if n == 7:
                        pe.wait_ge(sq_done, at(l, 1, 1))
                        pe.wait_ge(*free(l, "ssq"))
                        o = pa_tile("ssq")
                        for k in range(2):
                            pe.matmul(o[:, 0:S], ones[:, :], sq[:, k, :], start=(k == 0), stop=(k == 1))
                        pe.matmul(o[:, S:2 * S], ones[:, :], sq[:, 2, :], start=True, stop=True)\
                            .then_inc(signal("ssq"), 1)
                    if n == U_W1 + 3:
                        pe.wait_ge(ls_ready, at(l, 1, 1))
                        pe.wait_ge(*free(l, "decay"))
                        o = pd_tile("decay")[0:8, 0:S]
                        tri = const[:, C_TRI:C_TRI + S]
                        pe.matmul(o, ls8[:, 0, :], tri, start=True, stop=False)
                        pe.matmul(o[:, P:S], ls8[:, 1, :], tri[:, 0:P], start=False, stop=True)\
                            .then_inc(signal("decay"), 1)

            def attend(l):
                pe.wait_ge(kr_sum, at(l, 2, 2))
                step = 0
                for n in range(NPROJ, U_WO):
                    kind, b, i = MIXER[n]
                    h_, l_ = take(l, MIX0 + n)
                    if kind == "gate":
                        if step == 8:
                            pe.wait_ge(*evacuated(l, "cmp"))
                            pe.wait_ge(*evacuated(l, "av"))
                        if step < NSLOT:
                            scores(l, step)
                        name = f"gate{b}_{i}"
                        pe.wait_ge(*free(l, name))
                        hv, lv = (w.rearrange("p (kt n) -> p kt n", kt=KT) for w in (h_, l_))
                        for k in range(KT):
                            if k == KT // 2 and 1 <= step <= NSLOT:
                                turn(l, step - 1)
                            last = mm3(pa_tile(name)[:, 0:S], hv[:, k, :], lv[:, k, :], xTh[:, k, :], xTl[:, k, :],
                                       k == 0, k == KT - 1)
                        last.then_inc(signal(name), 1)
                        if 1 <= step <= NSLOT:
                            values(l, step - 1)
                        step += 1
                        continue
                    if i == 0:
                        pe.wait_ge(o_out, at(l, PAIRS, 2 * b + 2 + 2))
                    wvh, wvl = (w.rearrange("p (kt n) -> p kt n", kt=2) for w in (h_, l_))
                    for q in range(4):
                        name = f"y{b}_{4 * i + q}"
                        pe.wait_ge(*free(l, name))
                        for k in range(2):
                            s_ = 2 * (b % 2) + k
                            last = mm3(pd_tile(name)[:, 0:S], wvh[:, k, P * q:P * q + P], wvl[:, k, P * q:P * q + P],
                                       oTh[:, s_, :], oTl[:, s_, :], k == 0, k == 1)
                        last.then_inc(signal(name), 1)

            def merged_out(l):
                for k in range(KT):
                    h_, l_ = take(l, MIX0 + U_WO + k)
                    pe.wait_ge(z_ready, at(l, KT, k + 1))
                    for t in range(TT):
                        for c in range(2):
                            w = slice(512 * c, 512 * c + 512)
                            last = mm3(ps[:, 2 * t + c, :], xTh[:, k, P * t:P * t + P], xTl[:, k, P * t:P * t + P],
                                       h_[:, w], l_[:, w], k == 0, k == KT - 1)
                        if k == KT - 1 and t == 0:
                            last.then_inc(acc_ready, 1)
                    last.then_inc(units_used, 1)

            def cross(l):
                j0 = MIX0 + U_X
                for i in range(2):
                    h_, l_ = take(l, j0 + i)
                    hv, lv = (w.rearrange("p (kt n) -> p kt n", kt=KT) for w in (h_, l_))
                    for k in range(KT):
                        last = mm3(ps[:, 4, S * i:S * i + S], hv[:, k, :], lv[:, k, :], memTh[:, k, :], memTl[:, k, :],
                                   k == 0, k == KT - 1)
                    last.then_inc(units_used, 1)
                half_units(l, j0 + 2, ps[:, 5, :], memTh, memTl).then_inc(units_used, 1)
                pe.wait_ge(xn_done, at(l, 4 * TT, 2 * TT))
                transpose_in(l, 3, xb)
                for i in range(2):
                    h_, l_ = take(l, j0 + 4 + i)
                    if i == 0:
                        pe.wait_ge(xk_out, at(l, 1, 1))
                    feature_tile(ps[:, 4, S * i:S * i + S], h_, l_, l, 3 if i == 0 else None).then_inc(units_used, 1)
                pe.wait_ge(xq_out, at(l, 1, 1))
                pe.wait_ge(xv_out, at(l, 1, 1))
                for h in range(NH):
                    r = slice(64 * (h % 2), 64 * (h % 2) + 64)
                    for q in range(TT):
                        last = pe.matmul(ps[:, h, S * q:S * q + S], xq[r, h // 2, P * q:P * q + P], xk[r, h // 2, :],
                                         start=True, stop=True)
                    last.then_inc(xs_ready, 1)
                for h in range(NH + 1):
                    if h < NH:
                        pe.wait_ge(xp_ready, at(l, NH, h + 1))
                        if h >= 2:
                            pe.wait_ge(xpt_out, at(l, NH, h - 1))
                        bank = ps[:, 5 + h % 2, :]
                        for k in range(TT):
                            for q in range(TT):
                                last = pe.transpose(bank[:, S * k + P * q:S * k + P * q + P],
                                                    pS[:, h % 2, S * q + P * k:S * q + P * k + P], ident)
                        last.then_inc(xpt_ready, 1)
                    if h >= 1:
                        g = h - 1
                        pe.wait_ge(xpt_out, at(l, NH, g + 1))
                        o = ps[64 * (g % 2):64 * (g % 2) + 64, 7 if g < 2 else 4, 0:S]
                        for k in range(TT):
                            last = pe.matmul(o, xv[:, k, HD * g:HD * g + HD], pT[:, g % 2, S * k:S * k + S],
                                             start=(k == 0), stop=(k == TT - 1))
                        last.then_inc(xo_ready, 1)
                for k in range(2):
                    h_, l_ = take(l, j0 + 6 + k)
                    pe.wait_ge(xo_out, at(l, 2, k + 1))
                    for t in range(TT):
                        for c in range(2):
                            w = slice(512 * c, 512 * c + 512)
                            last = mm3(ps[:, 2 * t + c, :], oTh[:, k, P * t:P * t + P], oTl[:, k, P * t:P * t + P],
                                       h_[:, w], l_[:, w], k == 0, k == 1)
                        if k == 1 and t == 0:
                            last.then_inc(acc_ready, 1)
                    last.then_inc(units_used, 1)
                pe.wait_ge(xn_done, at(l, 4 * TT, 3 * TT))
                transpose_in(l, 4, xb)

            pe.sem_inc(units_used, WT_SLOTS)
            with pe.Fori(0, L) as l:
                ffn(l, 0, 0, 1)
                pe.wait_ge(xn_done, at(l, 4 * TT, TT))
                transpose_in(l, 2, xb)
                project(l)
                attend(l)
                merged_out(l)
                cross(l)
                ffn(l, 1, FFN2_0, 4)
                pe.wait_ge(xn_done, at(l, 4 * TT, 4 * TT))
                transpose_in(l, 5, xb)

        @block.scalar
        def _(act):
            def split_hi(l, j, more=0):
                act.wait_ge(raw_in[j % RAW_SLOTS], raw_fills(l, j, more) * 16)
                act.wait_ge(units_used, units_before(l, j, more) + 1)
                if unit_at(j)[0] == "pair":
                    act.wait_ge(pair_in, at(l, 64, 48 if unit_at(j)[1] == B_KS else 64))
                if unit_at(j)[0] == "kr":
                    act.wait_ge(pair_in, at(l, 64, 32))
                for src, dst in split_views(unit_at(j), j % RAW_SLOTS, wh[:, j % WT_SLOTS, :]):
                    last = act.activation(dst, src, ACT.Copy)
                last.then_inc(hi_done, 1)

            def ahead(l, j, more=0):
                if j + AHEAD < UNITS:
                    split_hi(l, j + AHEAD, more)

            def normalise(l, s):
                for t in range(TT):
                    act.wait_ge(nm_done, at(l, 4 * TT, TT * s + t + 1))
                    act.activation(xb[:, t, :], xb[:, t, :], ACT.Identity, bias=nmr[:, t:t + 1],
                                   scale=rstd[:, t:t + 1]).then_inc(xn_done, 1)

            def evacuate(l, idx, s=None):
                for k in range(KT):
                    if k % 2 == 0:
                        act.wait_ge(tp_ready, at(l, 16, 4 * idx + k // 2 + 1))
                    src = tp_bank(k // 2)[:, k % 2, :, :].rearrange("p t n -> p (t n)")
                    if s is None:
                        act.activation(z[:, k, :], src, ACT.Copy).then_inc(xf_done, 1)
                    else:
                        act.activation(z[:, k, :], src, ACT.Identity, bias=col(LNB + 8 * s + k),
                                       scale=col(LNG + 8 * s + k)).then_inc(xf_done, 1)

            def silu(l, f, up, more=0):
                act.wait_ge(units_used, unit_done(l, up, more))
                act.activation(hs[:, f % 2, :], ps[:, 4 + f % 2, 0:256], ACT.Silu).then_inc(silu_done, 1)

            def ffn(l, j0):
                for n in range(3):
                    ahead(l, j0 + n)
                silu(l, 0, j0 + 1)
                ahead(l, j0 + 3)
                ahead(l, j0 + 4)

                def turn(j, i=0):
                    ahead(l, j, i)
                    silu(l, 1, j - 2, i)
                    for n in range(1, 4):
                        ahead(l, j + n, i)
                    silu(l, 2, j + 1, i)
                    ahead(l, j + 4, i)
                    ahead(l, j + 5, i)
                with act.Fori(0, FT // 2 - 2) as i:
                    turn(j0 + 5, i)
                turn(j0 + 5 + 6 * (FT // 2 - 2))
                silu(l, FT - 1, j0 + FFN_UNITS - 3)
                ahead(l, j0 + FFN_UNITS - 1)

            def pa_wait(l, name):
                act.wait_ge(*ready(l, name))
                return pa_tile(name)

            def pa_main(l, name):
                src = pa_wait(l, name)[:, 0:S]
                bcol = col(BIAS[name])
                if name in ("dcq0", "dcq1", "dckv"):
                    i = ("dcq0", "dcq1", "dckv").index(name)
                    act.activation(cqf[:, i, :], src, ACT.Identity, bias=bcol).then_inc(pa_out, 1)
                elif name == "kc":
                    for i in range(2):
                        r = slice(64 * i, 64 * i + 64)
                        act.activation(x2[0:64, i, :], src[r, :], ACT.Identity, bias=bcol[r, :])
                        last = act.activation(x2[64:128, i, 0:S - 1], src[r, 1:S], ACT.Identity, bias=bcol[r, :])
                    last.then_inc(pa_out, 1)
                elif name == "ks":
                    for i in range(2):
                        r = slice(64 * i, 64 * i + 64)
                        act.activation(kB[0:64, i, :], src[r, :], ACT.Identity, bias=bcol[r, :])
                        last = act.activation(kB[64:128, i, :], src[r, :], ACT.Identity, bias=bcol[r, :])
                    last.then_inc(pa_out, 1)
                else:
                    dst = {"bq": qB, "cq": qC, "ck": kC, "aq": qA, "ak": kA}[name[:2]][:, int(name[2]), :]
                    act.activation(dst, src, ACT.Identity, bias=bcol).then_inc(pa_out, 1)

            def exp_head(l, n):
                if HEADS[n][2] == "cmp":
                    act.wait_ge(s_max, at(l, NSLOT, n + 1))
                    act.activation(pc[:, :, :, 0:CMPW], pc[:, :, :, 0:CMPW], ACT.Exp).then_inc(p_exp, 1)
                    return
                act.wait_ge(s_max, at(l, NSLOT, n + 1))
                i = n % 2
                act.activation(pS[:, i, 0:P], pS[:, i, 0:P], ACT.Exp, bias=stat[:, i, 1, 0:1], accum_out=stat[:, i, 2, 0:1])
                act.activation(pS[:, i, P:3 * P], pS[:, i, P:3 * P], ACT.Exp, bias=stat[:, i, 1, 1:2],
                               accum_out=stat[:, i, 2, 1:2]).then_inc(p_exp, 1)

            def copy_turned(l, n):
                act.wait_ge(pt_ready, at(l, NSLOT, n + 1))
                if HEADS[n][2] == "cmp":
                    act.activation(pcT[:, :], PT_BANK[:, 0:S], ACT.Copy).then_inc(pt_out, 1)
                    return
                if n >= 2:
                    act.wait_ge(pv_done, at(l, NSLOT, n - 1))
                act.activation(pT[:, n % 2, 0:3 * P], PT_BANK[:, 0:3 * P], ACT.Copy).then_inc(pt_out, 1)

            def pair_hi(l, pair):
                act.wait_ge(pv_done, at(l, NSLOT, PAIR_END[pair] + 1))
                s_ = pair % 4
                act.activation(oTh[:, s_, :], o_bank(pair), ACT.Copy).then_inc(o_hi, 1)

            def mixer(l):
                for n in range(NPROJ):
                    if n - 1 in MAIN_PA:
                        pa_main(l, MAIN_PA[n - 1])
                    if n == 9:
                        src = pa_wait(l, "ssq")
                        act.activation(rms[:, 0, :], src[:, 0:S], ACT.Sqrt, bias=eps_rms[:, 0:1], scale=1.0 / 256)
                        act.activation(rms[:, 1, :], src[:, S:2 * S], ACT.Sqrt, bias=eps_rms[:, 0:1], scale=1.0 / 128)\
                            .then_inc(pa_out, 1)
                        act.wait_ge(*evacuated(l, "kr"))
                        act.activation(krs[0:32, :], krt[32:64, :], ACT.Copy).then_inc(kr_shift, 1)
                    if n == 12:
                        act.wait_ge(kr_added, at(l, 1, 1))
                        src = krs[0:32, :].unsqueeze(1).broadcast_to([32, NH, S])
                        act.activation(kD[64:96, :, :], src, ACT.Copy).then_inc(kr_sum, 1)
                        act.activation(kD[96:128, :, :], src, ACT.Copy).then_inc(kr_sum, 1)
                        act.wait_ge(*evacuated(l, "gf"))
                        act.activation(gth[:, :, :], gl[:, :, 0:12], ACT.Tanh, scale=0.5).then_inc(gth_done, 1)
                        act.wait_ge(fx_abs, at(l, 1, 1))
                        act.activation(fx[:, 2, :, :], fx[:, 1, :, :], ACT.Exp, scale=-1.0).then_inc(fx_exp, 1)
                        act.wait_ge(fx_exp, at(l, 1, 1))
                        act.activation(fx[:, 3, :, :], fx[:, 2, :, :], ACT.Ln, bias=1.0).then_inc(fx_ln, 1)
                    if n == U_UKV:
                        for i in range(2):
                            src = pa_wait(l, f"kn{i}")
                            act.activation(kD[0:64, 2 * i, :], src[0:64, 0:S], ACT.Copy)
                            act.activation(kD[0:64, 2 * i + 1, :], src[64:128, 0:S], ACT.Copy).then_inc(pa_out, 1)
                    if n in (U_W1 + 5, U_W1 + 9):
                        br = 0 if n == U_W1 + 5 else 1
                        act.wait_ge(hu_done, at(l, 2, br + 1))
                        act.activation(hu[:, br, :], hu[:, br, :], ACT.Tanh, scale=0.7978845608028654).then_inc(hg_done, 1)
                    ahead(l, MIX0 + n)
                step = 0
                for n in range(NPROJ, U_WO):
                    if n == NPROJ:
                        src = pa_wait(l, "cmp")
                        act.activation(kcmp[0:64, 0:CMPW], src[0:64, 0:CMPW], ACT.Copy)
                        act.activation(kcmp[64:128, CMPW:2 * CMPW], src[64:128, 0:CMPW], ACT.Copy)
                        act.activation(vcmp[:, :], src[:, 64:128], ACT.Copy).then_inc(pa_out, 1)
                    if MIXER[n - 1][0] == "gate":
                        gate_tanh(l, step - 1)
                    ahead(l, MIX0 + n)
                    if MIXER[n][0] != "gate":
                        continue
                    if step in PAIR_AT:
                        pair_hi(l, PAIR_AT[step])
                    if step < NSLOT:
                        exp_head(l, step)
                    if 1 <= step <= NSLOT:
                        copy_turned(l, step - 1)
                    step += 1
                for k in range(KT):
                    act.wait_ge(y_out, at(l, 3 * KT, 2 * KT + k + 1))
                    act.activation(xTh[:, k, :], z[:, k, :], ACT.Copy, scale=0.5).then_inc(zh_done, 1)
                    ahead(l, MIX0 + U_WO + k)

            def gate_tanh(l, g):
                b, n = divmod(g, KT)
                src = pa_wait(l, f"gate{b}_{n}")[:, 0:S]
                if b == 2:
                    act.wait_ge(*evacuated(l, f"y0_{n}"))
                if b == 3:
                    act.wait_ge(y_out, at(l, 3 * KT, n + 1))
                act.activation(gates[:, KT * (b % 2) + n, :], src, ACT.Tanh, bias=col(HALF + BRANCHES[b] * KT + n),
                               scale=0.5).then_inc(pa_out, 1)

            def cross(l):
                j0 = MIX0 + U_X
                normalise(l, 1)
                evacuate(l, 3, 1)
                act.wait_ge(units_used, unit_done(l, j0 + 1))
                act.activation(xk[:, :, :].rearrange("p i s -> p (i s)"), ps[:, 4, :], ACT.Copy).then_inc(xk_out, 1)
                for i in range(5):
                    ahead(l, j0 + i)
                act.wait_ge(units_used, unit_done(l, j0 + 5))
                act.activation(xq[:, :, :].rearrange("p i s -> p (i s)"), ps[:, 4, :], ACT.Copy).then_inc(xq_out, 1)
                ahead(l, j0 + 5)
                for h in range(NH + 1):
                    if h < NH:
                        act.wait_ge(xmax, at(l, NH, h + 1))
                        if h >= 2:
                            act.wait_ge(xpt_ready, at(l, NH, h - 1))
                        i = h % 2
                        for q in range(TT):
                            last = act.activation(pS[:, i, S * q:S * q + S], ps[:, h, S * q:S * q + S], ACT.Exp,
                                                  bias=stat[:, i, 1, q:q + 1], scale=SCALE, accum_out=stat[:, i, 2, q:q + 1])
                        last.then_inc(xexp, 1)
                    if h >= 1:
                        g = h - 1
                        act.wait_ge(xpt_ready, at(l, NH, g + 1))
                        if g >= 2:
                            act.wait_ge(xo_ready, at(l, NH, g - 1))
                        act.activation(pT[:, g % 2, :], ps[:, 5 + g % 2, :], ACT.Copy).then_inc(xpt_out, 1)
                for k in range(2):
                    act.wait_ge(xo_ready, at(l, NH, 2 * k + 2))
                    act.activation(oTh[:, k, :], ps[:, 7 if k == 0 else 4, 0:S], ACT.Copy).then_inc(xo_hi, 1)
                ahead(l, j0 + 6)
                ahead(l, j0 + 7)
                normalise(l, 2)
                evacuate(l, 4, 2)

            act.wait_ge(credits_set, 1)
            evacuate(0, 0)
            act.wait_ge(trig_done, 1)
            act.activation(cs[:, :], angle, ACT.Sin).then_inc(sin_done, 1)
            act.wait_ge(sin_done, 1)
            act.activation(csq[64:128, :], cs[64:128, :], ACT.Copy).then_inc(sin_done, 1)
            act.wait_ge(xT_ready, 4)
            evacuate(0, 1)
            with act.Fori(0, L) as l:
                for j in range(AHEAD):
                    split_hi(l, j)
                ffn(l, 0)
                act.wait_ge(cols_ready, at(l, 1, 1))
                normalise(l, 0)
                evacuate(l, 2, 0)
                mixer(l)
                cross(l)
                ffn(l, FFN2_0)
                normalise(l, 3)
                evacuate(l, 5, 3)

        @block.vector
        def _(dve):
            def split_lo(l, j, more=0):
                dve.wait_ge(hi_done, units_before(l, j, more) + 1)
                views = zip(split_views(unit_at(j), j % RAW_SLOTS, wh[:, j % WT_SLOTS, :]),
                            split_views(unit_at(j), j % RAW_SLOTS, wl[:, j % WT_SLOTS, :]))
                for (src, hi), (_, lo) in views:
                    last = dve.tensor_tensor(lo, src, hi.bitcast(F32), ALU.subtract)
                last.then_inc(lo_done, 1)

            def ahead(l, j, more=0):
                if j + AHEAD < UNITS:
                    split_lo(l, j + AHEAD, more)

            def split_act(fh, fl, src):
                dve.tensor_copy(fh, src)
                dve.drain()
                return dve.tensor_tensor(fl, src, fh.bitcast(F32), ALU.subtract)

            def split_x(l, idx, th=xTh, tl=xTl):
                for q in range(4):
                    dve.wait_ge(xf_done, at(l, 32, 8 * idx + 2 * q + 2))
                    k = slice(2 * q, 2 * q + 2)
                    split_act(th[:, k, :], tl[:, k, :], z[:, k, :]).then_inc(xT_ready, 1)

            def norm(l, s, j_end):
                for t in range(TT):
                    if t == 0:
                        dve.wait_ge(acc_ready, at(l, 4, s + 1))
                    else:
                        dve.wait_ge(units_used, unit_done(l, j_end))
                    dve.wait_ge(x_done, at(l, 4 * TT, TT * s + t + 1))
                    acc = ps[:, 2 * t:2 * t + 2, :].rearrange("p a b -> p (a b)")
                    dve.scalar_tensor_tensor(xb[:, t, :], xb[:, t, :], ALPHA, acc, ALU.mult, ALU.add)
                    dve.drain()
                    for c in range(2):
                        dve.bn_stats(bst[:, t, c, :], xb[:, t, 512 * c:512 * c + 512])
                    dve.drain()
                    dve.bn_aggr(mv[:, t, :], bst[:, t, :, :].rearrange("p c s -> p (c s)"))
                    dve.drain()
                    dve.tensor_scalar(vare[:, t:t + 1], mv[:, t, 1:2], LN_EPS, None, ALU.add).then_inc(stat_done, 1)
                for t in range(TT):
                    dve.wait_ge(rstd_done, at(l, 4 * TT, TT * s + t + 1))
                    dve.scalar_tensor_tensor(nmr[:, t:t + 1], mv[:, t, 0:1], -1.0, rstd[:, t:t + 1], ALU.mult, ALU.mult)\
                        .then_inc(nm_done, 1)

            def hidden(l, which, f, more=0):
                dve.wait_ge(silu_done, at(l, 2 * FT, FT * which + f + 1) + more * 2)
                p = f % 2
                dve.scalar_tensor_tensor(hf[:, p, :], hs[:, p, :], 0.5, ps[:, 4 + p, 256:512], ALU.mult, ALU.mult)\
                    .then_inc(gu_out, 1)
                dve.drain()
                split_act(oTh[:, p, :], oTl[:, p, :], hf[:, p, :]).then_inc(hT_ready, 1)

            def ffn(l, which, j0):
                for n in range(3):
                    ahead(l, j0 + n)
                hidden(l, which, 0)
                ahead(l, j0 + 3)
                ahead(l, j0 + 4)

                def turn(j, i=0):
                    f = 1 + (j - j0 - 5) // 3
                    ahead(l, j, i)
                    hidden(l, which, f, i)
                    for n in range(1, 4):
                        ahead(l, j + n, i)
                    hidden(l, which, f + 1, i)
                    ahead(l, j + 4, i)
                    ahead(l, j + 5, i)
                with dve.Fori(0, FT // 2 - 2) as i:
                    turn(j0 + 5, i)
                turn(j0 + 5 + 6 * (FT // 2 - 2))
                hidden(l, which, FT - 1)
                ahead(l, j0 + FFN_UNITS - 1)

            def pd_wait(l, name):
                dve.wait_ge(*ready(l, name))
                return pd_tile(name)

            def value_out(l, name, dst, b0):
                n = dst.shape[2]
                src = pd_wait(l, name)[:, 0:TT * n].rearrange("p (t n) -> p t n", t=TT)
                bb = vbias[:, b0:b0 + n].unsqueeze(1).broadcast_to([P, TT, n])
                dve.tensor_tensor(dst, src, bb, ALU.add).then_inc(pd_out, 1)

            def softmax_max(l, n):
                b, h, kind = HEADS[n]
                dve.wait_ge(s_ready, at(l, NSLOT, n + 1))
                i = n % 2
                src = S_BANK
                if kind == "cmp":
                    lg = pc[:, :, :, 0:CMPW].rearrange("p q h c -> p (q h) c")
                    tab = const[:, C_CMPB:C_CMPB + 128].rearrange("p (g c) -> p g c", c=CMPW)
                    dve.scalar_tensor_tensor(lg, src[:, 0:128].rearrange("p (g c) -> p g c", c=CMPW), SCALE, tab,
                                             ALU.mult, ALU.add).then_inc(s_out, 1)
                    dve.drain()
                    dve.tensor_reduce(cstat[:, 0, :], lg, AX.X, ALU.max)
                    dve.drain()
                    dve.tensor_tensor(lg, lg, cstat[:, 0, :].unsqueeze(2).broadcast_to([P, 8, CMPW]), ALU.subtract)\
                        .then_inc(s_max, 1)
                    return
                scale = SCALE_D if kind == "d" else SCALE
                if n >= 2:
                    dve.wait_ge(pt_ready, at(l, NSLOT, n - 1))
                dve.memset(fence[:, :], 0.0)
                dve.tensor_tensor_reduce(pS[:, i, 0:P], src[:, 0:P], bias_table(kind, h, 0), scale, -3.4e38,
                                         ALU.add, ALU.max, stat[:, i, 0, 0:1])
                dve.tensor_tensor_reduce(pS[:, i, P:3 * P], src[:, P:3 * P], bias_table(kind, h, 1), scale, -3.4e38,
                                         ALU.add, ALU.max, stat[:, i, 0, 1:2]).then_inc(s_out, 1)
                dve.drain()
                dve.tensor_scalar(stat[:, i, 1, :], stat[:, i, 0, :], -1.0, None, ALU.mult).then_inc(s_max, 1)

            def softmax_norm(l, n):
                b, h, kind = HEADS[n]
                dve.wait_ge(p_exp, at(l, NSLOT, n + 1))
                i = n % 2
                if kind == "cmp":
                    lg = pc[:, :, :, 0:CMPW].rearrange("p q h c -> p (q h) c")
                    tab = const[:, C_CMPM:C_CMPM + 128].rearrange("p (g c) -> p g c", c=CMPW)
                    dve.tensor_tensor(lg, lg, tab, ALU.mult)
                    dve.drain()
                    dve.tensor_reduce(cstat[:, 1, :], lg, AX.X, ALU.add)
                    dve.drain()
                    dve.tensor_scalar(cstat[:, 1, :], cstat[:, 1, :], 1e-30, None, ALU.max)
                    dve.drain()
                    dve.reciprocal(cstat[:, 2, :], cstat[:, 1, :])
                    dve.drain()
                    g0 = gt[:, :, :].rearrange("p q (h b) -> p q h b", b=3)[:, :, :, 0]
                    dve.tensor_tensor(cstat[:, 2, :].rearrange("p (q h) -> p q h", h=NH),
                                      cstat[:, 2, :].rearrange("p (q h) -> p q h", h=NH), g0, ALU.mult)
                    dve.drain()
                    dve.tensor_tensor(lg, lg, cstat[:, 2, :].unsqueeze(2).broadcast_to([P, 8, CMPW]), ALU.mult)\
                        .then_inc(p_ready, 1)
                    return
                dve.tensor_scalar(stat[:, i, 2, :], stat[:, i, 2, :], 1e-30, None, ALU.max)
                dve.drain()
                dve.reciprocal(stat[:, i, 3, :], stat[:, i, 2, :])
                dve.drain()
                parts = ((0, 0, P), (1, P, 3 * P))
                for q, c0, c1 in parts:
                    if kind in "sw":
                        g = 3 * h + (1 if kind == "s" else 2)
                        last = dve.tensor_scalar(pS[:, i, c0:c1], pS[:, i, c0:c1], stat[:, i, 3, q:q + 1],
                                                 gt[:, q, g:g + 1], ALU.mult, ALU.mult)
                    else:
                        last = dve.tensor_scalar(pS[:, i, c0:c1], pS[:, i, c0:c1], stat[:, i, 3, q:q + 1], None, ALU.mult)
                last.then_inc(p_ready, 1)

            def pair_lo(l, pair):
                dve.wait_ge(o_hi, at(l, PAIRS, pair + 1))
                s_ = pair % 4
                dve.tensor_tensor(oTl[:, s_, :], o_bank(pair), oTh[:, s_, :].bitcast(F32), ALU.subtract).then_inc(o_out, 1)

            def merge(l, b, tiles):
                for n in tiles:
                    src = pd_wait(l, f"y{b}_{n}")[:, 0:S]
                    g = gates[:, KT * (b % 2) + n, :]
                    dve.wait_ge(*evacuated(l, f"gate{b}_{n}"))
                    dst = z[:, n, :] if b == 0 else g
                    dve.scalar_tensor_tensor(dst, g, 1.0, src, ALU.add, ALU.mult).then_inc(pd_out, 1)
                if b:
                    dve.drain()
                    for n in tiles:
                        dve.tensor_tensor(z[:, n, :], z[:, n, :], gates[:, KT * (b % 2) + n, :], ALU.add).then_inc(y_out, 1)

            def mixer(l):
                for n in range(NPROJ):
                    if n == 3:
                        dve.wait_ge(*evacuated(l, "dckv"))
                        dve.tensor_tensor(sq, cqf, cqf, ALU.mult).then_inc(sq_done, 1)
                    if n == 4:
                        src = pd_wait(l, "kr")
                        bcol = col(BIAS["kr"])
                        dve.scalar_tensor_tensor(krt[0:64, :], src[0:64, 0:S], bcol[0:64, :], cs[0:64, :], ALU.add, ALU.mult)
                        dve.tensor_scalar(krt[64:80, :], src[64:80, 0:S], bcol[64:80, :], None, ALU.add).then_inc(pd_out, 1)
                    if n == 6:
                        dve.wait_ge(*evacuated(l, "kc"))
                        for br in range(2):
                            for lp in range(16):
                                src = x2[:, br, 2 * lp:2 * lp + 16 * (CMP - 1) + 1:16]
                                last = dve.tensor_scalar(blkf[:, br, lp, :], src, col(POS + 16 * br + lp), None, ALU.add)
                        dve.drain()
                        parts = (w[:, 0:32 * CMPW].rearrange("p (bl c) -> p bl c", c=CMPW)[:, :, 0:CMP] for w in (blkh, blkl))
                        split_act(*parts,
                                  blkf[:, :, :, :].rearrange("p b l c -> p (b l) c")).then_inc(blk_ready, 1)
                    if n == 9:
                        value_out(l, "vs", vB[:, :, :], 256)
                    if n == 10:
                        dve.wait_ge(*evacuated(l, "ssq"))
                        dve.reciprocal(rms, rms)
                        dve.drain()
                        for i in range(3):
                            dve.scalar_tensor_tensor(cqf[:, i, :], cqf[:, i, :], col(QN + i), rms[:, i // 2, :],
                                                     ALU.mult, ALU.mult)
                        dve.drain()
                        split_act(oTh[:, 0:3, :], oTl[:, 0:3, :], cqf).then_inc(cqn_ready, 1)
                        dve.wait_ge(kr_shift, at(l, 1, 1))
                        dve.tensor_tensor(krs[0:32, :], krt[0:32, :], krs[0:32, :], ALU.add).then_inc(kr_added, 1)
                    if n == 7:
                        src = pd_wait(l, "gf")[:, 0:32].rearrange("p (t n) -> p t n", t=TT)
                        dve.tensor_copy(gl[:, :, :], src).then_inc(pd_out, 1)
                        dve.drain()
                        f = gl[:, :, 12:16]
                        dve.tensor_scalar(fx[:, 0, :, :], f, -1.0, None, ALU.mult)
                        dve.tensor_scalar(fx[:, 4, :, :], f, 0.0, None, ALU.min)
                        dve.drain()
                        dve.tensor_tensor(fx[:, 1, :, :], f, fx[:, 0, :, :], ALU.max).then_inc(fx_abs, 1)
                    if n == 14:
                        dve.wait_ge(gth_done, at(l, 1, 1))
                        dve.tensor_scalar(gt[:, :, :], gth[:, :, :], 0.5, 0.5, ALU.mult, ALU.add)
                        dve.wait_ge(fx_ln, at(l, 1, 1))
                        dve.tensor_tensor(fx[:, 0, :, :], fx[:, 4, :, :], fx[:, 3, :, :], ALU.subtract)
                        dve.drain()
                        for i in range(2):
                            last = dve.tensor_scalar(ls8[:, :, 4 * i:4 * i + 4], fx[:, 0, :, :], 1.0 / SCALE, None, ALU.mult)
                        last.then_inc(ls_ready, 1)
                    if n == U_CV + 2:
                        value_out(l, "cv", vC[:, :, :], 384)
                    if n in (U_UQ, U_UQ + 1):
                        for h in (2 * (n - U_UQ), 2 * (n - U_UQ) + 1):
                            src = pd_wait(l, f"q{h}")[:, 0:S]
                            dve.tensor_tensor(qD[:, h, :], src, csq[:, :], ALU.mult).then_inc(pd_out, 1)
                    if n == U_UKV:
                        for t in range(TT):
                            src = pd_wait(l, f"vd{t}")[:, 0:S]
                            dve.tensor_copy(vD[:, t, :], src).then_inc(pd_out, 1)
                    if n in (U_W1 + 4, U_W1 + 8):
                        br = 0 if n == U_W1 + 4 else 1
                        src = pd_wait(l, f"hid{br}")
                        dve.tensor_copy(hx[:, br, :], src[0:CMPW, 0:S]).then_inc(pd_out, 1)
                        dve.drain()
                        dve.tensor_tensor(hu[:, br, :], hx[:, br, :], hx[:, br, :], ALU.mult)
                        dve.drain()
                        dve.tensor_scalar(hu[:, br, :], hu[:, br, :], 0.044715, 1.0, ALU.mult, ALU.add)
                        dve.drain()
                        dve.tensor_tensor(hu[:, br, :], hu[:, br, :], hx[:, br, :], ALU.mult).then_inc(hu_done, 1)
                    if n == U_W1 + 5:
                        src = pd_wait(l, "decay")[0:8, 0:S]
                        for h in range(NH):
                            sel = const[0:8, C_SEL + h:C_SEL + 13 + h]
                            dve.tensor_scalar(lq[:, h, :], src, sel[:, 0:1], sel[:, 4:5], ALU.mult, ALU.add)
                            last = dve.tensor_scalar(rk[:, h, :], src, sel[:, 8:9], sel[:, 12:13], ALU.mult, ALU.add)
                        last.then_inc(pd_out, 1)
                    if n in (U_W1 + 6, U_W1 + 10):
                        br = 0 if n == U_W1 + 6 else 1
                        dve.wait_ge(hg_done, at(l, 2, br + 1))
                        dve.scalar_tensor_tensor(hx[:, br, :], hu[:, br, :], 1.0, hx[:, br, :], ALU.add, ALU.mult)\
                            .then_inc(gelu_done, 1)
                    if n in (U_W1 + 9, U_W1 + 13):
                        br = (n - U_W1 - 9) // 4
                        src = pd_wait(l, f"turn{br}")[:, 0:2 * CMPW]
                        dve.tensor_scalar(hT[:, :, :].rearrange("p k c -> p (k c)"), src, 0.5, None, ALU.mult)\
                            .then_inc(pd_out, 1)
                        dve.drain()
                        src = hT[:, :, :]
                        if br == 0:
                            split_act(hkh[:, :, :], hkl[:, :, :], src).then_inc(hid_ready, 1)
                        else:
                            for k in range(2):
                                s_ = src[:, k, :].unsqueeze(1).broadcast_to([P, NH, CMPW])
                                last = split_act(hvh[:, k, :, 0:CMPW], hvl[:, k, :, 0:CMPW], s_)
                            last.then_inc(hid_ready, 1)
                    if n == U_AV + 2:
                        value_out(l, "av", vA[:, :, :], 0)
                    ahead(l, MIX0 + n)
                step = 0
                for n in range(NPROJ, U_WO):
                    kind, b, i = MIXER[n]
                    if kind == "branch":
                        merge(l, b, range(4 * i, 4 * i + 4))
                        ahead(l, MIX0 + n)
                        continue
                    if step in PAIR_AT:
                        pair_lo(l, PAIR_AT[step])
                    if step < NSLOT:
                        softmax_max(l, step)
                    ahead(l, MIX0 + n)
                    if step < NSLOT:
                        softmax_norm(l, step)
                    step += 1
                for k in range(KT):
                    dve.wait_ge(zh_done, at(l, KT, k + 1))
                    dve.scalar_tensor_tensor(xTl[:, k, :], z[:, k, :], 0.5, xTh[:, k, :].bitcast(F32), ALU.mult,
                                             ALU.subtract).then_inc(z_ready, 1)
                    ahead(l, MIX0 + U_WO + k)

            def cross(l):
                j0 = MIX0 + U_X
                norm(l, 1, j0 - 1)
                split_x(l, 3)
                dve.wait_ge(units_used, unit_done(l, j0 + 3))
                dve.tensor_copy(xv[:, :, :].rearrange("p t n -> p (t n)"), ps[:, 5, :]).then_inc(xv_out, 1)
                for i in range(5):
                    ahead(l, j0 + i)

                def maxima(h):
                    dve.wait_ge(xs_ready, at(l, NH, h + 1))
                    i = h % 2
                    dve.tensor_reduce(stat[:, i, 0, :], ps[:, h, :].rearrange("p (q k) -> p q k", q=TT), AX.X, ALU.max)
                    dve.drain()
                    dve.tensor_scalar(stat[:, i, 1, :], stat[:, i, 0, :], -SCALE, None, ALU.mult).then_inc(xmax, 1)

                maxima(0)
                ahead(l, j0 + 5)
                for h in range(NH):
                    if h + 1 < NH:
                        maxima(h + 1)
                    dve.wait_ge(xexp, at(l, NH, h + 1))
                    i = h % 2
                    dve.reciprocal(stat[:, i, 3, :], stat[:, i, 2, :])
                    dve.drain()
                    for q in range(TT):
                        last = dve.tensor_scalar(pS[:, i, S * q:S * q + S], pS[:, i, S * q:S * q + S],
                                                 stat[:, i, 3, q:q + 1], None, ALU.mult)
                    last.then_inc(xp_ready, 1)
                for k in range(2):
                    dve.wait_ge(xo_hi, at(l, 2, k + 1))
                    dve.tensor_tensor(oTl[:, k, :], ps[:, 7 if k == 0 else 4, 0:S], oTh[:, k, :].bitcast(F32),
                                      ALU.subtract).then_inc(xo_out, 1)
                ahead(l, j0 + 6)
                ahead(l, j0 + 7)
                norm(l, 2, j0 + 7)
                split_x(l, 4)

            dve.memset(eps_rms[:, :], RMS_EPS)
            dve.sem_inc(lo_done, RAW_SLOTS)
            dve.sem_inc(pa_out, 2)
            dve.sem_inc(pd_out, 2)
            dve.sem_inc(gu_out, 2)
            dve.sem_inc(s_out, 1)
            dve.sem_inc(pt_out, 1)
            dve.sem_inc(o_out, 2)
            dve.sem_inc(x_done, TT)
            dve.drain()
            dve.sem_inc(credits_set, 1)
            dve.wait_ge(const_in, 16 * N_CONST_DMAS)
            tf, an, kn, rr = (trig[:, i * S:(i + 1) * S] for i in range(4))
            dve.tensor_copy(tf, posi)
            dve.drain()
            dve.tensor_scalar(an, tf, const[:, C_INV:C_INV + 1], None, ALU.mult)
            dve.drain()
            dve.tensor_scalar(kn, an, 1.0 / TWO_PI, const[:, C_OFF:C_OFF + 1], ALU.mult, ALU.add)
            dve.drain()
            dve.tensor_scalar(kn, kn, ROUND, None, ALU.add)
            dve.drain()
            dve.tensor_scalar(kn, kn, ROUND, None, ALU.subtract)
            dve.drain()
            for c in (PI_1, PI_2, PI_3):
                dve.scalar_tensor_tensor(an, kn, -c, an, ALU.mult, ALU.add)
                dve.drain()
            dve.tensor_scalar(an, an, const[:, C_PHASE:C_PHASE + 1], 3.1415925, ALU.add, ALU.min)
            dve.drain()
            dve.tensor_scalar(angle, an, -3.1415925, None, ALU.max).then_inc(trig_done, 1)
            dve.wait_ge(cols_psum, 1)
            dve.tensor_copy(cols[:, :], ps[:, 5, 0:294])
            split_x(0, 0, memTh, memTl)
            split_x(0, 1)
            with dve.Fori(0, L) as l:
                for dst, n, src in ((0, NB, 0), (LNG, 32, 96), (LNB, 32, 160), (POS, 32, 224), (QN, 2, 288), (KN, 1, 292)):
                    dve.tensor_copy(cur[:, dst:dst + n], cols[:, bass.ds(l * n + src, n)])
                dve.drain()
                dve.tensor_scalar(cur[:, HALF:HALF + 32], cur[:, GB0:GB0 + 32], 0.5, None, ALU.mult).then_inc(cols_ready, 1)
                for j in range(AHEAD):
                    split_lo(l, j)
                ffn(l, 0, 0)
                norm(l, 0, FFN_UNITS - 1)
                split_x(l, 2)
                dve.wait_ge(vb_in, at(l, 64, 64))
                mixer(l)
                cross(l)
                ffn(l, 1, FFN2_0)
                norm(l, 3, UNITS - 1)
                split_x(l, 5)


_INPUTS = ("x", "mem", "positions", "ln_g", "ln_b", "ffn1_w_in", "ffn1_w_out", "ffn2_w_in", "ffn2_w_out", "w_in",
           "b_in", "w_branch", "w_o", "mla_q_norm", "mla_w_uq", "mla_kv_norm", "mla_w_ukv", "nsa_cmp_pos",
           "nsa_cmp_w1", "nsa_cmp_w2", "xa_w_q", "xa_w_kv", "xa_w_o")


def kernel(**inputs):
    import concourse.bacc as bacc
    from concourse.bass_utils import run_bass_kernel_spmd
    nc = bacc.Bacc("TRN2", target_bir_lowering=False, num_devices=1)
    arrays, a = {}, {}
    for name in _INPUTS:
        v = np.ascontiguousarray(inputs[name])
        arrays["in_" + name] = v
        a[name] = nc.dram_tensor("in_" + name, v.shape, mybir.dt.from_np(v.dtype), kind="ExternalInput").ap()
    arrays["in_const"] = constants()
    a["const"] = nc.dram_tensor("in_const", (P, NCONST), F32, kind="ExternalInput").ap()
    out = nc.dram_tensor("out_0", (1, S, D), F32, kind="ExternalOutput").ap()
    build(nc, a, out)
    r = run_bass_kernel_spmd(nc, [arrays], core_ids=[0])
    return r.results[0]["out_0"]
```

```python
from contextlib import ExitStack

import numpy as np
import concourse.bass as bass
from concourse import mybir

F32 = mybir.dt.float32
F32R = mybir.dt.float32r
I32 = mybir.dt.int32
ACT = mybir.ActivationFunctionType
ALU = mybir.AluOpType
AX = mybir.AxisListType

P = 128
D = 1024
S = 256
L = 2
FF = 2816
KT = D // P
TT = S // P
FT = FF // P
HD = 64
NH = 4
CMP = 15
CMPW = 16
WINDOW = 80
SCALE = HD ** -0.5
SCALE_D = 96 ** -0.5
ALPHA = (2 * L) ** 0.25
LN_EPS = 1e-5
RMS_EPS = 1e-6
NEG = -1e30

RAW_SLOTS = 3
WT_SLOTS = 6
AHEAD = WT_SLOTS - 1

A_Q, A_K, A_V, B_Q, B_KC, B_KS, B_VS, B_KW, B_VW, B_G = 0, 256, 512, 768, 1024, 1152, 1216, 1280, 1344, 1408
C_Q, C_K, C_V, C_F, D_CQ, D_CKV, D_KR, G_M = 1420, 1676, 1932, 2188, 2192, 2448, 2576, 2608

BRANCHES = (3, 2, 0, 1)
PROJ = [("col", D_CQ), ("col", D_CQ + 128), ("col", D_CKV), ("kr",), ("col", B_KC), ("pair", B_KS),
        ("col", B_Q), ("col", B_Q + 128), ("pair", B_VS),
        ("col", C_Q), ("w1", 0, 0), ("col", C_Q + 128), ("w1", 0, 1), ("col", C_K), ("w1", 0, 2),
        ("col", C_K + 128), ("w1", 0, 3), ("half", C_V, 0), ("half", C_V, 1), ("w1", 1, 0), ("col", A_Q), ("uq", 0),
        ("w1", 1, 1), ("col", A_Q + 128), ("uq", 1), ("w1", 1, 2), ("col", A_K), ("w1", 1, 3), ("ukv",),
        ("col", A_K + 128), ("half", A_V, 0), ("half", A_V, 1)]
MIXER = list(PROJ)
AFTER_GATE = {8: (0, 0), 10: (0, 1), 13: (1, 0), 16: (1, 1), 20: (2, 0), 24: (2, 1), 28: (3, 0), 31: (3, 1)}
for _s in range(4 * KT):
    MIXER += [("gate", *divmod(_s, KT))] 
    if _s == 3:
        MIXER += [("w2", 0), ("w2", 1)]
    if _s in AFTER_GATE:
        MIXER += [("branch", *AFTER_GATE[_s])]
MIXER += [("wo", _k) for _k in range(KT)]
MIXER += [("xk", 0), ("xk", 1), ("xv", 0), ("xv", 1), ("xq", 0), ("xq", 1), ("xo", 0), ("xo", 1)]

FFN_UNITS = 3 * FT
MIX0 = FFN_UNITS
FFN2_0 = MIX0 + len(MIXER)
UNITS = FFN2_0 + FFN_UNITS
assert UNITS % WT_SLOTS == 0 and UNITS % RAW_SLOTS == 0 and WT_SLOTS == 6 and RAW_SLOTS == 3

PA = ["dcq0", "dcq1", "dckv", "kc", "ks", "bq0", "bq1", "ssq", "cq0", "cq1", "ck0", "ck1", "aq0", "aq1", "ak0", "kn0",
      "kn1", "ak1"] + [f"gate0_{n}" for n in range(4)] + ["cmp"] + [f"gate{b}_{n}" for b in range(4) for n in
                                                                    range(KT) if (b, n) > (0, 3)]
PD = ["kr", "gf", "vs", "vst", "cv", "decay", "q0", "q1", "q2", "q3", "turn0", "vd0", "vd1", "av", "turn1"] + [
    f"y{b}_{n}" for b in range(4) for n in range(KT)]

MAIN_PA = {PROJ.index(("col", c)): name for c, name in (
    (D_CQ, "dcq0"), (D_CQ + 128, "dcq1"), (D_CKV, "dckv"), (B_KC, "kc"), (B_Q, "bq0"), (B_Q + 128, "bq1"),
    (C_Q, "cq0"), (C_Q + 128, "cq1"), (C_K, "ck0"), (C_K + 128, "ck1"), (A_Q, "aq0"), (A_Q + 128, "aq1"),
    (A_K, "ak0"), (A_K + 128, "ak1"))} | {PROJ.index(("pair", B_KS)): "ks"}
U_KR, U_VS, U_CV, U_UQ0, U_UQ1, U_UKV, U_AV, U_W2, U_WO = (MIXER.index(u) for u in (
    ("kr",), ("pair", B_VS), ("half", C_V, 0), ("uq", 0), ("uq", 1), ("ukv",), ("half", A_V, 0), ("w2", 0), ("wo", 0)))
U_HID = tuple(PROJ.index(("w1", br, 3)) for br in range(2))
U_DECAY = PROJ.index(("w1", 1, 0))
U_TURN = (U_HID[0] + 9, len(PROJ) - 1)
NPROJ = len(PROJ)
U_X = U_WO + KT
ENDS_UNIT = {name: n for n, name in MAIN_PA.items()}
ENDS_UNIT |= {"kr": U_KR, "vs": U_VS, "cv": U_CV + 1, "q1": U_UQ0, "q3": U_UQ1, "vd1": U_UKV, "av": U_AV + 1,
              "cmp": U_W2 + 1}
for _n, _u in enumerate(MIXER):
    if _u[0] == "gate":
        ENDS_UNIT[f"gate{_u[1]}_{_u[2]}"] = _n
    if _u[0] == "branch":
        ENDS_UNIT[f"y{_u[1]}_{4 * _u[2] + 3}"] = _n
PA_MID = [n for n in PA if n not in ENDS_UNIT]
PD_MID = [n for n in PD if n not in ENDS_UNIT]

HEADS = [(0, h, "d") for h in range(NH)] + [(1, h, "c") for h in range(NH)] + [(2, h, "a") for h in range(NH)]
CMP_SLOT = len(HEADS)
HEADS += [(3, 0, "cmp")] + [(3, h, kind) for h in range(NH) for kind in ("s", "w")]
NSLOT = len(HEADS)
PAIR_AT = {3: 0, 5: 1, 7: 2, 9: 3, 11: 4, 13: 5, 18: 6, 22: 7}
PAIR_END = {pair: step - 2 for step, pair in PAIR_AT.items()}
PAIRS = 8

BIAS = {"dcq0": 0, "dcq1": 1, "dckv": 2, "kr": 3, "kc": 4, "ks": 5, "bq0": 6, "bq1": 7, "cq0": 8, "cq1": 9,
        "ck0": 10, "ck1": 11, "aq0": 12, "aq1": 13, "ak0": 14, "ak1": 15}
NB = 48
GB0 = 16
LNG, LNB, POS, QN, KN, HALF = NB, NB + 32, NB + 64, NB + 96, NB + 98, NB + 99
NCOLS = HALF + 32

C_ID, C_CAUSAL, C_ALIBI, C_TRI = 0, 128, 384, 384 + 8 * 256
C_CMPB, C_CMPM = C_TRI + 256, C_TRI + 256 + 128
C_INV, C_OFF, C_PHASE, C_SEL = C_CMPM + 128, C_CMPM + 129, C_CMPM + 130, C_CMPM + 131
NCONST = C_SEL + 16
TWO_PI = 2 * np.pi
PI_1 = float(np.float32(6.28125))
PI_2 = 0.0019350051879882812
PI_3 = float(np.float32(TWO_PI - PI_1 - PI_2))
ROUND = float(1.5 * 2 ** 23)


def constants():
    t = np.arange(P)
    c = np.zeros((P, NCONST), np.float32)
    c[:, C_ID:C_ID + P] = np.eye(P)
    diag = np.where(t[None, :] <= t[:, None], 0.0, NEG)
    c[:, C_CAUSAL + P:C_CAUSAL + 2 * P] = diag
    slopes = 2.0 ** -np.arange(1, 9)
    dist = (t[:, None] - t[None, :]).astype(np.float64)
    for i in range(8):
        at = C_ALIBI + 256 * i
        c[:, at:at + P] = -slopes[i] * (dist + P) / SCALE
        c[:, at + P:at + 2 * P] = np.where(dist >= 0, -slopes[i] * dist / SCALE, NEG)
    tri = (t[:, None] <= np.arange(S)[None, :]).astype(np.float32)
    c[:, C_TRI:C_TRI + S] = tri
    for q in range(TT):
        for h in range(NH):
            at = (q * NH + h) * CMPW
            gone = (q * P + t[:, None]) - (np.arange(CMPW) * 16 + 31)[None, :]
            seen = (gone >= 0) & (np.arange(CMPW) < CMP)[None, :]
            c[:, C_CMPB + at:C_CMPB + at + CMPW] = np.where(seen, -slopes[2 * h + 1] * gone, NEG)
            c[:, C_CMPM + at:C_CMPM + at + CMPW] = seen
    inv = (np.float32(10000.0) ** (-np.arange(0, 32, 2, dtype=np.float32) / np.float32(32))).astype(np.float32)
    both = np.concatenate([inv, inv])
    for base in (0, 64):
        c[base:base + 32, C_INV] = both
        c[base + 32:base + 64, C_INV] = np.concatenate([-inv, inv])
        c[base:base + 32, C_OFF] = 0.25
        c[base:base + 32, C_PHASE] = np.pi / 2
    for h in range(NH):
        c[h, C_SEL + h] = 1.0
        c[NH + h, C_SEL + 4 + h] = 1.0
        c[NH + h, C_SEL + 8 + h] = -1.0
        c[h, C_SEL + 12 + h] = 1.0
    return c


def build(nc, a, out):
    with ExitStack() as ctx:
        def sb(name, shape, dt=F32):
            return ctx.enter_context(nc.sbuf_tensor(name, shape, dt))

        def sem(name):
            return ctx.enter_context(nc.semaphore(name))

        raw = sb("raw", [P, RAW_SLOTS, 1024])
        wh = sb("wh", [P, WT_SLOTS, 1024], F32R)
        wl = sb("wl", [P, WT_SLOTS, 1024], F32R)
        xb = sb("xb", [P, TT, D])
        xTh, xTl = sb("xTh", [P, KT, S], F32R), sb("xTl", [P, KT, S], F32R)
        memTh, memTl = sb("memTh", [P, KT, S], F32R), sb("memTl", [P, KT, S], F32R)
        gb = sb("gb", [P, 2, D])
        gates = sb("gates", [P, 2 * KT, S])
        z = sb("z", [P, KT, S])
        oTh, oTl = sb("oTh", [P, 4, S], F32R), sb("oTl", [P, 4, S], F32R)
        qD, kD, vD = sb("qD", [P, NH, S]), sb("kD", [P, NH, S]), sb("vD", [P, TT, 256])
        qC, kC, vC = sb("qC", [P, 2, S]), sb("kC", [P, 2, S]), sb("vC", [P, TT, 256])
        qA, kA, vA = sb("qA", [P, 2, S]), sb("kA", [P, 2, S]), sb("vA", [P, TT, 256])
        qB, kB, vB = sb("qB", [P, 2, S]), sb("kB", [P, 2, S]), sb("vB", [P, TT, 128])
        x2 = sb("x2", [P, 2, S])
        blkf = sb("blkf", [P, 2, 16, CMP])
        blkh, blkl = sb("blkh", [P, 32 * CMPW + WINDOW - CMPW], F32R), sb("blkl", [P, 32 * CMPW + WINDOW - CMPW], F32R)
        hkh, hkl = sb("hkh", [P, 2, CMPW], F32R), sb("hkl", [P, 2, CMPW], F32R)
        hvh, hvl = sb("hvh", [P, 2, NH, 32], F32R), sb("hvl", [P, 2, NH, 32], F32R)
        kcmp, vcmp = sb("kcmp", [P, 2 * CMPW]), sb("vcmp", [P, HD])
        pc = sb("pc", [P, TT, NH, 32])
        pcT = sb("pcT", [P, S])
        cstat = sb("cstat", [P, 3, 8])
        pS = sb("pS", [P, 2, 512])
        pT = sb("pT", [P, 2, 512])
        stat = sb("stat", [P, 2, 4, 2])
        gl, gth = sb("gl", [P, TT, 16]), sb("gth", [P, TT, 12])
        gt = sb("gt", [P, TT, 12])
        fx = sb("fx", [P, 5, TT, 4])
        ls8 = sb("ls8", [P, TT, 8])
        vbias = sb("vbias", [P, 640])
        trig = sb("trig", [P, S])
        csq = sb("csq", [P, S])
        rows = sb("rows", [P, 3, P])
        const = sb("const", [P, NCONST])
        cur = sb("cur", [P, NCOLS])
        ones = sb("ones", [P, P])
        bst, mv = sb("bst", [P, TT, 2, 6]), sb("mv", [P, TT, 2])
        vare, rstd, nmr = sb("vare", [P, TT]), sb("rstd", [P, TT]), sb("nmr", [P, TT])
        mhalf, eps_rms, fence = sb("mhalf", [P, 1]), sb("eps_rms", [P, 1]), sb("fence", [P, 1])
        ps = ctx.enter_context(nc.psum_tensor("ps", [P, 8, 512], F32))

        cqf, sq, rms = gates[:, 0:3, :], gates[:, 3:6, :], gates[:, 6:8, :]
        krt, krs = gates[:, 8, :], gates[:, 9, :]
        vsT = gates[:, 14, :]
        decay = gates[0:8, 15, :]
        hT = gates[:, 14, 0:2 * CMPW].rearrange("p (k c) -> p k c", k=2)
        hx, hu = gates[0:CMPW, 10:12, :], gates[0:CMPW, 12:14, :]
        stage = gates[:, 8:16, :].rearrange("p a s -> p (a s)").rearrange("p (t d) -> p t d", t=TT)
        cs, angle = trig[0:64, :], trig[64:128, :]
        posi = gates[64:128, 4, :].bitcast(I32)
        tf, an, kn = (gates[64:128, i, :] for i in (5, 6, 7))
        hs, hf = z[:, 0:2, :], z[:, 2:4, :]
        lq, rk = z[0:8, 0:4, :], z[0:8, 4:8, :]
        xq, xk, xv = qA, kA, vA

        ident_in, x_in, mem_in, const_in, rows_in, pos_in = (sem(n) for n in (
            "ident_in", "x_in", "mem_in", "const_in", "rows_in", "pos_in"))
        memT_ready = sem("memT_ready")
        raw_in = [sem(f"raw_in{i}") for i in range(RAW_SLOTS)]
        pair_in = sem("pair_in")
        hi_done, lo_done = sem("hi_done"), sem("lo_done")
        units_used = sem("units_used")
        pa_ready, pa_out = sem("pa_ready"), sem("pa_out")
        pd_ready, pd_out = sem("pd_ready"), sem("pd_out")
        cols_ready, cols_psum = sem("cols_ready"), sem("cols_psum")
        trig_done, setup_done = sem("trig_done"), sem("setup_done")
        acc_ready, stat_done, rstd_done = sem("acc_ready"), sem("stat_done"), sem("rstd_done")
        nm_done, xn_done = sem("nm_done"), sem("xn_done")
        tp_ready, xf_done, xT_ready = sem("tp_ready"), sem("xf_done"), sem("xT_ready")
        x_mul, x_done = sem("x_mul"), sem("x_done")
        gb_in, vb_in, out_done = sem("gb_in"), sem("vb_in"), sem("out_done")
        silu_done, gu_out, hT_ready = sem("silu_done"), sem("gu_out"), sem("hT_ready")
        sq_done, cqn_ready = sem("sq_done"), sem("cqn_ready")
        kr_shift, kr_added, kr_sum = sem("kr_shift"), sem("kr_added"), sem("kr_sum")
        gth_done, fx_abs, fx_exp, fx_ln, ls_ready = (sem("gth_done"), sem("fx_abs"), sem("fx_exp"), sem("fx_ln"),
                                                     sem("ls_ready"))
        blk_ready, hu_done, hg_done, hid_ready, gelu_done = (sem(n) for n in ("blk_ready", "hu_done", "hg_done",
                                                                             "hid_ready", "gelu_done"))
        s_ready, s_out, s_max = sem("s_ready"), sem("s_out"), sem("s_max")
        p_exp, p_ready = sem("p_exp"), sem("p_ready")
        pt_ready, pt_out, pv_done = sem("pt_ready"), sem("pt_out"), sem("pv_done")
        o_hi, o_out = sem("o_hi"), sem("o_out")
        zh_done, z_ready, y_out = sem("zh_done"), sem("z_ready"), sem("y_out")
        xk_out, xv_out, xq_out = sem("xk_out"), sem("xv_out"), sem("xq_out")
        xs_ready, xmax, xexp, xp_ready = sem("xs_ready"), sem("xmax"), sem("xexp"), sem("xp_ready")
        xpt_ready, xpt_out, xo_ready, xo_hi, xo_out = (sem("xpt_ready"), sem("xpt_out"), sem("xo_ready"),
                                                       sem("xo_hi"), sem("xo_out"))
        credits_set, sin_done = sem("credits_set"), sem("sin_done")

        ident = const[:, C_ID:C_ID + P]

        def bias_table(kind, h, q):
            if kind in "dc":
                at = C_CAUSAL
            else:
                at = C_ALIBI + 256 * (2 * h + (kind != "a"))
            return const[:, at + P:at + 2 * P] if q == 0 else const[:, at:at + 2 * P]

        def col(i):
            return cur[:, i:i + 1]

        def k_rows(w):
            return w.rearrange("(kt p) n -> p kt n", p=P)

        def by_row_tiles(w, l):
            return w.rearrange("l (kt p) n -> (l kt) p n", p=P)[bass.ds(l * KT, KT)].rearrange("kt p n -> p kt n")

        def ffn_source(w_in, w_out, l, what, f):
            if what == "g" and isinstance(f, int) and f == 0:
                return by_row_tiles(w_in, l)[:, :, 0:P]
            if what == "out" and isinstance(f, int) and f == 0:
                return w_out.rearrange("l (f p) n -> (l f) p n", p=P)[l * FT]
            if what == "out":
                return w_out[l].rearrange("(f p) n -> f p n", p=P)[f]
            return k_rows(w_in[l]).rearrange("p kt (c f j) -> c f p kt j", c=2, f=FT)[0 if what == "g" else 1][f]

        def mixer_source(unit, l):
            kind, x = unit[0], unit[1] if len(unit) > 1 else 0
            w_in = k_rows(a["w_in"][l])
            if kind == "col" and x == 0:
                return by_row_tiles(a["w_in"], l)[:, :, 0:P]
            if kind == "col":
                return w_in[:, :, x:x + P]
            if kind == "half":
                return w_in[:, 4 * unit[2]:4 * unit[2] + 4, x:x + 256]
            if kind == "pair":
                return w_in[:, :, x:x + 256].rearrange("p kt (c j) -> p kt c j", c=2)[:, :, :, 0:HD]
            if kind == "uq":
                return k_rows(a["mla_w_uq"][l])[:, :, 192 * x:192 * x + 192]
            if kind == "ukv":
                return a["mla_w_ukv"][l]
            if kind == "w1":
                return a["nsa_cmp_w1"][l][x].rearrange("(c lp p) n -> c p lp n", c=4, p=P)[unit[2]]
            if kind == "w2":
                return k_rows(a["nsa_cmp_w2"][l][x])
            if kind == "gate":
                at = G_M + BRANCHES[x] * D + unit[2] * P
                return w_in[:, :, at:at + P]
            if kind == "branch":
                w = k_rows(a["w_branch"][l][BRANCHES[x]])
                return w[:, :, 512 * unit[2]:512 * unit[2] + 512]
            if kind == "wo":
                return a["w_o"][l].rearrange("(k p) n -> k p n", p=P)[x]
            if kind == "xk":
                return k_rows(a["xa_w_kv"][l])[:, :, P * x:P * x + P]
            if kind == "xv":
                return k_rows(a["xa_w_kv"][l])[:, 4 * x:4 * x + 4, 256:512]
            if kind == "xq":
                return k_rows(a["xa_w_q"][l])[:, :, P * x:P * x + P]
            return a["xa_w_o"][l].rearrange("(k p) n -> k p n", p=P)[x]

        def raw_view(unit, slot):
            r = raw[:, slot, :]
            kind = unit[0]
            if kind in ("col", "gate", "xk", "xq"):
                return r.rearrange("p (kt n) -> p kt n", kt=KT)
            if kind in ("half", "xv"):
                return r.rearrange("p (kt n) -> p kt n", kt=4)
            if kind == "kr":
                return r[:, 0:KT * 48].rearrange("p (kt n) -> p kt n", kt=KT)
            if kind == "pair":
                return r.rearrange("p (kt c j) -> p kt c j", kt=KT, c=2)
            if kind == "uq":
                return r[:, 0:384].rearrange("p (kt n) -> p kt n", kt=2)
            if kind == "ukv":
                return r[:, 0:512]
            if kind == "w1":
                return r.rearrange("p (lp n) -> p lp n", lp=4)
            if kind == "w2":
                return r[:, 0:128].rearrange("p (kt n) -> p kt n", kt=2)
            if kind == "branch":
                return r.rearrange("p (kt n) -> p kt n", kt=2)
            return r

        def split_views(unit, rslot, w):
            r = raw[:, rslot, :]
            kind = unit[0]
            if kind == "kr":
                s_, d_ = raw_view(unit, rslot), w.rearrange("p (kt n) -> p kt n", kt=KT)
                return [(s_[:, :, 0:32], d_[:, :, 0:32]), (s_[:, :, 16:32], d_[:, :, 32:48]),
                        (s_[:, :, 0:16], d_[:, :, 48:64]), (s_[:, :, 32:48], d_[:, :, 64:80]),
                        (s_[:, :, 0:48], d_[:, :, 80:128])]
            if kind == "uq":
                s_ = r[:, 0:384].rearrange("p (kh n) -> p kh n", n=96)
                d_ = w[:, 0:512].rearrange("p (kh n) -> p kh n", n=P)
                return [(s_, d_[:, :, 0:96]), (s_[:, :, 80:96], d_[:, :, 96:112]), (s_[:, :, 64:80], d_[:, :, 112:128])]
            if kind == "ukv":
                s_ = r[:, 0:512].rearrange("p (h c n) -> p c h n", h=NH, c=2)
                return [(s_, w[:, 0:512].rearrange("p (c h n) -> p c h n", h=NH, c=2))]
            if kind == "w2":
                s_ = raw_view(unit, rslot)
                d_ = w[:, 0:256].rearrange("p (kt n) -> p kt n", kt=2)
                return [(s_, d_[:, :, 0:HD]), (s_, d_[:, :, HD:P])]
            return [(r, w)]

        PLAIN = ("ffn",)

        def unit_at(j):
            return MIXER[j - MIX0] if MIX0 <= j < FFN2_0 else PLAIN

        def hidden_slot(f):
            return 3 if f == FT - 1 else f % 2

        def units_before(l, j, more=0):
            return l * UNITS + more * 6 + j

        def raw_fills(l, j, more=0):
            return l * (UNITS // RAW_SLOTS) + more * 2 + j // RAW_SLOTS + 1

        def at(l, per_layer, n):
            return l * per_layer + n

        def unit_done(l, j, more=0):
            return units_before(l, j, more) + 1 + WT_SLOTS

        def signal(name):
            return units_used if name in ENDS_UNIT else pa_ready if name in PA else pd_ready

        def ready(l, name):
            if name in ENDS_UNIT:
                return units_used, unit_done(l, MIX0 + ENDS_UNIT[name])
            own = PA_MID if name in PA else PD_MID
            return (pa_ready if name in PA else pd_ready), at(l, len(own), own.index(name) + 1)

        def free(l, name):
            own = PA if name in PA else PD
            return (pa_out if name in PA else pd_out), at(l, len(own), own.index(name) + 1)

        def evacuated(l, name):
            own = PA if name in PA else PD
            return (pa_out if name in PA else pd_out), at(l, len(own), own.index(name) + 3)

        N_ROWS_DMAS = L * 15 + 5

        def load_rows(q):
            for l in range(L):
                b = a["b_in"][l]

                def bias_rows(r0, at_, n):
                    q.dma_start(rows[l * NB + r0:l * NB + r0 + n, 0, :],
                                 b[at_:at_ + n * P].rearrange("(r c) -> r c", c=P)).then_inc(rows_in, 16)

                def bias_part(r0, c0, at_, n):
                    q.dma_start(rows[l * NB + r0:l * NB + r0 + 1, 0, c0:c0 + n],
                                 b[at_:at_ + n].unsqueeze(0)).then_inc(rows_in, 16)
                bias_rows(BIAS["dcq0"], D_CQ, 3)
                for c0, at_, n in ((0, D_KR, 32), (32, D_KR + 16, 16), (48, D_KR, 16), (64, B_G, 12), (76, C_F, 4),
                                   (80, D_KR, 32), (112, D_KR, 16)):
                    bias_part(BIAS["kr"], c0, at_, n)
                bias_rows(BIAS["kc"], B_KC, 1)
                bias_part(BIAS["ks"], 0, B_KS, HD)
                bias_part(BIAS["ks"], HD, B_KW, HD)
                bias_rows(BIAS["bq0"], B_Q, 2)
                bias_rows(BIAS["cq0"], C_Q, 4)
                bias_rows(BIAS["aq0"], A_Q, 4)
                bias_rows(GB0, G_M, 32)
            q.dma_start(rows[0:64, 1, :], a["ln_g"].rearrange("l s (k c) -> (l s k) c", c=P)).then_inc(rows_in, 16)
            q.dma_start(rows[64:128, 1, :], a["ln_b"].rearrange("l s (k c) -> (l s k) c", c=P)).then_inc(rows_in, 16)
            q.dma_start(rows[0:64, 2, :], a["nsa_cmp_pos"].rearrange("l b (r two) c -> (l b r) (two c)", two=2))\
                .then_inc(rows_in, 16)
            q.dma_start(rows[64:68, 2, :], a["mla_q_norm"].rearrange("l (k c) -> (l k) c", c=P)).then_inc(rows_in, 16)
            q.dma_start(rows[68:70, 2, :], a["mla_kv_norm"]).then_inc(rows_in, 16)

        block = ctx.enter_context(nc.Block())

        @block.sync
        def _(sp):
            sp.dma_start(const[:, 0:P], a["const"][:, 0:P]).then_inc(ident_in, 16)
            def load(src, dst, l, j, more=0):
                sp.wait_ge(lo_done, units_before(l, j, more) + 1)
                sp.dma_start(dst, src).then_inc(raw_in[j % RAW_SLOTS], 16)

            def load_ffn(l, j, w_in, w_out, what, f, more=0):
                dst = raw[:, j % RAW_SLOTS, :]
                if what != "out":
                    dst = dst.rearrange("p (kt n) -> p kt n", kt=KT)
                load(ffn_source(w_in, w_out, l, what, f), dst, l, j, more)

            FIRST = (("g", 0), ("u", 0), ("g", 1), ("u", 1), ("out", 0))

            def first_units(l_from, j0, w_in, w_out, l):
                for n, (what, f) in enumerate(FIRST):
                    dst = raw[:, (j0 + n) % RAW_SLOTS, :]
                    if what != "out":
                        dst = dst.rearrange("p (kt n) -> p kt n", kt=KT)
                    load(ffn_source(w_in, w_out, l_from, what, f), dst, l, j0 + n)

            def ffn(l, j0, w_in, w_out):
                with sp.Fori(0, FT // 2 - 2) as i:
                    for n, (what, f) in enumerate((("g", 2), ("u", 2), ("out", 1), ("g", 3), ("u", 3), ("out", 2))):
                        load_ffn(l, j0 + 5 + n, w_in, w_out, what, i * 2 + f, i)
                for n, (what, f) in enumerate((("g", FT - 2), ("u", FT - 2), ("g", FT - 1), ("u", FT - 1),
                                               ("out", FT - 3), ("out", FT - 2), ("out", FT - 1))):
                    load_ffn(l, j0 + FFN_UNITS - 7 + n, w_in, w_out, what, f)

            for n, (what, f) in enumerate(FIRST):
                if n == 1:
                    sp.dma_start(xb[:, :, :], a["x"][0].rearrange("(t p) d -> p t d", p=P)).then_inc(x_in, 16)
                if n == 3:
                    sp.dma_start(stage, a["mem"][0].rearrange("(t p) d -> p t d", p=P)).then_inc(mem_in, 16)
                load_ffn(0, n, a["ffn1_w_in"], a["ffn1_w_out"], what, f)
            with sp.Fori(0, L) as l:
                ffn(l, 0, a["ffn1_w_in"], a["ffn1_w_out"])
                for n, unit in enumerate(MIXER):
                    j = MIX0 + n
                    dst = raw_view(unit, j % RAW_SLOTS)
                    if unit[0] == "kr":
                        w_in = k_rows(a["w_in"][l])
                        sp.wait_ge(lo_done, units_before(l, j) + 1)
                        sp.dma_start(dst[:, :, 0:32], w_in[:, :, D_KR:D_KR + 32]).then_inc(pair_in, 16)
                        sp.dma_start(dst[:, :, 32:44], w_in[:, :, B_G:B_G + 12]).then_inc(pair_in, 16)
                        load(w_in[:, :, C_F:C_F + 4], dst[:, :, 44:48], l, j)
                        continue
                    src = mixer_source(unit, l)
                    if unit[0] == "pair":
                        sp.wait_ge(lo_done, units_before(l, j) + 1)
                        sp.dma_start(dst[:, :, 0, :], src[:, :, 0, :]).then_inc(pair_in, 16)
                        src, dst = src[:, :, 1, :], dst[:, :, 1, :]
                    load(src, dst, l, j)
                first_units(l, FFN2_0, a["ffn2_w_in"], a["ffn2_w_out"], l)
                ffn(l, FFN2_0, a["ffn2_w_in"], a["ffn2_w_out"])
                first_units((l + 1) % L, UNITS, a["ffn1_w_in"], a["ffn1_w_out"], l)
            for t in range(TT):
                sp.wait_ge(x_done, L * 4 * TT + t + 1)
                sp.dma_start(out[0].rearrange("(t p) d -> t p d", p=P)[t], xb[:, t, :]).then_inc(out_done, 16)
            sp.wait_ge(out_done, TT * 16)

        @block.gpsimd
        def _(pool):
            pool.memset(mhalf[:, :], -0.5)
            pool.memset(ones[:, :], 1.0)
            pool.memset(csq[0:64, :], 1.0)
            pool.memset(kcmp[:, :], 0.0)
            pool.memset(blkh[:, :].bitcast(F32), 0.0)
            pool.memset(blkl[:, :].bitcast(F32), 0.0)
            pool.memset(hvh[:, :, :, :].bitcast(F32), 0.0)
            pool.memset(hvl[:, :, :, :].bitcast(F32), 0.0)
            pool.memset(pc[:, :, :, :], 0.0).then_inc(setup_done, 1)
            pool.wait_ge(setup_done, 1)

            pool.dma_start(posi, a["positions"].broadcast_to([64, S])).then_inc(pos_in, 16)
            pool.dma_start(const[:, P:NCONST], a["const"][:, P:NCONST]).then_inc(const_in, 16)
            load_rows(pool)
            pool.wait_ge(pos_in, 16)
            pool.wait_ge(const_in, 16)
            pool.tensor_copy(tf, posi)
            pool.drain()
            low = const[64:128, :]
            pool.tensor_scalar(an, tf, low[:, C_INV:C_INV + 1], None, ALU.mult)
            pool.drain()
            pool.tensor_scalar(kn, an, 1.0 / TWO_PI, low[:, C_OFF:C_OFF + 1], ALU.mult, ALU.add)
            pool.drain()
            pool.tensor_scalar(kn, kn, ROUND, None, ALU.add)
            pool.drain()
            pool.tensor_scalar(kn, kn, ROUND, None, ALU.subtract)
            pool.drain()
            for c in (PI_1, PI_2, PI_3):
                pool.tensor_scalar(tf, kn, c, None, ALU.mult)
                pool.drain()
                pool.tensor_tensor(an, an, tf, ALU.subtract)
                pool.drain()
            pool.tensor_scalar(an, an, low[:, C_PHASE:C_PHASE + 1], 3.1415925, ALU.add, ALU.min)
            pool.drain()
            pool.tensor_scalar(angle, an, -3.1415925, None, ALU.max).then_inc(trig_done, 1)
            pool.drain()

            def norm(l, s):
                pool.wait_ge(x_done, at(l, 4 * TT, TT * s + TT))
                pool.dma_start(gb[:, 0, :], a["ln_g"][l][s:s + 1, :].broadcast_to([P, D])).then_inc(gb_in, 16)
                pool.dma_start(gb[:, 1, :], a["ln_b"][l][s:s + 1, :].broadcast_to([P, D])).then_inc(gb_in, 16)
                for t in range(TT):
                    pool.wait_ge(stat_done, at(l, 4 * TT, TT * s + t + 1))
                    pool.tensor_tensor(rstd[:, t:t + 1], vare[:, t:t + 1], mhalf[:, :], ALU.pow).then_inc(rstd_done, 1)
                pool.wait_ge(gb_in, at(l, 4 * 32, 32 * s + 32))
                for t in range(TT):
                    pool.wait_ge(tp_ready, at(l, 16, 8 + 4 * s + 2 * t + 2))
                    pool.tensor_tensor(xb[:, t, :], xb[:, t, :], gb[:, 0, :], ALU.mult).then_inc(x_mul, 1)
                    pool.wait_ge(x_mul, at(l, 4 * TT, TT * s + t + 1))
                    pool.tensor_tensor(xb[:, t, :], xb[:, t, :], gb[:, 1, :], ALU.add).then_inc(x_done, 1)

            with pool.Fori(0, L) as l:
                bl = a["b_in"][l].unsqueeze(0)
                for to, frm, n in ((0, A_V, 256), (256, B_VS, HD), (320, B_VW, HD), (384, C_V, 256)):
                    pool.dma_start(vbias[:, to:to + n], bl[:, frm:frm + n].broadcast_to([P, n])).then_inc(vb_in, 16)
                for s in range(4):
                    norm(l, s)

        def turned(t, k):
            return ps[:, (6, 2)[t] + k // 4, P * (k % 4):P * (k % 4) + P]

        def turned_bank(t, half):
            return ps[:, (6, 2)[t] + half, :].rearrange("p (k n) -> p k n", k=4)

        def pa_tile(name):
            return ps[:, PA.index(name) % 2, :]

        def pd_tile(name):
            return ps[:, 2 + PD.index(name) % 2, :]

        S_BANK = ps[:, 4, :]

        def hidden_bank(br):
            return ps[:, 4 + br, 0:S]

        PT_BANK = ps[:, 5, :]

        def o_bank(pair):
            return ps[:, 6 + pair % 2, 0:S]

        def value_tile(kind, h, t):
            if kind == "s":
                return vB[:, t, 0:HD]
            if kind == "w":
                return vB[:, t, HD:2 * HD]
            v = {"d": vD, "c": vC, "a": vA}[kind]
            return v[:, t, HD * h:HD * h + HD]

        @block.tensor
        def _(pe):
            def mm3(o, lh, ll, rh, rl, first, last):
                pe.matmul(o, lh, rh, start=first, stop=False)
                pe.matmul(o, lh, rl, start=False, stop=False)
                return pe.matmul(o, ll, rh, start=False, stop=last)

            def transpose_tile(l, t, src, sub=None):
                if sub is not None:
                    pe.wait_ge(xn_done, at(l, 4 * TT, TT * sub + t + 1))
                for k in range(KT):
                    last = pe.transpose(turned(t, k), src[:, t, P * k:P * k + P], ident)
                    if k % 4 == 3:
                        last.then_inc(tp_ready, 1)

            def transpose_in(l, src, sub=None):
                for t in range(TT):
                    transpose_tile(l, t, src, sub)

            def take(l, j, more=0):
                pe.wait_ge(lo_done, units_before(l, j, more) + RAW_SLOTS + 1)
                s_ = j % WT_SLOTS
                return wh[:, s_, :], wl[:, s_, :]

            pe.sem_inc(units_used, WT_SLOTS)
            pe.wait_ge(ident_in, 16)
            pe.wait_ge(x_in, 16)
            transpose_in(0, xb)
            pe.wait_ge(mem_in, 16)
            pe.wait_ge(xT_ready, KT // 2)
            transpose_in(0, stage)

            def feature_tile(o, h_, l_, l, ln=None):
                hv, lv = (w.rearrange("p (kt n) -> p kt n", kt=KT) for w in (h_, l_))
                for k in range(KT):
                    if ln is not None and k % 2 == 0:
                        pe.wait_ge(xT_ready, at(l, 16, 4 * ln + k // 2 + 1))
                    last = mm3(o, hv[:, k, :], lv[:, k, :], xTh[:, k, :], xTl[:, k, :], k == 0, k == KT - 1)
                return last

            def half_units(l, j, o, xh=xTh, xl=xTl, between=None):
                parts = [[w.rearrange("p (kt n) -> p kt n", kt=4) for w in take(l, j + i)] for i in range(2)]
                for t in range(TT):
                    if t and between:
                        between()
                    for k in range(KT):
                        hv, lv = parts[k // 4]
                        last = mm3(o[:, S * t:S * t + S], xh[:, k, P * t:P * t + P], xl[:, k, P * t:P * t + P],
                                   hv[:, k % 4, :], lv[:, k % 4, :], k == 0, k == KT - 1)
                        if t == TT - 1 and k == 3:
                            last.then_inc(units_used, 1)
                return last

            def ffn(l, which, j0, ln):
                def hidden(f, j, more=0, ln_=None):
                    h_, l_ = take(l, j, more)
                    pe.wait_ge(gu_out, at(l, 2 * FT, FT * which + f + 1) + more * 2)
                    feature_tile(ps[:, 4 + f % 2, 0:S], h_, l_, l, ln_).then_inc(units_used, 1)
                    h_, l_ = take(l, j + 1, more)
                    feature_tile(ps[:, 4 + f % 2, S:2 * S], h_, l_, l).then_inc(units_used, 1)

                def down_half(f, t, h_, l_):
                    th, tl = (w[:, hidden_slot(f), P * t:P * t + P] for w in (oTh, oTl))
                    for c in range(2):
                        w = slice(512 * c, 512 * c + 512)
                        last = mm3(ps[:, 2 * t + c, :], th, tl, h_[:, w], l_[:, w], f == 0, f == FT - 1)
                    return last

                def down(f, j, more=0):
                    h_, l_ = take(l, j, more)
                    pe.wait_ge(hT_ready, at(l, 2 * FT, FT * which + f + 1) + more * 2)
                    down_half(f, 0, h_, l_)
                    down_half(f, 1, h_, l_).then_inc(units_used, 1)

                def last_downs(j):
                    parts = [take(l, j + i) for i in range(3)]
                    for i in range(3):
                        pe.wait_ge(hT_ready, at(l, 2 * FT, FT * which + FT - 2 + i))
                        last = down_half(FT - 3 + i, 0, *parts[i])
                    last.then_inc(acc_ready, 1)
                    for i in range(3):
                        down_half(FT - 3 + i, 1, *parts[i]).then_inc(units_used, 1)

                hidden(0, j0, ln_=ln)
                hidden(1, j0 + 2)
                pe.wait_ge(memT_ready, KT // 2)
                down(0, j0 + 4)
                with pe.Fori(0, FT // 2 - 2) as i:
                    hidden(2, j0 + 5, i)
                    down(1, j0 + 7, i)
                    hidden(3, j0 + 8, i)
                    down(2, j0 + 10, i)
                j = j0 + FFN_UNITS - 7
                hidden(FT - 2, j)
                if which == 0:
                    pe.wait_ge(rows_in, 16 * N_ROWS_DMAS)
                    for i, (n, at_) in enumerate(((96, 0), (128, 96), (70, 224))):
                        last = pe.transpose(ps[:, 7, at_:at_ + n], rows[0:n, i, :], ident[0:n, 0:n])
                    last.then_inc(cols_psum, 1)
                hidden(FT - 1, j + 2)
                last_downs(j + 4)

            def scores(l, n):
                b, h, kind = HEADS[n]
                pe.wait_ge(s_out, at(l, NSLOT, n + 1))
                o = S_BANK
                if kind == "cmp":
                    for q in range(TT):
                        for hh in (0, 2):
                            i = (q * NH + hh) * CMPW
                            last = pe.matmul(o[:, i:i + 2 * CMPW], qB[:, hh // 2, P * q:P * q + P], kcmp[:, :],
                                             start=True, stop=True)
                    last.then_inc(s_ready, 1)
                    return
                for q in range(TT):
                    ob = o[:, 0:P] if q == 0 else o[:, P:3 * P]
                    nk = P * (q + 1)
                    if kind == "d":
                        last = pe.matmul(ob, qD[:, h, P * q:P * q + P], kD[:, h, 0:nk], start=True, stop=True)
                        continue
                    r = slice(64 * (h % 2), 64 * (h % 2) + 64)
                    qq = {"c": qC, "a": qA}.get(kind, qB)[r, h // 2, P * q:P * q + P]
                    if kind in "sw":
                        kk = kB[r, 0 if kind == "s" else 1, 0:nk]
                    else:
                        kk = (kC if kind == "c" else kA)[r, h // 2, 0:nk]
                    last = pe.matmul(ob, qq, kk, start=True, stop=(kind != "c"))
                    if kind == "c":
                        last = pe.matmul(ob, lq[:, h, P * q:P * q + P], rk[:, h, 0:nk], start=False, stop=True)
                last.then_inc(s_ready, 1)

            def turn(l, n):
                pe.wait_ge(p_ready, at(l, NSLOT, n + 1))
                pe.wait_ge(pt_out, at(l, NSLOT, n + 1))
                for i in range(2 if HEADS[n][2] == "cmp" else 3):
                    src = (pc[:, i, :, :].rearrange("p h c -> p (h c)") if HEADS[n][2] == "cmp"
                           else pS[:, n % 2, P * i:P * i + P])
                    last = pe.transpose(PT_BANK[:, P * i:P * i + P], src, ident)
                last.then_inc(pt_ready, 1)

            def cmp_values(h):
                r = slice(32 * h, 32 * h + CMPW)
                return pe.matmul(o_bank(6 + h // 2)[64 * (h % 2):64 * (h % 2) + 64, :], vcmp[r, :], pcT[r, :],
                                 start=True, stop=False)

            def values(l, n):
                b, h, kind = HEADS[n]
                pair = 2 * b + h // 2
                pe.wait_ge(pt_out, at(l, NSLOT, n + 2))
                if kind == "cmp":
                    pe.wait_ge(o_out, at(l, PAIRS, 6 + 1))
                    cmp_values(0)
                    cmp_values(1).then_inc(pv_done, 1)
                    return
                if kind == "s" and h == 2:
                    pe.wait_ge(o_out, at(l, PAIRS, 7 + 1))
                    cmp_values(2)
                    cmp_values(3)
                if kind in "dca" and h % 2 == 0:
                    pe.wait_ge(o_out, at(l, PAIRS, pair + 1))
                o = o_bank(pair)[64 * (h % 2):64 * (h % 2) + 64, :]
                pe.matmul(o, value_tile(kind, h, 0), pT[:, n % 2, 0:S], start=kind in "dca", stop=False)
                last = pe.matmul(o[:, P:S], value_tile(kind, h, 1), pT[:, n % 2, S:S + P], start=False,
                                 stop=kind != "s")
                last.then_inc(pv_done, 1)

            def project(l):
                for n in range(NPROJ):
                    if n in (U_CV, U_AV):
                        name = "cv" if n == U_CV else "av"
                        pe.wait_ge(*free(l, name))
                        half_units(l, MIX0 + n, pd_tile(name)).then_inc(signal(name), 1)
                    elif n not in (U_CV + 1, U_AV + 1):
                        h_, l_ = take(l, MIX0 + n)
                    if n in MAIN_PA:
                        name = MAIN_PA[n]
                        pe.wait_ge(*free(l, name))
                        feature_tile(pa_tile(name)[:, 0:S], h_, l_, l, 1 if n == 0 else None).then_inc(signal(name), 1)
                    elif n == U_KR:
                        pe.wait_ge(*free(l, "kr"))
                        feature_tile(pd_tile("kr")[:, 0:S], h_, l_, l).then_inc(signal("kr"), 1)
                    elif n == U_VS:
                        pe.wait_ge(*free(l, "vs"))
                        feature_tile(pd_tile("vs")[:, 0:S], h_, l_, l).then_inc(signal("vs"), 1)
                    elif n in (U_UQ0, U_UQ1):
                        if n == U_UQ0:
                            pe.wait_ge(cqn_ready, at(l, 1, 1))
                        for h in range(2):
                            name = f"q{2 * (n == U_UQ1) + h}"
                            pe.wait_ge(*free(l, name))
                            for k in range(2):
                                c0 = 256 * k + P * h
                                last = mm3(pd_tile(name)[:, 0:S], h_[:, c0:c0 + P], l_[:, c0:c0 + P],
                                           oTh[:, k, :], oTl[:, k, :], k == 0, k == 1)
                            last.then_inc(signal(name), 1)
                    elif n == U_UKV:
                        for i in range(2):
                            pe.wait_ge(*free(l, f"kn{i}"))
                            mm3(pa_tile(f"kn{i}")[:, 0:S], h_[:, P * i:P * i + P], l_[:, P * i:P * i + P],
                                oTh[:, 2, :], oTl[:, 2, :], True, True).then_inc(signal(f"kn{i}"), 1)
                        for t in range(TT):
                            pe.wait_ge(*free(l, f"vd{t}"))
                            mm3(pd_tile(f"vd{t}")[:, 0:S], oTh[:, 2, P * t:P * t + P], oTl[:, 2, P * t:P * t + P],
                                h_[:, 256:512], l_[:, 256:512], True, True).then_inc(signal(f"vd{t}"), 1)
                    elif PROJ[n][0] == "w1":
                        _, br, c = PROJ[n]
                        if (br, c) == (0, 0):
                            pe.wait_ge(blk_ready, at(l, 1, 1))
                        wvh, wvl = (w.rearrange("p (lp n) -> p lp n", lp=4) for w in (h_, l_))
                        for lp in range(4):
                            b0 = (16 * br + 4 * c + lp) * CMPW
                            last = mm3(hidden_bank(br)[0:WINDOW, :], blkh[:, b0:b0 + WINDOW], blkl[:, b0:b0 + WINDOW],
                                       wvh[:, lp, :], wvl[:, lp, :], c == 0 and lp == 0, c == 3 and lp == 3)
                        last.then_inc(units_used, 1)
                    if n == 5:
                        pe.wait_ge(*evacuated(l, "kr"))
                        pe.wait_ge(*free(l, "gf"))
                        for t in range(TT):
                            last = pe.matmul(pd_tile("gf")[:, 16 * t:16 * t + 16], krt[64:80, P * t:P * t + P],
                                             ident[64:80, 64:80], start=True, stop=True)
                        last.then_inc(signal("gf"), 1)
                    if n == U_VS + 2:
                        pe.wait_ge(*evacuated(l, "vs"))
                        pe.wait_ge(*free(l, "vst"))
                        for t in range(TT):
                            last = pe.transpose(pd_tile("vst")[:, P * t:P * t + P], vsT[:, P * t:P * t + P], ident)
                        last.then_inc(signal("vst"), 1)
                    if n in U_TURN:
                        br = U_TURN.index(n)
                        pe.wait_ge(gelu_done, at(l, 2, br + 1))
                        pe.wait_ge(*free(l, f"turn{br}"))
                        for k in range(2):
                            last = pe.matmul(pd_tile(f"turn{br}")[:, CMPW * k:CMPW * k + CMPW],
                                             hx[:, br, P * k:P * k + P], ident[0:CMPW, 0:CMPW], start=True, stop=True)
                        last.then_inc(signal(f"turn{br}"), 1)
                    if n == 7:
                        pe.wait_ge(sq_done, at(l, 1, 1))
                        pe.wait_ge(*free(l, "ssq"))
                        o = pa_tile("ssq")
                        for k in range(2):
                            pe.matmul(o[:, 0:S], ones[:, :], sq[:, k, :], start=(k == 0), stop=(k == 1))
                        pe.matmul(o[:, S:2 * S], ones[:, :], sq[:, 2, :], start=True, stop=True)\
                            .then_inc(signal("ssq"), 1)
                    if n == U_DECAY:
                        pe.wait_ge(ls_ready, at(l, 1, 1))
                        pe.wait_ge(*free(l, "decay"))
                        o = pd_tile("decay")[0:8, 0:S]
                        tri = const[:, C_TRI:C_TRI + S]
                        pe.matmul(o, ls8[:, 0, :], tri, start=True, stop=False)
                        pe.matmul(o[:, P:S], ls8[:, 1, :], tri[:, 0:P], start=False, stop=True)\
                            .then_inc(signal("decay"), 1)

            def compressed(l, i, h_, l_):
                pe.wait_ge(hid_ready, at(l, 2, i + 1))
                wvh, wvl = (w[:, 0:256].rearrange("p (kt n) -> p kt n", kt=2) for w in (h_, l_))
                if i == 0:
                    pe.wait_ge(*free(l, "cmp"))
                for k in range(2):
                    if i == 0:
                        last = mm3(pa_tile("cmp")[:, 0:CMPW], wvh[:, k, :], wvl[:, k, :], hkh[:, k, :], hkl[:, k, :],
                                   k == 0, k == 1)
                    else:
                        last = mm3(pa_tile("cmp")[:, 64:128], hvh[:, k, :, :].rearrange("p h c -> p (h c)"),
                                   hvl[:, k, :, :].rearrange("p h c -> p (h c)"),
                                   wvh[:, k, 0:HD], wvl[:, k, 0:HD], k == 0, k == 1)
                last.then_inc(units_used, 1)

            def attend(l):
                pe.wait_ge(kr_sum, at(l, 2, 2))
                step = 0
                for n in range(NPROJ, U_WO):
                    h_, l_ = take(l, MIX0 + n)
                    if MIXER[n][0] == "w2":
                        compressed(l, MIXER[n][1], h_, l_)
                        continue
                    kind, b, i = MIXER[n]
                    if kind == "gate":
                        if step == 8:
                            pe.wait_ge(*evacuated(l, "cmp"))
                            pe.wait_ge(*evacuated(l, "av"))
                        if step < NSLOT:
                            scores(l, step)
                        name = f"gate{b}_{i}"
                        pe.wait_ge(*free(l, name))
                        hv, lv = (w.rearrange("p (kt n) -> p kt n", kt=KT) for w in (h_, l_))
                        for k in range(KT):
                            if k == KT // 2 and 1 <= step <= NSLOT:
                                turn(l, step - 1)
                            last = mm3(pa_tile(name)[:, 0:S], hv[:, k, :], lv[:, k, :], xTh[:, k, :], xTl[:, k, :],
                                       k == 0, k == KT - 1)
                        last.then_inc(signal(name), 1)
                        if 1 <= step <= NSLOT:
                            values(l, step - 1)
                        step += 1
                        continue
                    if i == 0:
                        pe.wait_ge(o_out, at(l, PAIRS, 2 * b + 2 + 2))
                    wvh, wvl = (w.rearrange("p (kt n) -> p kt n", kt=2) for w in (h_, l_))
                    for q in range(4):
                        name = f"y{b}_{4 * i + q}"
                        pe.wait_ge(*free(l, name))
                        for k in range(2):
                            s_ = 2 * (b % 2) + k
                            last = mm3(pd_tile(name)[:, 0:S], wvh[:, k, P * q:P * q + P], wvl[:, k, P * q:P * q + P],
                                       oTh[:, s_, :], oTl[:, s_, :], k == 0, k == 1)
                        last.then_inc(signal(name), 1)

            def merged_half(k, t, h_, l_):
                for c in range(2):
                    w = slice(512 * c, 512 * c + 512)
                    last = mm3(ps[:, 2 * t + c, :], xTh[:, k, P * t:P * t + P], xTl[:, k, P * t:P * t + P],
                               h_[:, w], l_[:, w], k == 0, k == KT - 1)
                return last

            def merged_out(l):
                pe.wait_ge(*evacuated(l, f"y3_{KT - 1}"))
                for k in range(KT - 3):
                    h_, l_ = take(l, MIX0 + U_WO + k)
                    pe.wait_ge(z_ready, at(l, KT, k + 1))
                    merged_half(k, 0, h_, l_)
                    merged_half(k, 1, h_, l_).then_inc(units_used, 1)
                tail = range(KT - 3, KT)
                parts = {k: take(l, MIX0 + U_WO + k) for k in tail}
                pe.wait_ge(z_ready, at(l, KT, KT))
                for k in tail:
                    last = merged_half(k, 0, *parts[k])
                last.then_inc(acc_ready, 1)
                for k in tail:
                    merged_half(k, 1, *parts[k]).then_inc(units_used, 1)

            def cross(l):
                j0 = MIX0 + U_X
                pe.wait_ge(memT_ready, KT // 2)
                for i in range(2):
                    h_, l_ = take(l, j0 + i)
                    hv, lv = (w.rearrange("p (kt n) -> p kt n", kt=KT) for w in (h_, l_))
                    for k in range(KT):
                        last = mm3(ps[:, 4, S * i:S * i + S], hv[:, k, :], lv[:, k, :], memTh[:, k, :], memTl[:, k, :],
                                   k == 0, k == KT - 1)
                    last.then_inc(units_used, 1)
                transpose_tile(l, 0, xb, 1)
                half_units(l, j0 + 2, ps[:, 5, :], memTh, memTl, lambda: transpose_tile(l, 1, xb, 1))\
                    .then_inc(units_used, 1)
                for i in range(2):
                    h_, l_ = take(l, j0 + 4 + i)
                    pe.wait_ge((xk_out, xv_out)[i], at(l, 1, 1))
                    feature_tile(ps[:, 4 + i, 0:S], h_, l_, l, 2 if i == 0 else None).then_inc(units_used, 1)
                for h in range(NH):
                    if h % 2 == 0:
                        pe.wait_ge(xq_out, at(l, 2, h // 2 + 1))
                    r = slice(64 * (h % 2), 64 * (h % 2) + 64)
                    for q in range(TT):
                        last = pe.matmul(ps[:, h, S * q:S * q + S], xq[r, h // 2, P * q:P * q + P], xk[r, h // 2, :],
                                         start=True, stop=True)
                    last.then_inc(xs_ready, 1)
                for h in range(NH + 1):
                    if h < NH:
                        pe.wait_ge(xp_ready, at(l, NH, h + 1))
                        if h >= 2:
                            pe.wait_ge(xpt_out, at(l, NH, h - 1))
                        bank = ps[:, 5 + h % 2, :]
                        for k in range(TT):
                            for q in range(TT):
                                last = pe.transpose(bank[:, S * k + P * q:S * k + P * q + P],
                                                    pS[:, h % 2, S * q + P * k:S * q + P * k + P], ident)
                        last.then_inc(xpt_ready, 1)
                    if h >= 1:
                        g = h - 1
                        pe.wait_ge(xpt_out, at(l, NH, g + 1))
                        o = ps[64 * (g % 2):64 * (g % 2) + 64, 7 if g < 2 else 4, 0:S]
                        for k in range(TT):
                            last = pe.matmul(o, xv[:, k, HD * g:HD * g + HD], pT[:, g % 2, S * k:S * k + S],
                                             start=(k == 0), stop=(k == TT - 1))
                        last.then_inc(xo_ready, 1)
                parts = [take(l, j0 + 6 + k) for k in range(2)]

                def out_half(k, t):
                    for c in range(2):
                        w = slice(512 * c, 512 * c + 512)
                        last = mm3(ps[:, 2 * t + c, :], oTh[:, k, P * t:P * t + P], oTl[:, k, P * t:P * t + P],
                                   parts[k][0][:, w], parts[k][1][:, w], k == 0, k == 1)
                    return last
                pe.wait_ge(xo_out, at(l, 2, 1))
                out_half(0, 0)
                pe.wait_ge(xo_out, at(l, 2, 2))
                out_half(1, 0).then_inc(acc_ready, 1)
                out_half(0, 1).then_inc(units_used, 1)
                out_half(1, 1).then_inc(units_used, 1)
                transpose_in(l, xb, 2)

            with pe.Fori(0, L) as l:
                ffn(l, 0, 0, 0)
                transpose_in(l, xb, 0)
                project(l)
                attend(l)
                merged_out(l)
                cross(l)
                ffn(l, 1, FFN2_0, 3)
                transpose_in(l, xb, 3)

        @block.scalar
        def _(act):
            def split_hi(l, j, more=0):
                act.wait_ge(raw_in[j % RAW_SLOTS], raw_fills(l, j, more) * 16)
                act.wait_ge(units_used, units_before(l, j, more) + 1)
                if unit_at(j)[0] == "pair":
                    act.wait_ge(pair_in, at(l, 64, 48 if unit_at(j)[1] == B_KS else 64))
                if unit_at(j)[0] == "kr":
                    act.wait_ge(pair_in, at(l, 64, 32))
                for src, dst in split_views(unit_at(j), j % RAW_SLOTS, wh[:, j % WT_SLOTS, :]):
                    last = act.activation(dst, src, ACT.Copy)
                last.then_inc(hi_done, 1)

            def ahead(l, j, more=0):
                split_hi(l, j + AHEAD, more)

            def normalise(l, s):
                act.wait_ge(nm_done, at(l, 4, s + 1))
                act.activation(xb[:, 0, :], xb[:, 0, :], ACT.Identity, bias=nmr[:, 0:1],
                               scale=rstd[:, 0:1]).then_inc(xn_done, 1)

            def evacuate(l, idx, s):
                for t in range(TT):
                    for k in range(KT):
                        if k % 4 == 0:
                            act.wait_ge(tp_ready, at(l, 16, 4 * idx + 2 * t + k // 4 + 1))
                        act.activation(z[:, k, P * t:P * t + P], turned(t, k), ACT.Identity, bias=col(LNB + 8 * s + k),
                                       scale=col(LNG + 8 * s + k)).then_inc(xf_done, 1)

            def turned_hi(idx, th):
                for i in range(4):
                    t, half = divmod(i, 2)
                    act.wait_ge(tp_ready, 4 * idx + i + 1)
                    act.activation(th[:, 4 * half:4 * half + 4, P * t:P * t + P], turned_bank(t, half), ACT.Copy)\
                        .then_inc(xf_done, 4)

            def silu(l, f, up, more=0):
                act.wait_ge(units_used, unit_done(l, up, more))
                act.activation(hs[:, f % 2, :], ps[:, 4 + f % 2, 0:256], ACT.Silu).then_inc(silu_done, 1)

            def ffn(l, j0):
                ahead(l, j0)
                ahead(l, j0 + 1)
                silu(l, 0, j0 + 1)
                for n in range(2, 5):
                    ahead(l, j0 + n)

                def turn(j, i=0):
                    ahead(l, j, i)
                    silu(l, 1, j - 2, i)
                    for n in range(1, 4):
                        ahead(l, j + n, i)
                    silu(l, 2, j + 1, i)
                    ahead(l, j + 4, i)
                    ahead(l, j + 5, i)
                with act.Fori(0, FT // 2 - 2) as i:
                    turn(j0 + 5, i)
                j = j0 + FFN_UNITS - 7
                silu(l, FT - 3, j - 2)
                ahead(l, j)
                ahead(l, j + 1)
                silu(l, FT - 2, j + 1)
                ahead(l, j + 2)
                ahead(l, j + 3)
                silu(l, FT - 1, j + 3)
                for n in range(4, 7):
                    ahead(l, j + n)

            def pa_wait(l, name):
                act.wait_ge(*ready(l, name))
                return pa_tile(name)

            def pa_main(l, name):
                src = pa_wait(l, name)[:, 0:S]
                bcol = col(BIAS[name])
                if name in ("dcq0", "dcq1", "dckv"):
                    i = ("dcq0", "dcq1", "dckv").index(name)
                    act.activation(cqf[:, i, :], src, ACT.Identity, bias=bcol).then_inc(pa_out, 1)
                elif name == "kc":
                    for i in range(2):
                        r = slice(64 * i, 64 * i + 64)
                        act.activation(x2[0:64, i, :], src[r, :], ACT.Identity, bias=bcol[r, :])
                        last = act.activation(x2[64:128, i, 0:S - 1], src[r, 1:S], ACT.Identity, bias=bcol[r, :])
                    last.then_inc(pa_out, 1)
                elif name == "ks":
                    for i in range(2):
                        r = slice(64 * i, 64 * i + 64)
                        act.activation(kB[0:64, i, :], src[r, :], ACT.Identity, bias=bcol[r, :])
                        last = act.activation(kB[64:128, i, :], src[r, :], ACT.Identity, bias=bcol[r, :])
                    last.then_inc(pa_out, 1)
                else:
                    dst = {"bq": qB, "cq": qC, "ck": kC, "aq": qA, "ak": kA}[name[:2]][:, int(name[2]), :]
                    act.activation(dst, src, ACT.Identity, bias=bcol).then_inc(pa_out, 1)

            def exp_head(l, n):
                if HEADS[n][2] == "cmp":
                    act.wait_ge(s_max, at(l, NSLOT, n + 1))
                    act.activation(pc[:, :, :, 0:CMPW], pc[:, :, :, 0:CMPW], ACT.Exp).then_inc(p_exp, 1)
                    return
                act.wait_ge(s_max, at(l, NSLOT, n + 1))
                i = n % 2
                act.activation(pS[:, i, 0:P], pS[:, i, 0:P], ACT.Exp, bias=stat[:, i, 1, 0:1], accum_out=stat[:, i, 2, 0:1])
                act.activation(pS[:, i, P:3 * P], pS[:, i, P:3 * P], ACT.Exp, bias=stat[:, i, 1, 1:2],
                               accum_out=stat[:, i, 2, 1:2]).then_inc(p_exp, 1)

            def copy_turned(l, n):
                act.wait_ge(pt_ready, at(l, NSLOT, n + 1))
                if HEADS[n][2] == "cmp":
                    act.activation(pcT[:, :], PT_BANK[:, 0:S], ACT.Copy).then_inc(pt_out, 1)
                    return
                if n >= 2:
                    act.wait_ge(pv_done, at(l, NSLOT, n - 1))
                act.activation(pT[:, n % 2, 0:3 * P], PT_BANK[:, 0:3 * P], ACT.Copy).then_inc(pt_out, 1)

            def pair_hi(l, pair):
                act.wait_ge(pv_done, at(l, NSLOT, PAIR_END[pair] + 1))
                s_ = pair % 4
                act.activation(oTh[:, s_, :], o_bank(pair), ACT.Copy).then_inc(o_hi, 1)

            def mixer(l):
                for n in range(NPROJ):
                    if n - 1 in MAIN_PA:
                        pa_main(l, MAIN_PA[n - 1])
                    if n == 0:
                        act.wait_ge(trig_done, 1)
                        act.activation(cs[:, :], angle, ACT.Sin).then_inc(sin_done, 1)
                        act.activation(csq[64:128, :], angle, ACT.Sin).then_inc(sin_done, 1)
                    if n == 9:
                        src = pa_wait(l, "ssq")
                        act.activation(rms[:, 0, :], src[:, 0:S], ACT.Sqrt, bias=eps_rms[:, 0:1], scale=1.0 / 256)
                        act.activation(rms[:, 1, :], src[:, S:2 * S], ACT.Sqrt, bias=eps_rms[:, 0:1], scale=1.0 / 128)\
                            .then_inc(pa_out, 1)
                        act.wait_ge(*evacuated(l, "kr"))
                        act.activation(krs[0:32, :], krt[32:64, :], ACT.Copy).then_inc(kr_shift, 1)
                    if n == 12:
                        act.wait_ge(kr_added, at(l, 1, 1))
                        src = krs[0:32, :].unsqueeze(1).broadcast_to([32, NH, S])
                        act.activation(kD[64:96, :, :], src, ACT.Copy).then_inc(kr_sum, 1)
                        act.activation(kD[96:128, :, :], src, ACT.Copy).then_inc(kr_sum, 1)
                    if n == 14:
                        act.wait_ge(*evacuated(l, "gf"))
                        act.activation(gth[:, :, :], gl[:, :, 0:12], ACT.Tanh, scale=0.5).then_inc(gth_done, 1)
                        act.wait_ge(fx_abs, at(l, 1, 1))
                        act.activation(fx[:, 2, :, :], fx[:, 1, :, :], ACT.Exp, scale=-1.0).then_inc(fx_exp, 1)
                        act.wait_ge(fx_exp, at(l, 1, 1))
                        act.activation(fx[:, 3, :, :], fx[:, 2, :, :], ACT.Ln, bias=1.0).then_inc(fx_ln, 1)
                    if n == U_UKV:
                        for i in range(2):
                            src = pa_wait(l, f"kn{i}")
                            act.activation(kD[0:64, 2 * i, :], src[0:64, 0:S], ACT.Copy)
                            act.activation(kD[0:64, 2 * i + 1, :], src[64:128, 0:S], ACT.Copy).then_inc(pa_out, 1)
                    if n - 2 in U_HID:
                        br = U_HID.index(n - 2)
                        act.wait_ge(hu_done, at(l, 2, br + 1))
                        act.activation(hu[:, br, :], hu[:, br, :], ACT.Tanh, scale=0.7978845608028654).then_inc(hg_done, 1)
                    ahead(l, MIX0 + n)
                step = 0
                for n in range(NPROJ, U_WO):
                    if n == U_W2 + 2:
                        src = pa_wait(l, "cmp")
                        act.activation(kcmp[0:64, 0:CMPW], src[0:64, 0:CMPW], ACT.Copy)
                        act.activation(kcmp[64:128, CMPW:2 * CMPW], src[64:128, 0:CMPW], ACT.Copy)
                        act.activation(vcmp[:, :], src[:, 64:128], ACT.Copy).then_inc(pa_out, 1)
                    if MIXER[n - 1][0] == "gate":
                        gate_tanh(l, step - 1)
                    if n == U_WO - 1:
                        for k in range(4):
                            merged_hi(l, k)
                    ahead(l, MIX0 + n)
                    if MIXER[n][0] != "gate":
                        continue
                    if step in PAIR_AT:
                        pair_hi(l, PAIR_AT[step])
                    if 1 <= step <= NSLOT:
                        copy_turned(l, step - 1)
                    if step < NSLOT:
                        exp_head(l, step)
                    step += 1
                for k in range(KT):
                    if k < 4:
                        merged_hi(l, 4 + k)
                    ahead(l, MIX0 + U_WO + k)

            def merged_hi(l, k):
                act.wait_ge(y_out, at(l, 3 * KT, 2 * KT + k + 1))
                act.activation(xTh[:, k, :], z[:, k, :], ACT.Copy, scale=0.5).then_inc(zh_done, 1)

            def gate_tanh(l, g):
                b, n = divmod(g, KT)
                src = pa_wait(l, f"gate{b}_{n}")[:, 0:S]
                if b == 2:
                    act.wait_ge(*evacuated(l, f"y0_{n}"))
                if b == 3:
                    act.wait_ge(y_out, at(l, 3 * KT, n + 1))
                act.activation(gates[:, KT * (b % 2) + n, :], src, ACT.Tanh, bias=col(HALF + BRANCHES[b] * KT + n),
                               scale=0.5).then_inc(pa_out, 1)

            def cross(l):
                j0 = MIX0 + U_X
                ahead(l, j0)
                normalise(l, 1)
                act.wait_ge(units_used, unit_done(l, j0 + 1))
                act.activation(xk[:, :, :].rearrange("p i s -> p (i s)"), ps[:, 4, :], ACT.Copy).then_inc(xk_out, 1)
                ahead(l, j0 + 1)
                evacuate(l, 3, 1)
                ahead(l, j0 + 2)
                for i in range(2):
                    act.wait_ge(units_used, unit_done(l, j0 + 4 + i))
                    act.activation(xq[:, i, :], ps[:, 4 + i, 0:S], ACT.Copy).then_inc(xq_out, 1)
                for h in range(NH + 1):
                    if h < NH:
                        act.wait_ge(xmax, at(l, NH, h + 1))
                        if h >= 2:
                            act.wait_ge(xpt_ready, at(l, NH, h - 1))
                        i = h % 2
                        for q in range(TT):
                            last = act.activation(pS[:, i, S * q:S * q + S], ps[:, h, S * q:S * q + S], ACT.Exp,
                                                  bias=stat[:, i, 1, q:q + 1], scale=SCALE, accum_out=stat[:, i, 2, q:q + 1])
                        last.then_inc(xexp, 1)
                    if h >= 1:
                        g = h - 1
                        act.wait_ge(xpt_ready, at(l, NH, g + 1))
                        if g >= 2:
                            act.wait_ge(xo_ready, at(l, NH, g - 1))
                        act.activation(pT[:, g % 2, :], ps[:, 5 + g % 2, :], ACT.Copy).then_inc(xpt_out, 1)
                for k in range(2):
                    act.wait_ge(xo_ready, at(l, NH, 2 * k + 2))
                    act.activation(oTh[:, k, :], ps[:, 7 if k == 0 else 4, 0:S], ACT.Copy).then_inc(xo_hi, 1)
                for i in range(3, 8):
                    ahead(l, j0 + i)
                normalise(l, 2)
                evacuate(l, 4, 2)

            act.wait_ge(credits_set, 1)
            split_hi(0, 0)
            turned_hi(0, xTh)
            split_hi(0, 1)
            split_hi(0, 2)
            turned_hi(1, memTh)
            split_hi(0, 3)
            split_hi(0, 4)
            with act.Fori(0, L) as l:
                ffn(l, 0)
                act.wait_ge(cols_ready, at(l, 1, 1))
                normalise(l, 0)
                evacuate(l, 2, 0)
                mixer(l)
                cross(l)
                ffn(l, FFN2_0)
                normalise(l, 3)
                evacuate(l, 5, 3)

        @block.vector
        def _(dve):
            def split_lo(l, j, more=0):
                dve.wait_ge(hi_done, units_before(l, j, more) + 1)
                views = zip(split_views(unit_at(j), j % RAW_SLOTS, wh[:, j % WT_SLOTS, :]),
                            split_views(unit_at(j), j % RAW_SLOTS, wl[:, j % WT_SLOTS, :]))
                for (src, hi), (_, lo) in views:
                    last = dve.tensor_tensor(lo, src, hi.bitcast(F32), ALU.subtract)
                last.then_inc(lo_done, 1)

            def ahead(l, j, more=0):
                split_lo(l, j + AHEAD, more)

            def split_act(fh, fl, src):
                dve.tensor_copy(fh, src)
                dve.drain()
                return dve.tensor_tensor(fl, src, fh.bitcast(F32), ALU.subtract)

            def turned_lo(idx, th, tl, ready_sem):
                for i in range(4):
                    t, half = divmod(i, 2)
                    to = (slice(None), slice(4 * half, 4 * half + 4), slice(P * t, P * t + P))
                    dve.wait_ge(xf_done, 16 * idx + 4 * i + 4)
                    last = dve.tensor_tensor(tl[to], turned_bank(t, half), th[to].bitcast(F32), ALU.subtract)
                    if t:
                        last.then_inc(ready_sem, 2)

            def split_x(l, idx):
                for half in range(2):
                    k = slice(4 * half, 4 * half + 4)
                    dve.wait_ge(xf_done, at(l, 64, 16 * idx + 4 * half + 4))
                    split_act(xTh[:, k, 0:P], xTl[:, k, 0:P], z[:, k, 0:P])
                for q in range(KT // 2):
                    k = slice(2 * q, 2 * q + 2)
                    dve.wait_ge(xf_done, at(l, 64, 16 * idx + KT + 2 * q + 2))
                    split_act(xTh[:, k, P:S], xTl[:, k, P:S], z[:, k, P:S]).then_inc(xT_ready, 1)

            def residual(l, s, t):
                dve.wait_ge(x_done, at(l, 4 * TT, TT * s + t + 1))
                acc = ps[:, 2 * t:2 * t + 2, :].rearrange("p a b -> p (a b)")
                dve.scalar_tensor_tensor(xb[:, t, :], xb[:, t, :], ALPHA, acc, ALU.mult, ALU.add)

            def variance(t):
                dve.drain()
                for c in range(2):
                    dve.bn_stats(bst[:, t, c, :], xb[:, t, 512 * c:512 * c + 512])
                dve.drain()
                dve.bn_aggr(mv[:, t, :], bst[:, t, :, :].rearrange("p c s -> p (c s)"))
                dve.drain()
                dve.tensor_scalar(vare[:, t:t + 1], mv[:, t, 1:2], LN_EPS, None, ALU.add).then_inc(stat_done, 1)

            def norm(l, s, j_end, between=None):
                dve.wait_ge(acc_ready, at(l, 4, s + 1))
                residual(l, s, 0)
                variance(0)
                if between:
                    between()
                if s == 2:
                    dve.wait_ge(units_used, unit_done(l, j_end))
                    residual(l, s, 1)
                dve.wait_ge(rstd_done, at(l, 4 * TT, TT * s + 1))
                dve.scalar_tensor_tensor(nmr[:, 0:1], mv[:, 0, 0:1], -1.0, rstd[:, 0:1], ALU.mult, ALU.mult)\
                    .then_inc(nm_done, 1)
                if s != 2:
                    dve.wait_ge(units_used, unit_done(l, j_end))
                    residual(l, s, 1)
                variance(1)
                dve.wait_ge(rstd_done, at(l, 4 * TT, TT * s + 2))
                dve.wait_ge(xn_done, at(l, 4 * TT, TT * s + 1))
                dve.tensor_scalar(xb[:, 1, :], xb[:, 1, :], mv[:, 1, 0:1], rstd[:, 1:2], ALU.subtract, ALU.mult)\
                    .then_inc(xn_done, 1)

            def columns(l):
                dve.wait_ge(cols_psum, at(l, 1, 1))
                for dst, n, src in ((0, NB, 0), (LNG, 32, 96), (LNB, 32, 160), (POS, 32, 224), (QN, 2, 288), (KN, 1, 292)):
                    dve.tensor_copy(cur[:, dst:dst + n], ps[:, 7, bass.ds(l * n + src, n)])
                dve.drain()
                dve.tensor_scalar(cur[:, HALF:HALF + 32], cur[:, GB0:GB0 + 32], 0.5, None, ALU.mult).then_inc(cols_ready, 1)

            def hidden(l, which, f, more=0):
                dve.wait_ge(silu_done, at(l, 2 * FT, FT * which + f + 1) + more * 2)
                p, o = f % 2, hidden_slot(f)
                dve.scalar_tensor_tensor(hf[:, p, :], hs[:, p, :], 0.5, ps[:, 4 + p, 256:512], ALU.mult, ALU.mult)\
                    .then_inc(gu_out, 1)
                dve.drain()
                split_act(oTh[:, o, :], oTl[:, o, :], hf[:, p, :]).then_inc(hT_ready, 1)

            def ffn(l, which, j0):
                ahead(l, j0)
                ahead(l, j0 + 1)
                hidden(l, which, 0)
                for n in range(2, 5):
                    ahead(l, j0 + n)

                def turn(j, i=0):
                    f = 1 + (j - j0 - 5) // 3
                    ahead(l, j, i)
                    hidden(l, which, f, i)
                    for n in range(1, 4):
                        ahead(l, j + n, i)
                    hidden(l, which, f + 1, i)
                    ahead(l, j + 4, i)
                    ahead(l, j + 5, i)
                with dve.Fori(0, FT // 2 - 2) as i:
                    turn(j0 + 5, i)
                j = j0 + FFN_UNITS - 7
                hidden(l, which, FT - 3)
                ahead(l, j)
                ahead(l, j + 1)
                hidden(l, which, FT - 2)
                if which == 0:
                    columns(l)
                ahead(l, j + 2)
                ahead(l, j + 3)
                hidden(l, which, FT - 1)
                ahead(l, j + 4)

            def pd_wait(l, name):
                dve.wait_ge(*ready(l, name))
                return pd_tile(name)

            def value_out(l, name, dst, b0):
                n = dst.shape[2]
                src = pd_wait(l, name)[:, 0:TT * n].rearrange("p (t n) -> p t n", t=TT)
                bb = vbias[:, b0:b0 + n].unsqueeze(1).broadcast_to([P, TT, n])
                dve.tensor_tensor(dst, src, bb, ALU.add).then_inc(pd_out, 1)

            def softmax_max(l, n):
                b, h, kind = HEADS[n]
                dve.wait_ge(s_ready, at(l, NSLOT, n + 1))
                i = n % 2
                src = S_BANK
                if kind == "cmp":
                    lg = pc[:, :, :, 0:CMPW].rearrange("p q h c -> p (q h) c")
                    tab = const[:, C_CMPB:C_CMPB + 128].rearrange("p (g c) -> p g c", c=CMPW)
                    dve.scalar_tensor_tensor(lg, src[:, 0:128].rearrange("p (g c) -> p g c", c=CMPW), SCALE, tab,
                                             ALU.mult, ALU.add).then_inc(s_out, 1)
                    dve.drain()
                    dve.tensor_reduce(cstat[:, 0, :], lg, AX.X, ALU.max)
                    dve.drain()
                    dve.tensor_tensor(lg, lg, cstat[:, 0, :].unsqueeze(2).broadcast_to([P, 8, CMPW]), ALU.subtract)\
                        .then_inc(s_max, 1)
                    return
                scale = SCALE_D if kind == "d" else SCALE
                if n >= 2:
                    dve.wait_ge(pt_ready, at(l, NSLOT, n - 1))
                dve.memset(fence[:, :], 0.0)
                dve.tensor_tensor_reduce(pS[:, i, 0:P], src[:, 0:P], bias_table(kind, h, 0), scale, -3.4e38,
                                         ALU.add, ALU.max, stat[:, i, 0, 0:1])
                dve.tensor_tensor_reduce(pS[:, i, P:3 * P], src[:, P:3 * P], bias_table(kind, h, 1), scale, -3.4e38,
                                         ALU.add, ALU.max, stat[:, i, 0, 1:2]).then_inc(s_out, 1)
                dve.drain()
                dve.tensor_scalar(stat[:, i, 1, :], stat[:, i, 0, :], -1.0, None, ALU.mult).then_inc(s_max, 1)

            def softmax_norm(l, n):
                b, h, kind = HEADS[n]
                dve.wait_ge(p_exp, at(l, NSLOT, n + 1))
                i = n % 2
                if kind == "cmp":
                    lg = pc[:, :, :, 0:CMPW].rearrange("p q h c -> p (q h) c")
                    tab = const[:, C_CMPM:C_CMPM + 128].rearrange("p (g c) -> p g c", c=CMPW)
                    dve.tensor_tensor(lg, lg, tab, ALU.mult)
                    dve.drain()
                    dve.tensor_reduce(cstat[:, 1, :], lg, AX.X, ALU.add)
                    dve.drain()
                    dve.tensor_scalar(cstat[:, 1, :], cstat[:, 1, :], 1e-30, None, ALU.max)
                    dve.drain()
                    dve.reciprocal(cstat[:, 2, :], cstat[:, 1, :])
                    dve.drain()
                    g0 = gt[:, :, :].rearrange("p q (h b) -> p q h b", b=3)[:, :, :, 0]
                    dve.tensor_tensor(cstat[:, 2, :].rearrange("p (q h) -> p q h", h=NH),
                                      cstat[:, 2, :].rearrange("p (q h) -> p q h", h=NH), g0, ALU.mult)
                    dve.drain()
                    dve.tensor_tensor(lg, lg, cstat[:, 2, :].unsqueeze(2).broadcast_to([P, 8, CMPW]), ALU.mult)\
                        .then_inc(p_ready, 1)
                    return
                dve.tensor_scalar(stat[:, i, 2, :], stat[:, i, 2, :], 1e-30, None, ALU.max)
                dve.drain()
                dve.reciprocal(stat[:, i, 3, :], stat[:, i, 2, :])
                dve.drain()
                parts = ((0, 0, P), (1, P, 3 * P))
                for q, c0, c1 in parts:
                    if kind in "sw":
                        g = 3 * h + (1 if kind == "s" else 2)
                        last = dve.tensor_scalar(pS[:, i, c0:c1], pS[:, i, c0:c1], stat[:, i, 3, q:q + 1],
                                                 gt[:, q, g:g + 1], ALU.mult, ALU.mult)
                    else:
                        last = dve.tensor_scalar(pS[:, i, c0:c1], pS[:, i, c0:c1], stat[:, i, 3, q:q + 1], None, ALU.mult)
                last.then_inc(p_ready, 1)

            def pair_lo(l, pair):
                dve.wait_ge(o_hi, at(l, PAIRS, pair + 1))
                s_ = pair % 4
                dve.tensor_tensor(oTl[:, s_, :], o_bank(pair), oTh[:, s_, :].bitcast(F32), ALU.subtract).then_inc(o_out, 1)

            def merged_lo(l, k):
                dve.wait_ge(zh_done, at(l, KT, k + 1))
                dve.scalar_tensor_tensor(xTl[:, k, :], z[:, k, :], 0.5, xTh[:, k, :].bitcast(F32), ALU.mult,
                                         ALU.subtract).then_inc(z_ready, 1)

            def merge(l, b, tiles, ends):
                for n in tiles:
                    src = pd_wait(l, f"y{b}_{n}")[:, 0:S]
                    g = gates[:, KT * (b % 2) + n, :]
                    dve.wait_ge(*evacuated(l, f"gate{b}_{n}"))
                    dst = z[:, n, :] if b == 0 else g
                    dve.scalar_tensor_tensor(dst, g, 1.0, src, ALU.add, ALU.mult).then_inc(pd_out, 1)
                    if ends:
                        merged_lo(l, n - 4)
                if b:
                    dve.drain()
                    for n in tiles:
                        dve.tensor_tensor(z[:, n, :], z[:, n, :], gates[:, KT * (b % 2) + n, :], ALU.add).then_inc(y_out, 1)

            def compression_split(l, br):
                src = pd_wait(l, f"turn{br}")[:, 0:2 * CMPW]
                dve.tensor_scalar(hT[:, :, :].rearrange("p k c -> p (k c)"), src, 0.5, None, ALU.mult).then_inc(pd_out, 1)
                dve.drain()
                if br == 0:
                    split_act(hkh[:, :, :], hkl[:, :, :], hT).then_inc(hid_ready, 1)
                else:
                    for k in range(2):
                        s_ = hT[:, k, :].unsqueeze(1).broadcast_to([P, NH, CMPW])
                        last = split_act(hvh[:, k, :, 0:CMPW], hvl[:, k, :, 0:CMPW], s_)
                    last.then_inc(hid_ready, 1)

            def mixer(l):
                for n in range(NPROJ):
                    if n == 3:
                        dve.wait_ge(*evacuated(l, "dckv"))
                        dve.tensor_tensor(sq, cqf, cqf, ALU.mult).then_inc(sq_done, 1)
                    if n == 4:
                        src = pd_wait(l, "kr")
                        bcol = col(BIAS["kr"])
                        dve.scalar_tensor_tensor(krt[0:64, :], src[0:64, 0:S], bcol[0:64, :], cs, ALU.add, ALU.mult)
                        dve.tensor_scalar(krt[64:80, :], src[64:80, 0:S], bcol[64:80, :], None, ALU.add).then_inc(pd_out, 1)
                    if n == 6:
                        dve.wait_ge(*evacuated(l, "kc"))
                        for br in range(2):
                            tokens = x2[:, br, :].rearrange("p (c s) -> p s c", s=16)
                            for a_ in range(2):
                                pos = cur[:, POS + 16 * br + 8 * a_:POS + 16 * br + 8 * a_ + 8]
                                dve.tensor_tensor(blkf[:, br, 8 * a_:8 * a_ + 8, :], tokens[:, 0:16:2, a_:a_ + CMP],
                                                  pos.unsqueeze(2).broadcast_to([P, 8, CMP]), ALU.add)
                        dve.drain()
                        parts = (w[:, 0:32 * CMPW].rearrange("p (bl c) -> p bl c", c=CMPW)[:, :, 0:CMP]
                                 for w in (blkh, blkl))
                        split_act(*parts,
                                  blkf[:, :, :, :].rearrange("p b l c -> p (b l) c")).then_inc(blk_ready, 1)
                    if n == 9:
                        dve.tensor_copy(vsT, pd_wait(l, "vs")[:, 0:S]).then_inc(pd_out, 1)
                    if n == U_VS + 4:
                        value_out(l, "vst", vB[:, :, :], 256)
                    if n == 10:
                        dve.wait_ge(*evacuated(l, "ssq"))
                        dve.wait_ge(kr_shift, at(l, 1, 1))
                        dve.tensor_tensor(krs[0:32, :], krt[0:32, :], krs[0:32, :], ALU.add).then_inc(kr_added, 1)
                        dve.reciprocal(rms[:, 0, :], rms[:, 0, :])
                    if n == 11:
                        dve.reciprocal(rms[:, 1, :], rms[:, 1, :])
                    if n == 13:
                        dve.drain()
                        for i in range(3):
                            dve.scalar_tensor_tensor(cqf[:, i, :], cqf[:, i, :], col(QN + i), rms[:, i // 2, :],
                                                     ALU.mult, ALU.mult)
                        dve.drain()
                        split_act(oTh[:, 0:3, :], oTl[:, 0:3, :], cqf).then_inc(cqn_ready, 1)
                    if n == 7:
                        src = pd_wait(l, "gf")[:, 0:32].rearrange("p (t n) -> p t n", t=TT)
                        dve.tensor_copy(gl[:, :, :], src).then_inc(pd_out, 1)
                        dve.drain()
                        f = gl[:, :, 12:16]
                        dve.tensor_scalar(fx[:, 0, :, :], f, -1.0, None, ALU.mult)
                        dve.tensor_scalar(fx[:, 4, :, :], f, 0.0, None, ALU.min)
                        dve.drain()
                        dve.tensor_tensor(fx[:, 1, :, :], f, fx[:, 0, :, :], ALU.max).then_inc(fx_abs, 1)
                    if n == 16:
                        dve.wait_ge(gth_done, at(l, 1, 1))
                        dve.tensor_scalar(gt[:, :, :], gth[:, :, :], 0.5, 0.5, ALU.mult, ALU.add)
                        dve.wait_ge(fx_ln, at(l, 1, 1))
                        dve.tensor_tensor(fx[:, 0, :, :], fx[:, 4, :, :], fx[:, 3, :, :], ALU.subtract)
                        dve.drain()
                        for i in range(2):
                            last = dve.tensor_scalar(ls8[:, :, 4 * i:4 * i + 4], fx[:, 0, :, :], 1.0 / SCALE, None, ALU.mult)
                        last.then_inc(ls_ready, 1)
                    if n == U_CV + 2:
                        value_out(l, "cv", vC[:, :, :], 384)
                    if n == U_DECAY + 1:
                        src = decay
                        dve.tensor_copy(src, pd_wait(l, "decay")[0:8, 0:S]).then_inc(pd_out, 1)
                        dve.drain()
                        for h in range(NH):
                            sel = const[0:8, C_SEL + h:C_SEL + 13 + h]
                            dve.tensor_scalar(lq[:, h, :], src, sel[:, 0:1], sel[:, 4:5], ALU.mult, ALU.add)
                            dve.tensor_scalar(rk[:, h, :], src, sel[:, 8:9], sel[:, 12:13], ALU.mult, ALU.add)
                    if n == U_TURN[0] + 1:
                        compression_split(l, 0)
                    if n in (U_UQ0, U_UQ1):
                        for h in (0, 1) if n == U_UQ0 else (2, 3):
                            src = pd_wait(l, f"q{h}")[:, 0:S]
                            dve.tensor_tensor(qD[:, h, :], src, csq[:, :], ALU.mult).then_inc(pd_out, 1)
                    if n == U_UKV:
                        for t in range(TT):
                            src = pd_wait(l, f"vd{t}")[:, 0:S]
                            dve.tensor_copy(vD[:, t, :], src).then_inc(pd_out, 1)
                    if n - 1 in U_HID:
                        br = U_HID.index(n - 1)
                        dve.wait_ge(units_used, unit_done(l, MIX0 + U_HID[br]))
                        dve.tensor_copy(hx[:, br, :], hidden_bank(br)[0:CMPW, :])
                        dve.drain()
                        dve.tensor_tensor(hu[:, br, :], hx[:, br, :], hx[:, br, :], ALU.mult)
                        dve.drain()
                        dve.tensor_scalar(hu[:, br, :], hu[:, br, :], 0.044715, 1.0, ALU.mult, ALU.add)
                        dve.drain()
                        dve.tensor_tensor(hu[:, br, :], hu[:, br, :], hx[:, br, :], ALU.mult).then_inc(hu_done, 1)
                    if n - 3 in U_HID:
                        br = U_HID.index(n - 3)
                        dve.wait_ge(hg_done, at(l, 2, br + 1))
                        dve.scalar_tensor_tensor(hx[:, br, :], hu[:, br, :], 1.0, hx[:, br, :], ALU.add, ALU.mult)\
                            .then_inc(gelu_done, 1)
                    ahead(l, MIX0 + n)
                step = 0
                for n in range(NPROJ, U_WO):
                    if n == NPROJ:
                        value_out(l, "av", vA[:, :, :], 0)
                        compression_split(l, 1)
                    if MIXER[n][0] == "w2":
                        ahead(l, MIX0 + n)
                        continue
                    kind, b, i = MIXER[n]
                    if kind == "branch":
                        merge(l, b, range(4 * i, 4 * i + 4), n == U_WO - 1)
                        ahead(l, MIX0 + n)
                        continue
                    if step in PAIR_AT:
                        pair_lo(l, PAIR_AT[step])
                    if step < NSLOT:
                        softmax_max(l, step)
                    ahead(l, MIX0 + n)
                    if step < NSLOT:
                        softmax_norm(l, step)
                    step += 1
                for k in range(KT):
                    if k < 4:
                        merged_lo(l, 4 + k)
                    if k < KT - 2:
                        ahead(l, MIX0 + U_WO + k)

            def cross(l):
                j0 = MIX0 + U_X
                norm(l, 1, j0 - 1, lambda: ahead(l, j0 - 2))
                ahead(l, j0 - 1)
                ahead(l, j0)
                split_x(l, 3)
                dve.wait_ge(units_used, unit_done(l, j0 + 3))
                dve.tensor_copy(xv[:, :, :].rearrange("p t n -> p (t n)"), ps[:, 5, :]).then_inc(xv_out, 1)
                ahead(l, j0 + 1)
                ahead(l, j0 + 2)

                def maxima(h):
                    dve.wait_ge(xs_ready, at(l, NH, h + 1))
                    i = h % 2
                    dve.tensor_reduce(stat[:, i, 0, :], ps[:, h, :].rearrange("p (q k) -> p q k", q=TT), AX.X, ALU.max)
                    dve.drain()
                    dve.tensor_scalar(stat[:, i, 1, :], stat[:, i, 0, :], -SCALE, None, ALU.mult).then_inc(xmax, 1)

                maxima(0)
                for h in range(NH):
                    if h + 1 < NH:
                        maxima(h + 1)
                    dve.wait_ge(xexp, at(l, NH, h + 1))
                    i = h % 2
                    dve.reciprocal(stat[:, i, 3, :], stat[:, i, 2, :])
                    dve.drain()
                    for q in range(TT):
                        last = dve.tensor_scalar(pS[:, i, S * q:S * q + S], pS[:, i, S * q:S * q + S],
                                                 stat[:, i, 3, q:q + 1], None, ALU.mult)
                    last.then_inc(xp_ready, 1)
                for k in range(2):
                    dve.wait_ge(xo_hi, at(l, 2, k + 1))
                    dve.tensor_tensor(oTl[:, k, :], ps[:, 7 if k == 0 else 4, 0:S], oTh[:, k, :].bitcast(F32),
                                      ALU.subtract).then_inc(xo_out, 1)
                for i in range(3, 5):
                    ahead(l, j0 + i)
                norm(l, 2, j0 + 7)
                split_x(l, 4)
                ahead(l, j0 + 5)
                ahead(l, j0 + 6)
                ahead(l, j0 + 7)

            dve.memset(eps_rms[:, :], RMS_EPS)
            dve.sem_inc(lo_done, RAW_SLOTS)
            dve.sem_inc(pa_out, 2)
            dve.sem_inc(pd_out, 2)
            dve.sem_inc(gu_out, 2)
            dve.sem_inc(s_out, 1)
            dve.sem_inc(pt_out, 1)
            dve.sem_inc(o_out, 2)
            dve.sem_inc(x_done, TT)
            dve.drain()
            dve.sem_inc(credits_set, 1)
            split_lo(0, 0)
            turned_lo(0, xTh, xTl, xT_ready)
            split_lo(0, 1)
            split_lo(0, 2)
            turned_lo(1, memTh, memTl, memT_ready)
            split_lo(0, 3)
            split_lo(0, 4)
            with dve.Fori(0, L) as l:
                ffn(l, 0, 0)
                norm(l, 0, FFN_UNITS - 1)
                split_x(l, 2)
                ahead(l, FFN_UNITS - 2)
                ahead(l, FFN_UNITS - 1)
                dve.wait_ge(vb_in, at(l, 64, 64))
                dve.wait_ge(const_in, 16)
                mixer(l)
                cross(l)
                ffn(l, 1, FFN2_0)
                norm(l, 3, UNITS - 1)
                split_x(l, 5)
                ahead(l, UNITS - 2)
                ahead(l, UNITS - 1)


_INPUTS = ("x", "mem", "positions", "ln_g", "ln_b", "ffn1_w_in", "ffn1_w_out", "ffn2_w_in", "ffn2_w_out", "w_in",
           "b_in", "w_branch", "w_o", "mla_q_norm", "mla_w_uq", "mla_kv_norm", "mla_w_ukv", "nsa_cmp_pos",
           "nsa_cmp_w1", "nsa_cmp_w2", "xa_w_q", "xa_w_kv", "xa_w_o")


def kernel(**inputs):
    import concourse.bacc as bacc
    from concourse.bass_utils import run_bass_kernel_spmd
    nc = bacc.Bacc("TRN2", target_bir_lowering=False, num_devices=1)
    arrays, a = {}, {}
    for name in _INPUTS:
        v = np.ascontiguousarray(inputs[name])
        arrays["in_" + name] = v
        a[name] = nc.dram_tensor("in_" + name, v.shape, mybir.dt.from_np(v.dtype), kind="ExternalInput").ap()
    arrays["in_const"] = constants()
    a["const"] = nc.dram_tensor("in_const", (P, NCONST), F32, kind="ExternalInput").ap()
    out = nc.dram_tensor("out_0", (1, S, D), F32, kind="ExternalOutput").ap()
    build(nc, a, out)
    r = run_bass_kernel_spmd(nc, [arrays], core_ids=[0])
    return r.results[0]["out_0"]
```
